# Optimizing a Trainium2 kernel written in Bass

```python
import math
import jax, jax.numpy as jnp
from jax import lax
import numpy as np

D_MODEL = 1024
BATCH = 1
SEQ = 1024
DEPTH = 2

N_META = 16
A_HEADS = 8
A_HEAD_DIM = 64
A_WIDTH = A_HEADS * A_HEAD_DIM
Q_RANK = 256
IDX_HEADS = 16
IDX_DIM = 64
TOPK_MAX = 256
Q_BLOCK = 128
B_HEADS = 8
B_KEY_DIM = 64
B_VAL_DIM = 64
B_KEY_WIDTH = B_HEADS * B_KEY_DIM
B_VAL_WIDTH = B_HEADS * B_VAL_DIM
CHUNK = 64
POOL_WINDOWS = (2, 4, 8, 16)
POOL_GROUPS = 4
POOL_GROUP_DIM = D_MODEL // POOL_GROUPS
MIX_WIDTH = A_WIDTH + B_VAL_WIDTH
IN_COLS = Q_RANK + 2 * A_WIDTH + IDX_DIM + IDX_HEADS + 2 * B_KEY_WIDTH + 2 * B_VAL_WIDTH
D_FF = -(-8 * D_MODEL // (3 * 256)) * 256
ALPHA = (2 * DEPTH) ** 0.25
BETA = (8 * DEPTH) ** -0.25
N_EVEN = (DEPTH + 1) // 2
N_ODD = DEPTH // 2
LN_EPS = 1e-5

kernel_name = "hybrid_dsa_hgrn2_pool_trunk"

def layer_norm(x, g, b):
    xf = x.astype(jnp.float32)
    mu = jnp.mean(xf, axis=-1, keepdims=True)
    var = jnp.mean(jnp.square(xf - mu), axis=-1, keepdims=True)
    y = (xf - mu) * lax.rsqrt(var + LN_EPS)
    return (y * g.astype(jnp.float32) + b.astype(jnp.float32)).astype(x.dtype)

def rms_norm(x, g):
    xf = x.astype(jnp.float32)
    y = xf * lax.rsqrt(jnp.mean(jnp.square(xf), axis=-1, keepdims=True) + LN_EPS)
    return (y * g.astype(jnp.float32)).astype(x.dtype)

def alibi_slopes(n):
    return 2.0 ** (-8.0 * jnp.arange(1, n + 1, dtype=jnp.float32) / n)

def dsa_attention(q, k, v, q_idx, k_idx, w_idx, topk):
    B, L = k.shape[0], k.shape[1]
    n_blk = -(-L // Q_BLOCK)
    Lq = n_blk * Q_BLOCK
    pad = Lq - L

    def to_blocks(a):
        a = jnp.pad(a, [(0, 0), (0, pad)] + [(0, 0)] * (a.ndim - 2))
        return a.reshape((B, n_blk, Q_BLOCK) + a.shape[2:]).swapaxes(0, 1)

    slopes = alibi_slopes(A_HEADS)
    key_pos = jnp.arange(L)
    scale = A_HEAD_DIM ** -0.5

    def block(args):
        qb, qib, wb, t = args
        s = jnp.einsum('bqhd,bsd->bqhs', qib, k_idx)
        score = jnp.einsum('bqhs,bqh->bqs', jax.nn.relu(s), wb).astype(jnp.float32)
        causal = key_pos[None, :] <= t[:, None]
        score = jnp.where(causal[None], score, -jnp.inf)
        _, idx = lax.top_k(score, topk)
        valid = idx <= t[None, :, None]
        k_sel = jax.vmap(lambda kb, ib: kb[ib])(k, idx)
        v_sel = jax.vmap(lambda vb, ib: vb[ib])(v, idx)
        logits = jnp.einsum('bqhd,bqkhd->bhqk', qb, k_sel).astype(jnp.float32) * scale
        dist = (t[None, :, None] - idx).astype(jnp.float32)
        logits = logits - slopes[None, :, None, None] * dist[:, None]
        logits = jnp.where(valid[:, None], logits, -jnp.inf)
        p = jax.nn.softmax(logits, axis=-1).astype(v.dtype)
        return jnp.einsum('bhqk,bqkhd->bqhd', p, v_sel)

    t_blocks = jnp.arange(Lq).reshape(n_blk, Q_BLOCK)
    out = lax.map(block, (to_blocks(q), to_blocks(q_idx), to_blocks(w_idx), t_blocks))
    out = out.swapaxes(0, 1).reshape(B, Lq, A_HEADS, A_HEAD_DIM)
    return out[:, :L]

def hgrn2_chunkwise(q, logf, k, v):
    B, L, H, DK = q.shape
    DV = v.shape[-1]
    left = (-N_META) % CHUNK
    right = (-(L + left)) % CHUNK
    Lp = L + left + right
    N = Lp // CHUNK

    def chunk(a):
        a = jnp.pad(a, ((0, 0), (left, right), (0, 0), (0, 0)))
        return a.reshape(B, N, CHUNK, H, a.shape[-1]).transpose(1, 0, 3, 2, 4)

    qc, gc, kc, vc = chunk(q), chunk(logf), chunk(k), chunk(v)
    causal = jnp.tril(jnp.ones((CHUNK, CHUNK), dtype=bool))

    def step(S, xs):
        qn, gn, kn, vn = xs
        b = jnp.cumsum(gn, axis=2)
        inter = jnp.einsum('bhtd,bhde->bhte', qn * jnp.exp(b), S)
        diff = b[:, :, :, None, :] - b[:, :, None, :, :]
        decay = jnp.exp(jnp.where(causal[:, :, None], diff, -jnp.inf))
        scores = jnp.einsum('bhtd,bhtsd,bhsd->bhts', qn, decay, kn)
        intra = jnp.einsum('bhts,bhse->bhte', scores, vn)
        b_last = b[:, :, -1:, :]
        S = jnp.exp(b_last[:, :, 0, :])[..., None] * S + jnp.einsum('bhsd,bhse->bhde', kn * jnp.exp(b_last - b), vn)
        return S, inter + intra

    S0 = jnp.zeros((B, H, DK, DV), v.dtype)
    _, out = lax.scan(step, S0, (qc, gc, kc, vc))
    out = out.transpose(1, 0, 3, 2, 4).reshape(B, Lp, H, DV)
    return out[:, left:left + L]

def attn_recurrent_mixer(h, w_in, cq_gain, w_uq, w_uq_idx, kidx_gain, kidx_bias, lb, onorm_gain, w_out, topk):
    B, L, _ = h.shape
    sizes = [Q_RANK, A_WIDTH, A_WIDTH, IDX_DIM, IDX_HEADS, B_KEY_WIDTH, B_KEY_WIDTH, B_VAL_WIDTH, B_VAL_WIDTH]
    splits = np.cumsum(sizes)[:-1].tolist()
    proj = h @ w_in
    c_q, k_a, v_a, k_i, w_i, q_b, z_f, i_b, g_b = jnp.split(proj, splits, axis=-1)
    c_q = rms_norm(c_q, cq_gain)
    q_a = (c_q @ w_uq).reshape(B, L, A_HEADS, A_HEAD_DIM)
    q_i = (c_q @ w_uq_idx).reshape(B, L, IDX_HEADS, IDX_DIM)
    k_i = layer_norm(k_i, kidx_gain, kidx_bias)
    w_i = w_i * (IDX_HEADS ** -0.5 * IDX_DIM ** -0.5)
    o_a = dsa_attention(q_a, k_a.reshape(B, L, A_HEADS, A_HEAD_DIM), v_a.reshape(B, L, A_HEADS, A_HEAD_DIM),
                        q_i, k_i, w_i, topk)
    z_f = z_f.reshape(B, L, B_HEADS, B_KEY_DIM)
    lb = lb.reshape(B_HEADS, B_KEY_DIM)
    logf = jnp.logaddexp(jnp.log(lb), jnp.log1p(-lb) + jax.nn.log_sigmoid(z_f.astype(jnp.float32))).astype(h.dtype)
    k_b = ((1.0 - lb) * jax.nn.sigmoid(-z_f.astype(jnp.float32))).astype(h.dtype)
    o_b = hgrn2_chunkwise(q_b.reshape(B, L, B_HEADS, B_KEY_DIM), logf, k_b,
                          i_b.reshape(B, L, B_HEADS, B_VAL_DIM))
    o_b = rms_norm(o_b, onorm_gain.reshape(B_HEADS, B_VAL_DIM)) * jax.nn.silu(g_b.reshape(B, L, B_HEADS, B_VAL_DIM))
    o = jnp.concatenate([o_a.reshape(B, L, A_WIDTH), o_b.reshape(B, L, B_VAL_WIDTH)], axis=-1)
    return o @ w_out

def multiscale_pool(h, w_pool, scale):
    B, L, D = h.shape
    hf = h.astype(jnp.float32)
    cs = jnp.concatenate([jnp.zeros((B, 1, D), jnp.float32), jnp.cumsum(hf, axis=1)], axis=1)
    pos = jnp.arange(L)
    outs = []
    for g, w in enumerate(POOL_WINDOWS):
        sl = slice(g * POOL_GROUP_DIM, (g + 1) * POOL_GROUP_DIM)
        cs_g = cs[..., sl]
        lo = jnp.maximum(pos + 1 - w, 0)
        cnt = (pos + 1 - lo).astype(jnp.float32)
        mean = (cs_g[:, 1:] - cs_g[:, lo]) / cnt[None, :, None]
        d = (mean - hf[..., sl]).astype(h.dtype)
        outs.append(d @ w_pool[g])
    return jnp.concatenate(outs, axis=-1) * scale

def swiglu(h, w_gate, w_up, w_down):
    return (jax.nn.silu(h @ w_gate) * (h @ w_up)) @ w_down

def setup_inputs(seed: int = 0) -> dict:
    key = jax.random.key(seed)
    ks = jax.random.split(key, 24)
    f32 = jnp.float32

    def nrm(k, shape, s):
        return jax.random.normal(k, shape, f32) * s

    D = D_MODEL
    return {
        "x": nrm(ks[0], (BATCH, SEQ, D), 1.0),
        "meta_tokens": nrm(ks[1], (N_META, D), 1.0),
        "w_in": nrm(ks[2], (N_EVEN, D, IN_COLS), D ** -0.5),
        "cq_gain": 1.0 + nrm(ks[3], (N_EVEN, Q_RANK), 0.02),
        "w_uq": nrm(ks[4], (N_EVEN, Q_RANK, A_WIDTH), Q_RANK ** -0.5),
        "w_uq_idx": nrm(ks[5], (N_EVEN, Q_RANK, IDX_HEADS * IDX_DIM), Q_RANK ** -0.5),
        "kidx_gain": 1.0 + nrm(ks[6], (N_EVEN, IDX_DIM), 0.02),
        "kidx_bias": nrm(ks[7], (N_EVEN, IDX_DIM), 0.02),
        "lb_raw": nrm(ks[8], (N_EVEN, B_KEY_WIDTH), 0.5),
        "onorm_gain": 1.0 + nrm(ks[9], (N_EVEN, B_VAL_WIDTH), 0.02),
        "w_out": nrm(ks[10], (N_EVEN, MIX_WIDTH, D), MIX_WIDTH ** -0.5 * BETA),
        "w_pool": nrm(ks[11], (N_ODD, POOL_GROUPS, POOL_GROUP_DIM, POOL_GROUP_DIM), POOL_GROUP_DIM ** -0.5 * BETA),
        "pool_scale": 1.0 + nrm(ks[12], (N_ODD, D), 0.02),
        "ln_mix_g": 1.0 + nrm(ks[13], (DEPTH, D), 0.02),
        "ln_mix_b": nrm(ks[14], (DEPTH, D), 0.02),
        "w_gate": nrm(ks[15], (DEPTH, D, D_FF), D ** -0.5),
        "w_up": nrm(ks[16], (DEPTH, D, D_FF), D ** -0.5),
        "w_down": nrm(ks[17], (DEPTH, D_FF, D), D_FF ** -0.5 * BETA),
        "ln_ffn_g": 1.0 + nrm(ks[18], (DEPTH, D), 0.02),
        "ln_ffn_b": nrm(ks[19], (DEPTH, D), 0.02),
    }

def reference(x, meta_tokens, w_in, cq_gain, w_uq, w_uq_idx, kidx_gain, kidx_bias, lb_raw, onorm_gain, w_out,
              w_pool, pool_scale, ln_mix_g, ln_mix_b, w_gate, w_up, w_down, ln_ffn_g, ln_ffn_b):
    B, S, D = x.shape
    topk = min(TOPK_MAX, S // 4)
    meta = jnp.broadcast_to(meta_tokens.astype(x.dtype)[None], (B, N_META, D))
    h = jnp.concatenate([meta, x], axis=1)
    lower = jnp.cumsum(jax.nn.softmax(lb_raw.astype(jnp.float32), axis=0), axis=0)
    lower = lower - lower[:1]
    for layer in range(DEPTH):
        j = layer // 2
        if layer % 2 == 0:
            mix = attn_recurrent_mixer(h, w_in[j], cq_gain[j], w_uq[j], w_uq_idx[j], kidx_gain[j], kidx_bias[j],
                                       lower[j], onorm_gain[j], w_out[j], topk)
        else:
            mix = multiscale_pool(h, w_pool[j], pool_scale[j])
        h = layer_norm(ALPHA * h + mix, ln_mix_g[layer], ln_mix_b[layer])
        h = layer_norm(ALPHA * h + swiglu(h, w_gate[layer], w_up[layer], w_down[layer]), ln_ffn_g[layer], ln_ffn_b[layer])
    return h[:, N_META:]


_drawn_inputs = setup_inputs


def setup_inputs(seed=0):
    import zlib

    import numpy as np

    out = dict(_drawn_inputs(seed))
    spreads = {}
    factors = {'meta_tokens': 4.549,
     'cq_gain': 4.722,
     'kidx_gain': 4.455,
     'kidx_bias': 4.833,
     'onorm_gain': 8.0,
     'pool_scale': 8.0}
    for name, (base, spread) in spreads.items():
        noise = np.random.default_rng([zlib.crc32(name.encode()), seed]).standard_normal(out[name].shape)
        drawn = base * np.exp(spread * noise) if base else spread * noise
        out[name] = __import__('jax').numpy.asarray(drawn.astype(out[name].dtype))
    for name, factor in factors.items():
        out[name] = (out[name] * factor).astype(out[name].dtype)
    return out
```

```python
from contextlib import ExitStack, contextmanager

import concourse.bass as bass
from concourse import mybir

F32 = mybir.dt.float32
F32R = mybir.dt.float32r
I32 = mybir.dt.int32
ALU = mybir.AluOpType
ACT = mybir.ActivationFunctionType

P = 128
D = 1024
DC = D // P
SEQ = 1024
N_META = 16
L = SEQ + N_META
A_HEADS = 8
HD = 64
A_WIDTH = A_HEADS * HD
Q_RANK = 256
QC = Q_RANK // P
IDX_HEADS = 16
IDX_WIDTH = IDX_HEADS * HD
TOPK = 256
D_FF = 2816
FF_TILES = D_FF // P
DEPTH = 2
ALPHA = (2 * DEPTH) ** 0.25
LN_EPS = 1e-5
POOL_WINDOWS = (2, 4, 8, 16)
PG = D // len(POOL_WINDOWS)

COL_CQ, COL_KA, COL_VA = 0, Q_RANK, Q_RANK + A_WIDTH
COL_KI = COL_VA + A_WIDTH
COL_WI = COL_KI + HD
COL_QB = COL_WI + IDX_HEADS
COL_ZF, COL_IB, COL_GB = COL_QB + A_WIDTH, COL_QB + 2 * A_WIDTH, COL_QB + 3 * A_WIDTH

TILES = [(0, N_META)] + [(N_META + P * i, P) for i in range(SEQ // P)]
NT = len(TILES)
CHUNKS3 = [(0, 352), (352, 344), (696, 344)]
NKEYS = [t0 + n for t0, n in TILES]
SC_OFF = [sum(NKEYS[:m]) for m in range(NT)]
SC_COLS = sum(NKEYS)
FIRST_TOPK = 2
MASKED = -1.0e30
TAKEN = -3.0e38
TAKEN_BELOW = -2.0e38


def key_chunks(n):
    k = -(-n // 512)
    w = -(-n // k // 8) * 8
    return [(a, min(w, n - a)) for a in range(0, n, w)]


def build(nc, ins, out):
    x, meta, w_in = ins["x"][0], ins["meta_tokens"], ins["w_in"][0]
    w_in_v = w_in.rearrange("(k p) f -> p k f", p=P)

    with ExitStack() as top:
        sems = []

        def sem(name):
            sems.append(nc.alloc_semaphore(name=name))
            return sems[-1]

        @contextmanager
        def stage():
            with ExitStack() as c:
                yield c
            nc.clear_and_free_semaphores(sems)
            nc.all_engine_barrier()
            sems.clear()

        def sb(ctx, name, shape, dt=F32):
            return ctx.enter_context(nc.sbuf_tensor(name, shape, dt))

        qz_dram = nc.dram_tensor("qz_scratch", [2, 4, P, L], F32, kind="Internal").ap()
        vg_dram = nc.dram_tensor("vg_scratch", [2, L, A_WIDTH], F32, kind="Internal").ap()

        banks = top.enter_context(nc.psum_tensor("banks", [P, 8, 512], F32))
        ident = sb(top, "ident", [P, P])

        with ExitStack() as mixer:
            score = sb(mixer, "score", [P, SC_COLS])
            cqT = sb(mixer, "cqT", [P, QC, L])
            kaT = sb(mixer, "kaT", [P, 4, L])
            va = sb(mixer, "va", [P, NT, A_WIDTH])
            with stage() as c:
                projection(nc, c, sem, sb, banks, ident, x, meta, w_in_v, ins, score, cqT, kaT, va, qz_dram, vg_dram)
            oT = sb(mixer, "oT", [P, DC, L])
            with stage() as c:
                attention(nc, c, sem, sb, banks, ident, ins, score, cqT, kaT, va, oT)
            with stage() as c:
                recurrence(nc, c, sem, sb, banks, ident, ins, oT, qz_dram, vg_dram)
            y_dram = nc.dram_tensor("y_scratch", [L, D], F32, kind="Internal").ap()
            with stage() as c:
                y = sb(c, "y_mix", [P, NT, D])
                out_projection(nc, c, sem, sb, banks, x, meta, ins, oT, y, y_dram)
        y = sb(top, "y", [P, NT, D])
        tiles = list(range(NT))
        with ExitStack() as l0:
            hH = sb(l0, "hH", [P, DC, L], F32R)
            hL = sb(l0, "hL", [P, DC, L], F32R)
            with stage() as c:
                norm(nc, c, sem, sb, banks, ident, "n0", y, tiles, ins["ln_mix_g"][0], ins["ln_mix_b"][0],
                     load=y_dram, split=(hH, hL))
            with stage() as c:
                ffn(nc, c, sem, sb, banks, "f0", y, hH, hL, tiles, CHUNKS3,
                    ins["w_gate"][0], ins["w_up"][0], ins["w_down"][0])
        with ExitStack() as c:
            hT = sb(c, "hT1", [P, DC, L])
            with stage() as c2:
                norm(nc, c2, sem, sb, banks, ident, "n1", y, tiles, ins["ln_ffn_g"][0], ins["ln_ffn_b"][0], plain=hT)
            with stage() as c2:
                pool_mixer(nc, c2, sem, sb, banks, ins, y, hT)
        tiles = list(range(1, NT))
        with ExitStack() as l1:
            hH = sb(l1, "hH1", [P, DC, L], F32R)
            hL = sb(l1, "hL1", [P, DC, L], F32R)
            with stage() as c:
                norm(nc, c, sem, sb, banks, ident, "n2", y, tiles, ins["ln_mix_g"][1], ins["ln_mix_b"][1],
                     split=(hH, hL))
            with stage() as c:
                ffn(nc, c, sem, sb, banks, "f1", y, hH, hL, tiles, [(N_META, 512), (N_META + 512, 512)],
                    ins["w_gate"][1], ins["w_up"][1], ins["w_down"][1])
        with stage() as c:
            norm(nc, c, sem, sb, banks, ident, "n3", y, tiles, ins["ln_ffn_g"][1], ins["ln_ffn_b"][1], store=out)


def projection(nc, c, sem, sb, banks, ident, x, meta, w_in_v, ins, score, cqT, kaT, va, qz_dram, vg_dram):
    NX = 3
    xt = sb(c, "xt", [P, NX, D])
    hT = sb(c, "hT", [P, DC, L])
    IC = Q_RANK + HD + IDX_HEADS
    w_idx = sb(c, "w_idx", [P, DC, IC])
    w_qi = sb(c, "w_qi", [P, QC, IDX_WIDTH])
    cq_gain = sb(c, "cq_gain_sb", [P, QC])
    ki_gb = sb(c, "ki_gb", [P, 2])
    CK = Q_RANK + 2 * HD
    cqk = sb(c, "cqk", [P, NT, CK])
    squares = sb(c, "squares", [P, Q_RANK])
    wi = sb(c, "wi", [P, NT, IDX_HEADS])
    bn6 = sb(c, "bn6", [P, NT, 6])
    var = sb(c, "var", [P, NT, 2])
    sumsq = sb(c, "sumsq", [P, NT, 1])
    std = sb(c, "std_p", [P, NT, 2])
    rstd = sb(c, "rstd_p", [P, NT, 2])
    mv = sb(c, "mv_p", [P, NT, 2])
    kiT = sb(c, "kiT", [P, L])
    qiT = sb(c, "qiT", [P, 2, 8, P])
    NR = 4
    relu = sb(c, "relu", [P, NR, 512])
    top8 = sb(c, "top8", [P, NT, 8])
    mark = sb(c, "round_mark", [P, 2])
    slab = sb(c, "slab", [P, 2, DC, 512])
    NS = 4
    stage = sb(c, "stage", [P, NS, 512])

    s_x = [sem(f"x_loaded{i}") for i in range(NX)]
    w_loaded, small_loaded = sem("w_loaded"), sem("small_loaded")
    slab_loaded = [sem("slab_loaded0"), sem("slab_loaded1")]
    ident_zero, ident_done = sem("ident_zero"), sem("ident_done")
    x_transposed, hT_act, hT_dve = sem("x_transposed"), sem("hT_act"), sem("hT_dve")
    idx_psum, idx_act, idx_dve = sem("idx_psum"), sem("idx_act"), sem("idx_dve")
    stats, std_done, normed = sem("stats"), sem("std_done"), sem("normed")
    cq_psum, cqT_done = sem("cq_psum"), sem("cqT_done")
    qi_psum, qi_done = sem("qi_psum"), sem("qi_done")
    sc_psum, relu_done, acc_done = sem("sc_psum"), sem("relu_done"), sem("acc_done")
    causal_done, topk_step, mask_done, mask_all = sem("causal_done"), sem("topk_step"), sem("mask_done"), sem("mask_all")
    slab_psum, slab_out = sem("slab_psum"), sem("slab_out")
    stored = [sem(f"stored{i}") for i in range(NS)]
    link = sem("dve_link")

    SLABS = [(COL_KA, True, "ka"), (COL_VA, False, "va"), (COL_ZF, True, 1), (COL_QB, True, 0),
             (COL_IB, False, 0), (COL_GB, False, 1)]
    slab_units = []
    for j, (_, fm, dest) in enumerate(SLABS):
        if fm:
            slab_units += [(j, fm, dest, ft, a, n) for ft in range(4) for a, n in CHUNKS3]
        else:
            slab_units += [(j, fm, dest, m, *TILES[m]) for m in range(NT)]
    last_unit = {j: max(i for i, u in enumerate(slab_units) if u[0] == j) for j in range(len(SLABS))}

    TM = list(range(FIRST_TOPK, NT))
    units, order = [], []
    for i, m in enumerate(TM):
        if i == 0:
            order.append(("qi", m))
        if i + 1 < len(TM):
            order.append(("qi", TM[i + 1]))
        first = len(units)
        units += [(m, 2 * ft + b, a, n) for ft in range(8) for a, n in key_chunks(NKEYS[m]) for b in range(2)]
        order.append(("sc", m, first, len(units)))
    last_of_tile = {m: max(i for i, u in enumerate(units) if u[0] == m) for m in TM}

    def score_bank(n):
        return 2 + 3 * (n % 2) + (n // 2) % 3

    block = c.enter_context(nc.Block())

    @block.sync
    def _(sp):
        for m, (t0, n) in enumerate(TILES):
            if m >= NX:
                sp.wait_ge(x_transposed, m - NX + 1)
            src = meta if m == 0 else x[t0 - N_META:t0 - N_META + n, :]
            sp.dma_start(xt[0:n, m % NX, :], src).then_inc(s_x[m % NX], 16)
            if m == 2:
                sp.dma_start(w_idx[:, :, 0:Q_RANK], w_in_v[:, :, 0:Q_RANK]).then_inc(w_loaded, 16)
                sp.dma_start(w_idx[:, :, Q_RANK:IC], w_in_v[:, :, COL_KI:COL_QB]).then_inc(w_loaded, 16)
        sp.dma_start(w_qi[:, :, :], ins["w_uq_idx"][0].rearrange("(k p) f -> p k f", p=P)).then_inc(w_loaded, 16)
        for k in range(QC):
            sp.dma_start(cq_gain[:, k:k + 1], ins["cq_gain"][0, k * P:(k + 1) * P].rearrange("(p a) -> p a", a=1))\
              .then_inc(small_loaded, 16)
        for b in range(2):
            for i, name in enumerate(("kidx_gain", "kidx_bias")):
                sp.dma_start(ki_gb[HD * b:HD * (b + 1), i:i + 1], ins[name][0].rearrange("(p a) -> p a", a=1))\
                  .then_inc(small_loaded, 16)
        for j, (col, _, _) in enumerate(SLABS):
            if j >= 2:
                sp.wait_ge(slab_psum, last_unit[j - 2] + 1)
            sp.dma_start(slab[:, j % 2, :, :], w_in_v[:, :, col:col + 512]).then_inc(slab_loaded[j % 2], 16)

    @block.gpsimd
    def _(pool):
        nc.gpsimd.memset(ident[:, :], 0.0).then_inc(ident_zero, 1)
        pool.wait_ge(ident_zero, 1)
        nc.gpsimd.affine_select(out=ident[:, :], in_=ident[:, :], compare_op=ALU.not_equal, fill=1.0, base=0,
                                pattern=[[-1, P]], channel_multiplier=1).then_inc(ident_done, 1)
        nc.gpsimd.memset(score[:, 0:SC_OFF[FIRST_TOPK]], 0.0).then_inc(ident_zero, 1)
        pool.wait_ge(ident_zero, 2)

        def causal(m, signal):
            n = TILES[m][1]
            at = score[0:n, SC_OFF[m] + NKEYS[m] - n:SC_OFF[m] + NKEYS[m]]
            nc.gpsimd.affine_select(out=at, in_=at, compare_op=ALU.is_ge, fill=MASKED, base=0, pattern=[[-1, n]],
                                    channel_multiplier=1).then_inc(signal, 1)

        for m in range(FIRST_TOPK):
            causal(m, mask_all)
        for m in TM:
            pool.wait_ge(acc_done, last_of_tile[m] + 1)
            causal(m, causal_done)
        for i, m in enumerate(TM):
            pool.wait_ge(mask_done, i + 1)
            causal(m, mask_all)
        pool.wait_ge(mask_all, NT)

    @block.tensor
    def _(pe):
        pe.wait_ge(ident_done, 1)
        for m, (t0, n) in enumerate(TILES):
            pe.wait_ge(s_x[m % NX], 16 * (m // NX + 1))
            if m >= 2:
                pe.wait_ge(hT_act, m - 1)
                pe.wait_ge(hT_dve, m - 1)
            for k in range(DC):
                bank = 2 * (m % 2) + k // 4
                last = nc.tensor.transpose(banks[:, bank, (k % 4) * P:(k % 4) * P + n], xt[0:n, m % NX, k * P:(k + 1) * P],
                                           ident[0:n, 0:n])
            last.then_inc(x_transposed, 1)
        pe.wait_ge(w_loaded, 48)
        for m, (t0, n) in enumerate(TILES):
            pe.wait_ge(hT_act, m + 1)
            pe.wait_ge(hT_dve, m + 1)
            if m >= 2:
                pe.wait_ge(idx_dve, m - 1)
            for k in range(DC):
                last = nc.tensor.matmul(banks[0:n, 4 + m % 2, 0:IC], hT[:, k, t0:t0 + n], w_idx[:, k, :],
                                        start=(k == 0), stop=(k == DC - 1))
            last.then_inc(idx_psum, 1)
        for m, (t0, n) in enumerate(TILES):
            pe.wait_ge(normed, m + 1)
            if m >= 2:
                pe.wait_ge(cqT_done, m - 1)
            for j in range(3):
                last = nc.tensor.transpose(banks[:, 6 + m % 2, j * P:j * P + n], cqk[0:n, m, j * P:(j + 1) * P],
                                           ident[0:n, 0:n])
            last.then_inc(cq_psum, 1)
        pe.wait_ge(cqT_done, NT)
        nqi = 0
        for what in order:
            if what[0] == "qi":
                t0, n = TILES[what[1]]
                if nqi:
                    pe.wait_ge(qi_done, nqi)
                for ft in range(8):
                    for k in range(QC):
                        last = nc.tensor.matmul(banks[:, ft // 4, (ft % 4) * P:(ft % 4 + 1) * P],
                                                w_qi[:, k, ft * P:(ft + 1) * P], cqT[:, k, t0:t0 + n],
                                                start=(k == 0), stop=(k == QC - 1))
                last.then_inc(qi_psum, 1)
                nqi += 1
            else:
                _, m, a, b = what
                pe.wait_ge(qi_done, TM.index(m) + 1)
                for i in range(a, b):
                    _, h, k0, kn = units[i]
                    if i >= 6:
                        pe.wait_ge(relu_done, i - 5)
                    r = slice(HD * (h % 2), HD * (h % 2 + 1))
                    nc.tensor.matmul(banks[:, score_bank(i), 0:kn], qiT[r, m % 2, h // 2, :], kiT[r, k0:k0 + kn],
                                     start=True, stop=True).then_inc(sc_psum, 1)
        pe.wait_ge(relu_done, len(units))
        for i, (j, fm, dest, idx, a, n) in enumerate(slab_units):
            pe.wait_ge(slab_loaded[j % 2], 16 * (j // 2 + 1))
            if i >= 8:
                pe.wait_ge(slab_out, i - 7)
            for k in range(DC):
                if fm:
                    last = nc.tensor.matmul(banks[:, i % 8, 0:n], slab[:, j % 2, k, idx * P:(idx + 1) * P],
                                            hT[:, k, a:a + n], start=(k == 0), stop=(k == DC - 1))
                else:
                    last = nc.tensor.matmul(banks[0:n, i % 8, :], hT[:, k, a:a + n], slab[:, j % 2, k, :],
                                            start=(k == 0), stop=(k == DC - 1))
            last.then_inc(slab_psum, 1)

    @block.scalar
    def _(act):
        for m, (t0, n) in enumerate(TILES):
            act.wait_ge(x_transposed, m + 1)
            src = banks[:, 2 * (m % 2), :].rearrange("p (k t) -> p k t", k=4)[:, :, 0:n]
            nc.scalar.activation(hT[:, 0:4, t0:t0 + n], src, ACT.Copy).then_inc(hT_act, 1)
        act.wait_ge(link, 1)
        for m, (t0, n) in enumerate(TILES):
            act.wait_ge(idx_dve, m + 1)
            if m:
                act.wait_ge(idx_act, m)
            nc.scalar.activation(squares[0:n, :], cqk[0:n, m, 0:Q_RANK], ACT.Square,
                                 accum_out=sumsq[0:n, m, :]).then_inc(idx_act, 1)
        act.wait_ge(stats, 1)
        nc.scalar.activation(std[:, :, :], var[:, :, :], ACT.Sqrt).then_inc(std_done, 1)
        nqi = 0
        for what in order:
            if what[0] == "qi":
                act.wait_ge(qi_psum, nqi + 1)
                nc.scalar.activation(qiT[:, what[1] % 2, :, :].rearrange("p f t -> p (f t)"),
                                     banks[:, 0:2, :].rearrange("p b t -> p (b t)"), ACT.Copy).then_inc(qi_done, 1)
                nqi += 1
            else:
                for i in range(what[2], what[3]):
                    kn = units[i][3]
                    act.wait_ge(sc_psum, i + 1)
                    if i >= NR:
                        act.wait_ge(acc_done, i - NR + 1)
                    nc.scalar.activation(relu[:, i % NR, 0:kn], banks[:, score_bank(i), 0:kn], ACT.Relu)\
                      .then_inc(relu_done, 1)
        staged = 0
        for i, (j, fm, dest, idx, a, n) in enumerate(slab_units):
            act.wait_ge(slab_psum, i + 1)
            if dest == "ka":
                nc.scalar.activation(kaT[:, idx, a:a + n], banks[:, i % 8, 0:n], ACT.Copy).then_inc(slab_out, 1)
                continue
            if dest == "va":
                nc.scalar.activation(va[0:n, idx, :], banks[0:n, i % 8, :], ACT.Copy).then_inc(slab_out, 1)
                continue
            s = staged % NS
            if staged >= NS:
                act.wait_ge(stored[s], 16 * (staged // NS))
            if fm:
                src, dst, to = banks[:, i % 8, 0:n], stage[:, s, 0:n], qz_dram[dest, idx, :, a:a + n]
            else:
                src, dst, to = banks[0:n, i % 8, :], stage[0:n, s, :], vg_dram[dest, a:a + n, :]
            nc.scalar.activation(dst, src, ACT.Silu if (not fm and dest == 1) else ACT.Copy).then_inc(slab_out, 1)
            act.wait_ge(slab_out, i + 1)
            act.dma_start(to, dst).then_inc(stored[s], 16)
            staged += 1
        for s in range(NS):
            act.wait_ge(stored[s], 16 * ((staged - s + NS - 1) // NS))

    @block.vector
    def _(dve):
        chain = [0]

        def linked(ins_):
            chain[0] += 1
            ins_.then_inc(link, 1)
            dve.wait_ge(link, chain[0])

        linked(nc.vector.memset(sumsq[:, :, :], 1.0))
        linked(nc.vector.memset(var[:, :, :], 1.0))
        linked(nc.vector.memset(mv[:, :, :], 1.0))
        for m, (t0, n) in enumerate(TILES):
            dve.wait_ge(x_transposed, m + 1)
            src = banks[:, 2 * (m % 2) + 1, :].rearrange("p (k t) -> p k t", k=4)[:, :, 0:n]
            nc.vector.tensor_copy(hT[:, 4:8, t0:t0 + n], src).then_inc(hT_dve, 1)
        for m, (t0, n) in enumerate(TILES):
            dve.wait_ge(idx_psum, m + 1)
            bank = banks[0:n, 4 + m % 2, :]
            nc.vector.tensor_copy(cqk[0:n, m, 0:Q_RANK + HD], bank[:, 0:Q_RANK + HD])
            nc.vector.bn_stats(bn6[0:n, m, :], bank[:, Q_RANK:Q_RANK + HD])
            nc.vector.tensor_scalar(wi[0:n, m, :], bank[:, Q_RANK + HD:IC], IDX_HEADS ** -0.5 * HD ** -0.5, None,
                                    ALU.mult).then_inc(idx_dve, 1)
        dve.wait_ge(idx_dve, NT)
        for m, (t0, n) in enumerate(TILES):
            last = nc.vector.bn_aggr(mv[0:n, m, :], bn6[0:n, m, :])
        linked(last)
        dve.wait_ge(idx_act, NT)
        linked(nc.vector.tensor_scalar(var[:, :, 0:1], sumsq[:, :, :], 1.0 / Q_RANK, LN_EPS, ALU.mult, ALU.add))
        nc.vector.tensor_scalar(var[:, :, 1:2], mv[:, :, 1:2], LN_EPS, None, ALU.add).then_inc(stats, 1)
        dve.wait_ge(std_done, 1)
        linked(nc.vector.reciprocal(rstd[:, :, :], std[:, :, :]))
        dve.wait_ge(idx_dve, NT)
        for m, (t0, n) in enumerate(TILES):
            k0 = Q_RANK
            nc.vector.tensor_scalar(cqk[0:n, m, k0 + HD:k0 + 2 * HD], cqk[0:n, m, k0:k0 + HD], mv[0:n, m, 0:1],
                                    rstd[0:n, m, 1:2], ALU.subtract, ALU.mult)
            linked(nc.vector.tensor_scalar(cqk[0:n, m, 0:k0], cqk[0:n, m, 0:k0], rstd[0:n, m, 0:1], None, ALU.mult))
            nc.vector.tensor_scalar(cqk[0:n, m, k0:k0 + HD], cqk[0:n, m, k0:k0 + HD], mv[0:n, m, 0:1],
                                    rstd[0:n, m, 1:2], ALU.subtract, ALU.mult).then_inc(normed, 1)
        dve.wait_ge(small_loaded, 16 * (QC + 4))
        for m, (t0, n) in enumerate(TILES):
            dve.wait_ge(cq_psum, m + 1)
            bank = banks[:, 6 + m % 2, :]
            for k in range(QC):
                nc.vector.tensor_scalar(cqT[:, k, t0:t0 + n], bank[:, k * P:k * P + n], cq_gain[:, k:k + 1], None,
                                        ALU.mult)
            nc.vector.tensor_scalar(kiT[:, t0:t0 + n], bank[:, QC * P:QC * P + n], ki_gb[:, 0:1], ki_gb[:, 1:2],
                                    ALU.mult, ALU.add).then_inc(cqT_done, 1)
        for i, (m, h, a, n) in enumerate(units):
            dve.wait_ge(relu_done, i + 1)
            at = score[:, SC_OFF[m] + a:SC_OFF[m] + a + n]
            if h == 0:
                nc.vector.tensor_scalar(at, relu[:, i % NR, 0:n], wi[:, m, h:h + 1], None, ALU.mult)\
                  .then_inc(acc_done, 1)
            else:
                dve.wait_ge(acc_done, i)
                nc.vector.scalar_tensor_tensor(out=at, in0=relu[:, i % NR, 0:n], scalar=wi[:, m, h:h + 1], in1=at,
                                               op0=ALU.mult, op1=ALU.add).then_inc(acc_done, 1)
        NM = len(TM)
        FREE = 1
        dve.wait_ge(causal_done, NM)
        dve.sem_inc(topk_step, FREE)
        with dve.Fori(0, TOPK // 8) as r:
            for i, m in enumerate(TM):
                at = score[:, SC_OFF[m]:SC_OFF[m] + NKEYS[m]]
                if i == 0:
                    dve.wait_ge(topk_step, FREE + r * (2 * NM))
                    nc.vector.memset(mark[:, 0:1], 0.0)
                nc.vector.max(top8[:, m, :], at).then_inc(topk_step, 1)
            for i, m in enumerate(TM):
                at = score[:, SC_OFF[m]:SC_OFF[m] + NKEYS[m]]
                if i == 0:
                    dve.wait_ge(topk_step, FREE + r * (2 * NM) + NM)
                    nc.vector.memset(mark[:, 1:2], 0.0)
                nc.vector.match_replace(at, top8[:, m, :], at, TAKEN).then_inc(topk_step, 1)
        dve.wait_ge(topk_step, FREE + TOPK // 8 * 2 * NM)
        for m in TM:
            at = score[:, SC_OFF[m]:SC_OFF[m] + NKEYS[m]]
            nc.vector.tensor_scalar(at, at, TAKEN_BELOW, MASKED, ALU.is_ge, ALU.mult).then_inc(mask_done, 1)


def attention(nc, c, sem, sb, banks, ident, ins, score, cqT, kaT, va, oT):
    w_qa = sb(c, "w_qa", [P, QC, A_WIDTH])
    qaT = sb(c, "qaT", [P, 2, 4, P])
    probs = sb(c, "probs", [P, 2, L])
    pT = sb(c, "pT", [P, 2, NT, P])
    nmax = sb(c, "nmax", [P, 2, 2])
    sums = sb(c, "sums", [P, 2, A_HEADS])
    rsums = sb(c, "rsums", [P, 2, A_HEADS])
    o_tok = sb(c, "o_tok", [P, 2, A_WIDTH])
    REL0 = TILES[-1][0]
    rel_i = sb(c, "rel_i", [2, L], I32)
    rel_f = sb(c, "rel_f", [2, L])
    rel = sb(c, "rel", [2, L], F32R)
    qpos_i = sb(c, "qpos_i", [2, P], I32)
    qpos = sb(c, "qpos", [2, P])
    alibi = sb(c, "alibi", [2, A_HEADS, P], F32R)

    w_loaded, iotas, rel_done, alibi_done = sem("wqa_loaded"), sem("iotas"), sem("rel_done"), sem("alibi_done")
    qa_psum, qa_done = sem("qa_psum"), sem("qa_done")
    qk_done, nmax_raw, nmax_done, exp_done = sem("qk_done"), sem("nmax_raw"), sem("nmax_done"), sem("exp_done")
    pt_psum, pt_act, pt_dve, pv_done = sem("pt_psum"), sem("pt_act"), sem("pt_dve"), sem("pv_done")
    rs_done, otok_done, ot_psum, oT_done = sem("rs_done"), sem("otok_done"), sem("ot_psum"), sem("oT_done")

    units = [(m, h) for m in range(NT) for h in range(A_HEADS)]
    NU = len(units)

    def dve_turns(i):
        return sum(m > 4 for m, _ in units[:i + 1])

    logits = banks[:, 0:3, :].rearrange("p b t -> p (b t)")

    block = c.enter_context(nc.Block())

    @block.sync
    def _(sp):
        sp.dma_start(w_qa[:, :, :], ins["w_uq"][0].rearrange("(k p) f -> p k f", p=P)).then_inc(w_loaded, 16)

    @block.gpsimd
    def _(pool):
        nc.gpsimd.iota(rel_i[:, :], pattern=[[1, L]], base=-REL0, channel_multiplier=0).then_inc(iotas, 1)
        nc.gpsimd.iota(qpos_i[:, :], pattern=[[-1, P]], base=0, channel_multiplier=0).then_inc(iotas, 1)
        pool.wait_ge(iotas, 2)
        nc.gpsimd.tensor_copy(rel_f[:, :], rel_i[:, :]).then_inc(iotas, 1)
        nc.gpsimd.tensor_copy(qpos[:, :], qpos_i[:, :]).then_inc(iotas, 1)
        pool.wait_ge(iotas, 4)
        nc.gpsimd.affine_select(out=rel_f[:, :], in_=rel_f[:, :], compare_op=ALU.is_ge, fill=1.0, base=0,
                                pattern=[[0, L]], channel_multiplier=-1).then_inc(rel_done, 1)
        nc.gpsimd.affine_select(out=qpos[:, :], in_=qpos[:, :], compare_op=ALU.is_gt, fill=1.0, base=0,
                                pattern=[[0, P]], channel_multiplier=1).then_inc(rel_done, 1)

    @block.tensor
    def _(pe):
        pe.wait_ge(w_loaded, 16)
        pe.wait_ge(alibi_done, 1)

        def project(m):
            t0, n = TILES[m]
            if m >= 1:
                pe.wait_ge(qa_done, m)
            if m >= 2:
                pe.wait_ge(oT_done, m - 1)
            for ft in range(4):
                for k in range(QC):
                    last = nc.tensor.matmul(banks[:, 7, ft * P:ft * P + n], w_qa[:, k, ft * P:(ft + 1) * P],
                                            cqT[:, k, t0:t0 + n], start=(k == 0), stop=(k == QC - 1))
            last.then_inc(qa_psum, 1)

        def qk(i):
            m, h = units[i]
            t0, n = TILES[m]
            if h == 0:
                pe.wait_ge(qa_done, m + 1)
            if i:
                pe.wait_ge(nmax_raw, i)
            r = slice(HD * (h % 2), HD * (h % 2 + 1))
            for a in range(0, NKEYS[m], 512):
                kn = min(512, NKEYS[m] - a)
                nc.tensor.matmul(logits[0:n, a:a + kn], alibi[:, h, 0:n], rel[:, REL0 - t0 + a:REL0 - t0 + a + kn],
                                 start=True, stop=False)
                last = nc.tensor.matmul(logits[0:n, a:a + kn], qaT[r, m % 2, h // 2, 0:n], kaT[r, h // 2, a:a + kn],
                                        start=False, stop=True)
            last.then_inc(qk_done, 1)

        def turn(i):
            m, h = units[i]
            n = TILES[m][1]
            pe.wait_ge(exp_done, i + 1)
            if i:
                pe.wait_ge(pt_act, i)
                if dve_turns(i - 1):
                    pe.wait_ge(pt_dve, dve_turns(i - 1))
            for j in range(m + 1):
                k0, kn = TILES[j]
                bank = 5 if j == 0 else 3 + (j - 1) // 4
                col = 0 if j == 0 else (j - 1) % 4 * P
                last = nc.tensor.transpose(banks[0:kn, bank, col:col + n], probs[0:n, i % 2, k0:k0 + kn],
                                           ident[0:n, 0:n])
            last.then_inc(pt_psum, 1)

        def pv(i):
            m, h = units[i]
            n = TILES[m][1]
            pe.wait_ge(pt_act, i + 1)
            if m > 4:
                pe.wait_ge(pt_dve, dve_turns(i))
            if h == 0 and m:
                pe.wait_ge(otok_done, m)
            for j in range(m + 1):
                kn = TILES[j][1]
                last = nc.tensor.matmul(banks[0:n, 6, h * HD:(h + 1) * HD], pT[0:kn, i % 2, j, 0:n],
                                        va[0:kn, j, h * HD:(h + 1) * HD], start=(j == 0), stop=(j == m))
            last.then_inc(pv_done, 1)
            return m if h == A_HEADS - 1 else None

        def turn_out(m):
            n = TILES[m][1]
            pe.wait_ge(otok_done, m + 1)
            if m + 1 < NT:
                pe.wait_ge(qa_done, m + 2)
            for ft in range(4):
                last = nc.tensor.transpose(banks[:, 7, ft * P:ft * P + n], o_tok[0:n, m % 2, ft * P:(ft + 1) * P],
                                           ident[0:n, 0:n])
            last.then_inc(ot_psum, 1)

        project(0)
        for i in range(NU + 4):
            if i < NU:
                qk(i)
                if units[i][1] == 4 and units[i][0] + 1 < NT:
                    project(units[i][0] + 1)
            if 1 <= i <= NU:
                turn(i - 1)
            if 2 <= i <= NU + 1:
                pv(i - 2)
            if i >= 4 and units[i - 4][1] == A_HEADS - 1:
                turn_out(units[i - 4][0])

    @block.scalar
    def _(act):
        def project(m):
            n = TILES[m][1]
            act.wait_ge(qa_psum, m + 1)
            nc.scalar.activation(qaT[:, m % 2, :, 0:n], banks[:, 7, :].rearrange("p (f t) -> p f t", f=4)[:, :, 0:n],
                                 ACT.Copy, scale=HD ** -0.5).then_inc(qa_done, 1)

        def exps(i):
            m, h = units[i]
            n = TILES[m][1]
            act.wait_ge(nmax_done, i + 1)
            at = probs[0:n, i % 2, 0:NKEYS[m]]
            if h == 0 and m >= 2:
                act.wait_ge(rs_done, m - 1)
            nc.scalar.activation(at, at, ACT.Exp, bias=nmax[0:n, i % 2, 1:2], accum_out=sums[0:n, m % 2, h:h + 1])\
              .then_inc(exp_done, 1)

        def turned(i):
            m, h = units[i]
            n = TILES[m][1]
            act.wait_ge(pt_psum, i + 1)
            if i >= 2:
                act.wait_ge(pv_done, i - 1)
            last = nc.scalar.activation(pT[0:N_META, i % 2, 0, 0:n], banks[0:N_META, 5, 0:n], ACT.Copy)
            if m:
                k = min(4, m)
                last = nc.scalar.activation(pT[:, i % 2, 1:1 + k, 0:n],
                                            banks[:, 3, 0:k * P].rearrange("p (f t) -> p f t", f=k), ACT.Copy)
            last.then_inc(pt_act, 1)

        project(0)
        for i in range(NU + 1):
            if i < NU:
                exps(i)
                if units[i][1] == 4 and units[i][0] + 1 < NT:
                    project(units[i][0] + 1)
            if i >= 1:
                turned(i - 1)

    @block.vector
    def _(dve):
        dve.wait_ge(rel_done, 2)
        nc.vector.tensor_copy(rel[:, :], rel_f[:, :])
        for h in range(A_HEADS):
            last = nc.vector.tensor_scalar(alibi[:, h, :], qpos[:, :], 2.0 ** (-8.0 * (h + 1) / A_HEADS), None, ALU.mult)
        last.then_inc(alibi_done, 1)

        def masked(i):
            m, h = units[i]
            n = TILES[m][1]
            N = NKEYS[m]
            dve.wait_ge(qk_done, i + 1)
            if i >= 2:
                dve.wait_ge(pt_psum, i - 1)
                dve.wait_ge(exp_done, i - 1)
            nc.vector.tensor_tensor_reduce(out=probs[0:n, i % 2, 0:N], in0=logits[0:n, 0:N],
                                           in1=score[0:n, SC_OFF[m]:SC_OFF[m] + N], scale=1.0, scalar=TAKEN,
                                           op0=ALU.add, op1=ALU.max, accum_out=nmax[0:n, i % 2, 0:1])\
              .then_inc(nmax_raw, 1)
            dve.wait_ge(nmax_raw, i + 1)
            nc.vector.tensor_scalar(nmax[0:n, i % 2, 1:2], nmax[0:n, i % 2, 0:1], -1.0, None, ALU.mult)\
              .then_inc(nmax_done, 1)

        def turned(i):
            m, h = units[i]
            n = TILES[m][1]
            dve.wait_ge(pt_psum, i + 1)
            if i >= 2:
                dve.wait_ge(pv_done, i - 1)
            if m > 4:
                k = m - 4
                nc.vector.tensor_copy(pT[:, i % 2, 5:5 + k, 0:n],
                                      banks[:, 4, 0:k * P].rearrange("p (f t) -> p f t", f=k)).then_inc(pt_dve, 1)

        def normed(m):
            n = TILES[m][1]
            dve.wait_ge(exp_done, A_HEADS * (m + 1))
            nc.vector.reciprocal(rsums[0:n, m % 2, :], sums[0:n, m % 2, :]).then_inc(rs_done, 1)
            dve.wait_ge(rs_done, m + 1)
            dve.wait_ge(pv_done, A_HEADS * (m + 1))
            if m >= 2:
                dve.wait_ge(ot_psum, m - 1)
            nc.vector.tensor_tensor(o_tok[0:n, m % 2, :].rearrange("p (h e) -> p h e", h=A_HEADS),
                                    banks[0:n, 6, :].rearrange("p (h e) -> p h e", h=A_HEADS),
                                    rsums[0:n, m % 2, :].rearrange("p (h e) -> p h e", e=1).to_broadcast([n, A_HEADS, HD]),
                                    ALU.mult).then_inc(otok_done, 1)

        def out(m):
            t0, n = TILES[m]
            dve.wait_ge(ot_psum, m + 1)
            nc.vector.tensor_copy(oT[:, 0:4, t0:t0 + n], banks[:, 7, :].rearrange("p (f t) -> p f t", f=4)[:, :, 0:n])\
              .then_inc(oT_done, 1)

        for i in range(NU + 4):
            if i < NU:
                masked(i)
            if 1 <= i <= NU:
                turned(i - 1)
            if i >= 3 and i - 3 < NU and units[i - 3][1] == A_HEADS - 1:
                normed(units[i - 3][0])
            if i >= 4 and units[i - 4][1] == A_HEADS - 1:
                out(units[i - 4][0])


def recurrence(nc, c, sem, sb, banks, ident, ins, oT, qz_dram, vg_dram):
    W = 4 * P
    PAD = P - N_META
    PAD_Z = 80.0
    LEVELS = 7
    zt = sb(c, "zt", [P, 2, 4, P])
    qt = sb(c, "qt", [P, 2, 4, P])
    vt = sb(c, "vt", [P, 2, A_WIDTH])
    gt = sb(c, "gt", [P, 2, A_WIDTH])
    t1 = sb(c, "t1", [P, W])
    u = sb(c, "u", [P, W])
    lnw = sb(c, "lnw", [P, W])
    wr = sb(c, "wr", [P, W])
    e2 = sb(c, "e2", [P, W])
    key = sb(c, "key", [P, W])
    logf = sb(c, "logf", [P, W])
    b = sb(c, "b", [P, W])
    keep = sb(c, "keep", [P, W])
    ex = sb(c, "ex", [P, 2, W])
    xl = sb(c, "xl", [P, 2, W])
    eb = sb(c, "eb", [P, W])
    qe = sb(c, "qe", [P, W])
    kd = sb(c, "kd", [P, W])
    ke = sb(c, "ke", [P, W])
    elast = sb(c, "elast", [P, 4])
    k_tok = sb(c, "k_tok", [P, W])
    S = sb(c, "S", [P, 8, P])
    state = sb(c, "state", [P, 4, P])
    it_s = sb(c, "it_s", [P, P], I32)
    it_t = sb(c, "it_t", [P, P], I32)
    xor = sb(c, "xor", [P, P], I32)
    shifted = sb(c, "shifted", [P, P], I32)
    after = sb(c, "after", [P, P], I32)
    masks = sb(c, "masks", [P, LEVELS + 1, P], I32)
    gain = sb(c, "gain", [P, A_WIDTH])
    gg = sb(c, "gg", [P, 2, A_WIDTH])
    sq = sb(c, "sq", [P, A_WIDTH])
    on = sb(c, "on", [P, A_WIDTH])
    ssum = sb(c, "ssum", [P, 8])
    stdh = sb(c, "stdh", [P, 8])
    rsh = sb(c, "rsh", [P, 8])

    loaded = [sem("rec_loaded0"), sem("rec_loaded1")]
    gain_loaded, pads, iota_done = sem("gain_loaded"), sem("pads"), sem("iota_done")
    vlink, alink = sem("rec_vector"), sem("rec_scalar")
    z_read, ex_in, ex_out, x_done, gram_psum, gram_read = (sem("z_read"), sem("ex_in"), sem("ex_out"), sem("x_done"),
                                                           sem("gram_psum"), sem("gram_read"))
    gates = {k: sem(f"g_{k}") for k in ("abs", "exp", "w", "ln", "mz", "e2", "key", "b", "eb", "qe", "kd", "ked", "ke",
                                        "kt", "ktok", "st", "state", "out", "sq", "ssum", "std", "on", "gg", "ot", "oT")}
    block = c.enter_context(nc.Block())

    def gram_index(m, l, back=0):
        i = m * LEVELS + l + back
        return i // LEVELS * (LEVELS + 1) + i % LEVELS + 2

    def halves(ap, l):
        h = 2 ** l
        return ap.rearrange("p (n two h) -> p n two h", two=2, h=h)

    @block.sync
    def _(sp):
        sp.dma_start(gain[:, :], ins["onorm_gain"][0:1, :].to_broadcast([P, A_WIDTH])).then_inc(gain_loaded, 16)
        sp.wait_ge(pads, 4)
        for m, (t0, n) in enumerate(TILES):
            s = m % 2
            if m >= 2:
                sp.wait_ge(gates["state"], m - 1)
                sp.wait_ge(gates["on"], m - 1)
                sp.wait_ge(gates["out"], m - 1)
            r = slice(P - n, P)
            for w, dst in ((1, zt), (0, qt)):
                sp.dma_start(dst[:, s, :, r], qz_dram[w, :, :, t0:t0 + n].rearrange("f p t -> p f t")).then_inc(loaded[s], 16)
            for w, dst in ((0, vt), (1, gt)):
                sp.dma_start(dst[r, s, :], vg_dram[w, t0:t0 + n, :]).then_inc(loaded[s], 16)

    @block.gpsimd
    def _(pool):
        nc.gpsimd.memset(zt[:, 0, :, :], PAD_Z).then_inc(pads, 1)
        nc.gpsimd.memset(qt[:, 0, :, :], 0.0).then_inc(pads, 1)
        nc.gpsimd.memset(vt[:, 0, :], 0.0).then_inc(pads, 1)
        nc.gpsimd.memset(gt[:, 0, :], 0.0).then_inc(pads, 1)
        nc.gpsimd.iota(it_s[:, :], pattern=[[0, P]], base=0, channel_multiplier=1).then_inc(iota_done, 1)
        nc.gpsimd.iota(it_t[:, :], pattern=[[1, P]], base=0, channel_multiplier=0).then_inc(iota_done, 1)
        pool.wait_ge(gain_loaded, 16)
        for m in range(NT):
            s = m % 2
            pool.wait_ge(loaded[s], 64 * (m // 2 + 1))
            if m >= 2:
                pool.wait_ge(gates["on"], m - 1)
            nc.gpsimd.tensor_tensor(gg[:, s, :], gt[:, s, :], gain[:, :], ALU.mult).then_inc(gates["gg"], 1)
            pool.wait_ge(gates["key"], m + 1)
            q2 = qt[:, s, :, :].rearrange("p f t -> p (f t)")
            for l in range(LEVELS):
                i = m * LEVELS + l
                pool.wait_ge(ex_out, i + 1)
                if i >= 2:
                    pool.wait_ge(gram_psum, gram_index(m, l, -2))
                e, xo = halves(ex[:, i % 2, :], l), halves(xl[:, i % 2, :], l)
                nc.gpsimd.tensor_tensor(xo[:, :, 0, :], e[:, :, 0, :], halves(key[:, :], l)[:, :, 0, :], ALU.mult)
                nc.gpsimd.tensor_tensor(xo[:, :, 1, :], e[:, :, 1, :], halves(q2, l)[:, :, 1, :], ALU.mult)\
                  .then_inc(x_done, 1)

    @block.scalar
    def _(act):
        def step(name, m, ins_):
            ins_.then_inc(gates[name], 1)

        for m in range(NT):
            s = m % 2
            act.wait_ge(loaded[s], 64 * (m // 2 + 1))
            z = zt[:, s, :, :].rearrange("p f t -> p (f t)")
            if m:
                act.wait_ge(gates["key"], m)
                act.wait_ge(gates["b"], m)
            step("abs", m, nc.scalar.activation(t1[:, :], z, ACT.Abs))
            act.wait_ge(gates["abs"], m + 1)
            step("exp", m, nc.scalar.activation(u[:, :], t1[:, :], ACT.Exp, scale=-1.0))
            act.wait_ge(gates["w"], m + 1)
            step("ln", m, nc.scalar.activation(lnw[:, :], wr[:, :], ACT.Ln))
            act.wait_ge(gates["mz"], m + 1)
            step("e2", m, nc.scalar.activation(e2[:, :], e2[:, :], ACT.Exp, scale=-1.0))
            act.wait_ge(gates["b"], m + 1)
            if m:
                act.wait_ge(gates["qe"], m)
            step("eb", m, nc.scalar.activation(eb[:, :], b[:, :], ACT.Exp))
            act.wait_ge(gates["kd"], m + 1)
            step("ked", m, nc.scalar.activation(kd[:, :], kd[:, :], ACT.Exp))
            for l in range(LEVELS):
                i = m * LEVELS + l
                act.wait_ge(ex_in, i + 1)
                nc.scalar.activation(ex[:, i % 2, :], ex[:, i % 2, :], ACT.Exp).then_inc(ex_out, 1)
            act.wait_ge(gates["kt"], m + 1)
            if m:
                act.wait_ge(gates["st"], m)
            step("ktok", m, nc.scalar.activation(k_tok[:, :], banks[:, 4, :], ACT.Copy))
            act.wait_ge(gates["ssum"], m + 1)
            step("std", m, nc.scalar.activation(stdh[:, :], ssum[:, :], ACT.Sqrt))

    @block.vector
    def _(dve):
        chain = [0]

        def linked(ins_):
            chain[0] += 1
            ins_.then_inc(vlink, 1)
            dve.wait_ge(vlink, chain[0])

        dve.wait_ge(iota_done, 2)
        linked(nc.vector.tensor_tensor(xor[:, :], it_s[:, :], it_t[:, :], ALU.bitwise_xor))
        linked(nc.vector.tensor_tensor(after[:, :], it_t[:, :], it_s[:, :], ALU.is_gt))
        for l in range(LEVELS):
            linked(nc.vector.tensor_scalar(shifted[:, :], xor[:, :], l, None, ALU.logical_shift_right))
            linked(nc.vector.scalar_tensor_tensor(out=masks[:, l, :], in0=shifted[:, :], scalar=1.0, in1=after[:, :],
                                                  op0=ALU.is_equal, op1=ALU.mult))
        linked(nc.vector.tensor_scalar(masks[:, LEVELS, :], xor[:, :], 0.0, None, ALU.is_equal))
        linked(nc.vector.memset(keep[:, :], 1.0))
        linked(nc.vector.memset(keep[:, :].rearrange("p (f t) -> p f t", f=4)[:, :, 0:1], 0.0))
        linked(nc.vector.memset(S[:, :, :], 0.0))
        linked(nc.vector.memset(state[:, :, :], 0.0))
        for m in range(NT):
            s = m % 2
            t0, n = TILES[m]
            z = zt[:, s, :, :].rearrange("p f t -> p (f t)")
            q2 = qt[:, s, :, :].rearrange("p f t -> p (f t)")
            dve.wait_ge(gates["exp"], m + 1)
            nc.vector.tensor_scalar(wr[:, :], u[:, :], 1.0, None, ALU.add).then_inc(gates["w"], 1)
            nc.vector.tensor_scalar(e2[:, :], z, 0.0, None, ALU.max).then_inc(gates["mz"], 1)
            dve.wait_ge(gates["ln"], m + 1)
            linked(nc.vector.scalar_tensor_tensor(out=logf[:, :], in0=z, scalar=0.0, in1=lnw[:, :], op0=ALU.min,
                                                  op1=ALU.subtract))
            if m:
                dve.wait_ge(gates["eb"], m)
            nc.vector.tensor_tensor_scan(b[:, :], keep[:, :], logf[:, :], 0.0, ALU.mult, ALU.add).then_inc(gates["b"], 1)
            linked(nc.vector.reciprocal(wr[:, :], wr[:, :]))
            dve.wait_ge(gates["e2"], m + 1)
            if m:
                dve.wait_ge(x_done, LEVELS * m)
                dve.wait_ge(gram_psum, (LEVELS + 1) * m)
            nc.vector.tensor_tensor(key[:, :], e2[:, :], wr[:, :], ALU.mult).then_inc(gates["key"], 1)
            dve.wait_ge(gates["b"], m + 1)
            b3 = b[:, :].rearrange("p (f t) -> p f t", f=4)
            last_b = b3[:, :, P - 1:P].to_broadcast([P, 4, P])
            if m:
                dve.wait_ge(gates["ke"], m)
            nc.vector.tensor_tensor(kd[:, :].rearrange("p (f t) -> p f t", f=4), last_b, b3, ALU.subtract)\
              .then_inc(gates["kd"], 1)

            def level_exponents(l):
                i = m * LEVELS + l
                if i >= 2:
                    dve.wait_ge(x_done, i - 1)
                h = 2 ** l
                bl, el = halves(b[:, :], l), halves(ex[:, i % 2, :], l)
                ref = bl[:, :, 0, h - 1:h].to_broadcast([P, W // (2 * h), h])
                nc.vector.tensor_tensor(el[:, :, 0, :], ref, bl[:, :, 0, :], ALU.subtract)
                nc.vector.tensor_tensor(el[:, :, 1, :], bl[:, :, 1, :], ref, ALU.subtract).then_inc(ex_in, 1)

            def level_scores(g, mask):
                if g:
                    dve.wait_ge(gram_read, g)
                for par in range(2):
                    n_ = 2 * g + par
                    dve.wait_ge(gram_psum, g + 1)
                    Sv = S[:, :, :].rearrange("p (f two) t -> p two f t", two=2)[:, par, :, :]
                    bank = (g % 2) * 2 + par
                    mk = masks[:, mask:mask + 1, :].to_broadcast([P, 4, P])
                    last = nc.vector.copy_predicated(Sv, mk, banks[:, bank, :].rearrange("p (f t) -> p f t", f=4))
                last.then_inc(gram_read, 1)

            level_exponents(0)
            if m:
                dve.wait_ge(gates["out"], m)
            level_scores(m * (LEVELS + 1), LEVELS)
            level_exponents(1)
            dve.wait_ge(gates["eb"], m + 1)
            nc.vector.tensor_tensor(qe[:, :], q2, eb[:, :], ALU.mult).then_inc(gates["qe"], 1)
            dve.wait_ge(gates["ked"], m + 1)
            dve.wait_ge(gates["key"], m + 1)
            if m:
                dve.wait_ge(gates["kt"], m)
            nc.vector.tensor_tensor(ke[:, :], key[:, :], kd[:, :], ALU.mult).then_inc(gates["ke"], 1)
            nc.vector.tensor_copy(elast[:, :], eb[:, :].rearrange("p (f t) -> p f t", f=4)[:, :, P - 1])
            for l in range(LEVELS):
                if l + 2 < LEVELS:
                    level_exponents(l + 2)
                level_scores(m * (LEVELS + 1) + l + 1, l)
            dve.wait_ge(gates["st"], m + 1)
            dve.wait_ge(gates["out"], m + 1)
            for f in range(4):
                for par in range(2):
                    r = slice(HD * par, HD * (par + 1))
                    last = nc.vector.scalar_tensor_tensor(out=state[r, f, r], in0=state[r, f, r],
                                                          scalar=elast[r, f:f + 1], in1=banks[r, 5, f * P + HD * par:f * P + HD * (par + 1)],
                                                          op0=ALU.mult, op1=ALU.add)
            last.then_inc(gates["state"], 1)
            o8 = banks[:, 6, :].rearrange("p (h e) -> p h e", h=8)
            if m:
                dve.wait_ge(gates["ot"], m)
            linked(nc.vector.tensor_copy(on[:, :], banks[:, 6, :]))
            linked(nc.vector.tensor_tensor(sq[:, :], on[:, :], on[:, :], ALU.mult))
            linked(nc.vector.tensor_reduce(ssum[:, :], sq[:, :].rearrange("p (h e) -> p h e", h=8),
                                           mybir.AxisListType.X, ALU.add))
            nc.vector.tensor_scalar(ssum[:, :], ssum[:, :], 1.0 / HD, LN_EPS, ALU.mult, ALU.add).then_inc(gates["ssum"], 1)
            dve.wait_ge(gates["std"], m + 1)
            linked(nc.vector.reciprocal(rsh[:, :], stdh[:, :]))
            linked(nc.vector.tensor_tensor(on[:, :].rearrange("p (h e) -> p h e", h=8),
                                           on[:, :].rearrange("p (h e) -> p h e", h=8),
                                           rsh[:, :].rearrange("p (h e) -> p h e", e=1).to_broadcast([P, 8, HD]), ALU.mult))
            dve.wait_ge(gates["gg"], m + 1)
            nc.vector.tensor_tensor(on[:, :], on[:, :], gg[:, s, :], ALU.mult).then_inc(gates["on"], 1)
            dve.wait_ge(gates["ot"], m + 1)
            nc.vector.tensor_copy(oT[:, 4:8, t0:t0 + n],
                                  banks[:, 7, :].rearrange("p (f t) -> p f t", f=4)[:, :, P - n:P]).then_inc(gates["oT"], 1)

    @block.tensor
    def _(pe):
        for m in range(NT):
            s = m % 2

            def gram(g, keys, queries):
                if g >= 2:
                    pe.wait_ge(gram_read, g - 1)
                for f in range(4):
                    for par in range(2):
                        r = slice(HD * par, HD * (par + 1))
                        last = nc.tensor.matmul(banks[:, (g % 2) * 2 + par, f * P:(f + 1) * P],
                                                keys[r, f * P:(f + 1) * P], queries[r, f * P:(f + 1) * P],
                                                start=True, stop=True)
                last.then_inc(gram_psum, 1)

            q2 = qt[:, s, :, :].rearrange("p f t -> p (f t)")
            pe.wait_ge(loaded[s], 64 * (m // 2 + 1))
            pe.wait_ge(gates["key"], m + 1)
            gram(m * (LEVELS + 1), key, q2)
            for l in range(LEVELS):
                i = m * LEVELS + l
                pe.wait_ge(x_done, i + 1)
                gram(m * (LEVELS + 1) + l + 1, xl[:, i % 2, :], xl[:, i % 2, :])
                if l == 1:
                    pe.wait_ge(gates["ke"], m + 1)
                    if m:
                        pe.wait_ge(gates["ktok"], m)
                    for f in range(4):
                        last = nc.tensor.transpose(banks[:, 4, f * P:(f + 1) * P], ke[:, f * P:(f + 1) * P], ident[:, :])
                    last.then_inc(gates["kt"], 1)
                if l == 3:
                    pe.wait_ge(gates["ktok"], m + 1)
                    if m:
                        pe.wait_ge(gates["state"], m)
                    for f in range(4):
                        last = nc.tensor.matmul(banks[:, 5, f * P:(f + 1) * P], k_tok[:, f * P:(f + 1) * P],
                                                vt[:, s, f * P:(f + 1) * P], start=True, stop=True)
                    last.then_inc(gates["st"], 1)
            pe.wait_ge(gram_read, (m + 1) * (LEVELS + 1))
            pe.wait_ge(gates["qe"], m + 1)
            if m:
                pe.wait_ge(gates["on"], m)
            for f in range(4):
                nc.tensor.matmul(banks[:, 6, f * P:(f + 1) * P], qe[:, f * P:(f + 1) * P], state[:, f, :],
                                 start=True, stop=False, skip_group_check=True)
                for par in range(2):
                    h = 2 * f + par
                    last = nc.tensor.matmul(banks[:, 6, h * HD:(h + 1) * HD], S[:, h, :], vt[:, s, h * HD:(h + 1) * HD],
                                            start=False, stop=(par == 1), skip_group_check=True)
            last.then_inc(gates["out"], 1)
            pe.wait_ge(gates["on"], m + 1)
            if m:
                pe.wait_ge(gates["oT"], m)
            for f in range(4):
                last = nc.tensor.transpose(banks[:, 7, f * P:(f + 1) * P], on[:, f * P:(f + 1) * P], ident[:, :])
            last.then_inc(gates["ot"], 1)


def out_projection(nc, c, sem, sb, banks, x, meta, ins, oT, y, y_dram):
    w = sb(c, "w_out_sb", [P, DC, D])
    loaded_w, done, added, stored = sem("w_out_loaded"), sem("op_psum"), sem("op_added"), sem("op_stored")
    h_loaded = [sem(f"op_h{i}") for i in range(3)]
    block = c.enter_context(nc.Block())

    @block.sync
    def _(sp):
        sp.dma_start(w[:, :, :], ins["w_out"][0].rearrange("(k p) f -> p k f", p=P)).then_inc(loaded_w, 16)
        for m, (t0, n) in enumerate(TILES):
            src = meta if m == 0 else x[t0 - N_META:t0 - N_META + n, :]
            if m >= 3:
                sp.wait_ge(h_loaded[m % 3], 16 * (m // 3))
            sp.dma_start(y[0:n, m, :], src).then_inc(h_loaded[m % 3], 16)
        for m, (t0, n) in enumerate(TILES):
            sp.wait_ge(added, 2 * (m + 1))
            sp.dma_start(y_dram[t0:t0 + n, :], y[0:n, m, :]).then_inc(stored, 16)
        sp.wait_ge(stored, 16 * NT)

    @block.tensor
    def _(pe):
        pe.wait_ge(loaded_w, 16)
        for i in range(2 * NT):
            t0, n = TILES[i // 2]
            if i >= 8:
                pe.wait_ge(added, i - 7)
            for k in range(DC):
                last = nc.tensor.matmul(banks[0:n, i % 8, :], oT[:, k, t0:t0 + n], w[:, k, (i % 2) * 512:(i % 2 + 1) * 512],
                                        start=(k == 0), stop=(k == DC - 1))
            last.then_inc(done, 1)

    @block.vector
    def _(dve):
        for i in range(2 * NT):
            m = i // 2
            n = TILES[m][1]
            dve.wait_ge(h_loaded[m % 3], 16 * (m // 3 + 1))
            dve.wait_ge(done, i + 1)
            at = y[0:n, m, (i % 2) * 512:(i % 2 + 1) * 512]
            nc.vector.scalar_tensor_tensor(out=at, in0=at, scalar=ALPHA, in1=banks[0:n, i % 8, :], op0=ALU.mult,
                                           op1=ALU.add).then_inc(added, 1)


def norm(nc, c, sem, sb, banks, ident, tag, y, tiles, g_row, b_row, load=None, split=None, plain=None, store=None):
    gb = sb(c, f"{tag}_g", [P, D])
    bb = sb(c, f"{tag}_b", [P, D])
    bn6 = sb(c, f"{tag}_bn6", [P, NT, 2, 6])
    mv = sb(c, f"{tag}_mv", [P, NT, 2])
    std = sb(c, f"{tag}_std", [P, NT])
    rstd = sb(c, f"{tag}_rstd", [P, NT])
    shift = sb(c, f"{tag}_shift", [P, NT])
    S = {k: sem(f"{tag}_{k}") for k in ("gb", "bn", "var", "std", "rstd", "shift", "scaled", "gained", "biased", "psum",
                                        "hi", "lo", "stored")}
    loads = [sem(f"{tag}_ld{i}") for i in range(3)]
    block = c.enter_context(nc.Block())
    J = len(tiles)

    @block.sync
    def _(sp):
        sp.dma_start(gb[:, :], g_row.rearrange("(a n) -> a n", a=1).to_broadcast([P, D])).then_inc(S["gb"], 16)
        sp.dma_start(bb[:, :], b_row.rearrange("(a n) -> a n", a=1).to_broadcast([P, D])).then_inc(S["gb"], 16)
        if load is not None:
            for j, m in enumerate(tiles):
                t0, n = TILES[m]
                if j >= 3:
                    sp.wait_ge(loads[j % 3], 16 * (j // 3))
                sp.dma_start(y[0:n, m, :], load[t0:t0 + n, :]).then_inc(loads[j % 3], 16)
        if store is not None:
            for j, m in enumerate(tiles):
                t0, n = TILES[m]
                sp.wait_ge(S["biased"], j + 1)
                sp.dma_start(store[0, t0 - N_META:t0 - N_META + n, :], y[0:n, m, :]).then_inc(S["stored"], 16)
            sp.wait_ge(S["stored"], 16 * J)

    @block.vector
    def _(dve):
        dve.wait_ge(S["gb"], 32)

        def stats(j):
            m = tiles[j]
            n = TILES[m][1]
            if load is not None:
                dve.wait_ge(loads[j % 3], 16 * (j // 3 + 1))
            nc.vector.bn_stats(bn6[0:n, m, 0, :], y[0:n, m, 0:512])
            nc.vector.bn_stats(bn6[0:n, m, 1, :], y[0:n, m, 512:D]).then_inc(S["bn"], 1)
            dve.wait_ge(S["bn"], 2 * j + 1)
            nc.vector.bn_aggr(mv[0:n, m, :], bn6[0:n, m, :, :].rearrange("p a b -> p (a b)")).then_inc(S["bn"], 1)
            dve.wait_ge(S["bn"], 2 * j + 2)
            nc.vector.tensor_scalar(mv[0:n, m, 1:2], mv[0:n, m, 1:2], LN_EPS, None, ALU.add).then_inc(S["var"], 1)

        def factors(j):
            m = tiles[j]
            n = TILES[m][1]
            dve.wait_ge(S["std"], j + 1)
            nc.vector.reciprocal(rstd[0:n, m:m + 1], std[0:n, m:m + 1]).then_inc(S["rstd"], 1)
            dve.wait_ge(S["rstd"], j + 1)
            nc.vector.tensor_scalar(shift[0:n, m:m + 1], mv[0:n, m, 0:1], rstd[0:n, m:m + 1], -1.0, ALU.mult, ALU.mult)\
              .then_inc(S["shift"], 1)

        def gains(j):
            m = tiles[j]
            n = TILES[m][1]
            dve.wait_ge(S["scaled"], j + 1)
            nc.vector.tensor_tensor(y[0:n, m, :], y[0:n, m, :], gb[0:n, :], ALU.mult).then_inc(S["gained"], 1)

        def low(j):
            m = tiles[j]
            t0, n = TILES[m]
            for q in range(2):
                i = 2 * j + q
                dve.wait_ge(S["hi"], i + 1)
                src = banks[:, i % 8, :].rearrange("p (k t) -> p k t", k=4)[:, :, 0:n]
                at = slice(4 * q, 4 * q + 4)
                nc.vector.tensor_tensor(split[1][:, at, t0:t0 + n], src, split[0][:, at, t0:t0 + n].bitcast(F32),
                                        ALU.subtract).then_inc(S["lo"], 1)

        for j in range(J + 3):
            if j < J:
                stats(j)
            if 1 <= j <= J:
                factors(j - 1)
            if 2 <= j <= J + 1:
                gains(j - 2)
            if split and j >= 3:
                low(j - 3)

    @block.gpsimd
    def _(pool):
        for j, m in enumerate(tiles):
            n = TILES[m][1]
            pool.wait_ge(S["gained"], j + 1)
            nc.gpsimd.tensor_tensor(y[0:n, m, :], y[0:n, m, :], bb[0:n, :], ALU.add).then_inc(S["biased"], 1)

    @block.scalar
    def _(act):
        def high(j):
            m = tiles[j]
            t0, n = TILES[m]
            for q in range(2):
                i = 2 * j + q
                act.wait_ge(S["psum"], i + 1)
                src = banks[:, i % 8, :].rearrange("p (k t) -> p k t", k=4)[:, :, 0:n]
                dst = split[0] if split else plain
                nc.scalar.activation(dst[:, 4 * q:4 * q + 4, t0:t0 + n], src, ACT.Copy).then_inc(S["hi"], 1)

        for j in range(J + 3):
            if j < J:
                m = tiles[j]
                n = TILES[m][1]
                act.wait_ge(S["var"], j + 1)
                nc.scalar.activation(std[0:n, m:m + 1], mv[0:n, m, 1:2], ACT.Sqrt).then_inc(S["std"], 1)
            if 1 <= j <= J:
                m = tiles[j - 1]
                n = TILES[m][1]
                act.wait_ge(S["shift"], j)
                nc.scalar.activation(y[0:n, m, :], y[0:n, m, :], ACT.Identity, bias=shift[0:n, m:m + 1],
                                     scale=rstd[0:n, m:m + 1]).then_inc(S["scaled"], 1)
            if store is None and j >= 3:
                high(j - 3)

    if store is None:
        @block.tensor
        def _(pe):
            for j, m in enumerate(tiles):
                n = TILES[m][1]
                pe.wait_ge(S["biased"], j + 1)
                for q in range(2):
                    i = 2 * j + q
                    if i >= 8:
                        pe.wait_ge(S["lo" if split else "hi"], i - 7)
                    for k in range(4):
                        kk = 4 * q + k
                        last = nc.tensor.transpose(banks[:, i % 8, k * P:k * P + n], y[0:n, m, kk * P:(kk + 1) * P],
                                                   ident[0:n, 0:n])
                    last.then_inc(S["psum"], 1)


def ffn(nc, c, sem, sb, banks, tag, y, hH, hL, tiles, chunks, w_gate, w_up, w_down):
    NCH = len(chunks)
    CW = max(n for _, n in chunks)
    NU = 2 * NCH
    NJ = 2 * len(tiles)
    wg = w_gate.rearrange("(k p) f -> p k f", p=P)
    wu = w_up.rearrange("(k p) f -> p k f", p=P)
    wd = w_down.rearrange("(i u p) f -> i p u f", u=2, p=P)
    raw = sb(c, f"{tag}_raw", [P, 2, DC, P])
    wH = sb(c, f"{tag}_wH", [P, 2, 2, DC, P], F32R)
    wL = sb(c, f"{tag}_wL", [P, 2, 2, DC, P], F32R)
    draw = sb(c, f"{tag}_draw", [P, 2, D])
    dH = sb(c, f"{tag}_dH", [P, 2, D], F32R)
    dL = sb(c, f"{tag}_dL", [P, 2, D], F32R)
    hidH = sb(c, f"{tag}_hidH", [P, 2, L], F32R)
    hidL = sb(c, f"{tag}_hidL", [P, 2, L], F32R)
    silu = sb(c, f"{tag}_silu", [P, 2, CW])
    hid = sb(c, f"{tag}_hid", [P, 2, CW])

    s = {k: sem(f"{tag}_{k}") for k in ("alpha", "raw", "w_hi", "w_lo", "draw", "d_hi", "d_lo", "gu_psum",
                                        "silu", "hid", "hid_hi", "hid_lo", "d_psum", "added")}
    FREE = 1
    block = c.enter_context(nc.Block())
    ITERS = FF_TILES // 2

    @block.sync
    def _(sp):
        with sp.Fori(0, ITERS) as i:
            for u in range(2):
                sp.wait_ge(s["w_hi"], FREE + 2 * i + u)
                sp.wait_ge(s["w_lo"], FREE + 2 * i + u)
                for g, w in enumerate((wg, wu)):
                    sp.dma_start(raw[:, g, :, :], w[:, :, bass.ds((2 * i + u) * P, P)]).then_inc(s["raw"], 16)
                if u == 0:
                    sp.wait_ge(s["d_hi"], FREE + i)
                    sp.wait_ge(s["d_lo"], FREE + i)
                    sp.dma_start(draw[:, :, :], wd[bass.ds(i, 1), :, :, :].rearrange("a p u f -> p (a u) f"))\
                      .then_inc(s["draw"], 16)

    @block.gpsimd
    def _(pool):
        pool.sem_inc(s["w_lo"], FREE)
        pool.sem_inc(s["d_lo"], FREE)
        for m in tiles:
            n = TILES[m][1]
            nc.gpsimd.tensor_scalar(y[0:n, m, :], y[0:n, m, :], ALPHA, 1.0, ALU.mult, ALU.mult).then_inc(s["alpha"], 1)
        with pool.Fori(0, ITERS) as i:
            for u in range(2):
                pool.wait_ge(s["w_hi"], FREE + 2 * i + u + 1)
                pool.wait_ge(s["gu_psum"], FREE + NU * i)
                nc.gpsimd.tensor_tensor(wL[:, u, :, :, :].rearrange("p g k f -> p (g k f)"),
                                        raw[:, :, :, :].rearrange("p g k f -> p (g k f)"),
                                        wH[:, u, :, :, :].rearrange("p g k f -> p (g k f)").bitcast(F32),
                                        ALU.subtract).then_inc(s["w_lo"], 1)
            pool.wait_ge(s["d_hi"], FREE + i + 1)
            nc.gpsimd.tensor_tensor(dL[:, :, :].rearrange("p u f -> p (u f)"), draw[:, :, :].rearrange("p u f -> p (u f)"),
                                    dH[:, :, :].rearrange("p u f -> p (u f)").bitcast(F32), ALU.subtract)\
              .then_inc(s["d_lo"], 1)

    @block.scalar
    def _(act):
        act.sem_inc(s["w_hi"], FREE)
        act.sem_inc(s["d_hi"], FREE)
        with act.Fori(0, ITERS) as i:
            act.wait_ge(s["gu_psum"], FREE + NU * i)
            for u in range(2):
                act.wait_ge(s["raw"], 32 * (2 * i + u + 1))
                nc.scalar.activation(wH[:, u, :, :, :], raw[:, :, :, :], ACT.Copy).then_inc(s["w_hi"], 1)
            act.wait_ge(s["draw"], 16 * (i + 1))
            act.wait_ge(s["d_psum"], FREE + NJ * i)
            nc.scalar.activation(dH[:, :, :], draw[:, :, :], ACT.Copy).then_inc(s["d_hi"], 1)

            def gate(q):
                n = chunks[q % NCH][1]
                act.wait_ge(s["gu_psum"], FREE + NU * i + q + 1)
                nc.scalar.activation(silu[:, q % 2, 0:n], banks[:, 2 * (q % 2), 0:n], ACT.Silu).then_inc(s["silu"], 1)

            def high(q):
                a, n = chunks[q % NCH]
                act.wait_ge(s["hid"], FREE + NU * i + q + 1)
                nc.scalar.activation(hidH[:, q // NCH, a:a + n], hid[:, q % 2, 0:n], ACT.Copy).then_inc(s["hid_hi"], 1)

            for q in range(NU):
                gate(q)
                high(q)

    @block.vector
    def _(dve):
        dve.sem_inc(s["hid"], FREE)
        dve.sem_inc(s["added"], FREE)
        with dve.Fori(0, ITERS) as i:
            for q in range(NU):
                a, n = chunks[q % NCH]
                dve.wait_ge(s["silu"], NU * i + q + 1)
                nc.vector.tensor_tensor(hid[:, q % 2, 0:n], silu[:, q % 2, 0:n], banks[:, 2 * (q % 2) + 1, 0:n], ALU.mult)\
                  .then_inc(s["hid"], 1)
                dve.wait_ge(s["hid_hi"], NU * i + q + 1)
                nc.vector.tensor_tensor(hidL[:, q // NCH, a:a + n], hid[:, q % 2, 0:n],
                                        hidH[:, q // NCH, a:a + n].bitcast(F32), ALU.subtract).then_inc(s["hid_lo"], 1)
            dve.wait_ge(s["alpha"], len(tiles))
            dve.wait_ge(s["added"], FREE + NJ * i)
            for j in range(NJ):
                m = tiles[j // 2]
                n = TILES[m][1]
                dve.wait_ge(s["d_psum"], FREE + NJ * i + j + 1)
                at = y[0:n, m, (j % 2) * 512:(j % 2 + 1) * 512]
                nc.vector.tensor_tensor(at, at, banks[0:n, 4 + j % 4, :], ALU.add).then_inc(s["added"], 1)

    @block.tensor
    def _(pe):
        pe.sem_inc(s["gu_psum"], FREE)
        pe.sem_inc(s["d_psum"], FREE)
        with pe.Fori(0, ITERS) as i:
            for q in range(NU):
                u, (a, n) = q // NCH, chunks[q % NCH]
                if q % NCH == 0:
                    pe.wait_ge(s["w_hi"], FREE + 2 * i + u + 1)
                    pe.wait_ge(s["w_lo"], FREE + 2 * i + u + 1)
                if q >= 2:
                    pe.wait_ge(s["hid"], FREE + NU * i + q - 1)
                else:
                    pe.wait_ge(s["hid"], FREE + NU * i)
                for g in range(2):
                    for k in range(DC):
                        for part, (w, h) in enumerate(((wH, hL), (wL, hH), (wH, hH))):
                            last = nc.tensor.matmul(banks[:, 2 * (q % 2) + g, 0:n], w[:, u, g, k, :], h[:, k, a:a + n],
                                                    start=(k == 0 and part == 0), stop=(k == DC - 1 and part == 2))
                last.then_inc(s["gu_psum"], 1)
            pe.wait_ge(s["d_lo"], FREE + i + 1)
            pe.wait_ge(s["hid_lo"], NU * i + NCH)
            for j0 in range(0, NJ, 4):
                for u in range(2):
                    if j0 == 0 and u == 1:
                        pe.wait_ge(s["hid_lo"], NU * (i + 1))
                    for j in range(j0, min(j0 + 4, NJ)):
                        t0, n = TILES[tiles[j // 2]]
                        if u == 0:
                            pe.wait_ge(s["added"], FREE + NJ * i + max(j - 3, 0))
                        for part, (w, h) in enumerate(((dH, hidL), (dL, hidH), (dH, hidH))):
                            last = nc.tensor.matmul(banks[0:n, 4 + j % 4, :], h[:, u, t0:t0 + n],
                                                    w[:, u, (j % 2) * 512:(j % 2 + 1) * 512],
                                                    start=(u == 0 and part == 0), stop=(u == 1 and part == 2))
                        if u == 1:
                            last.then_inc(s["d_psum"], 1)


def pool_mixer(nc, c, sem, sb, banks, ins, y, hT):
    w = sb(c, "w_pool_sb", [P, 4, 2, PG])
    scale = sb(c, "pool_scale_sb", [P, D])
    sa = sb(c, "sum_a", [P, L])
    sb_ = sb(c, "sum_b", [P, L])
    dT = sb(c, "dT", [P, DC, L])
    tmp = sb(c, "pool_tmp", [P, 2, 512])
    loaded, link, diff, psum, scaled, added = (sem("pool_loaded"), sem("pool_link"), sem("pool_diff"), sem("pool_psum"),
                                               sem("pool_scaled"), sem("pool_added"))
    block = c.enter_context(nc.Block())

    @block.sync
    def _(sp):
        sp.dma_start(w[:, :, :, :], ins["w_pool"][0].rearrange("g (k p) f -> p g k f", p=P)).then_inc(loaded, 16)
        sp.dma_start(scale[:, :], ins["pool_scale"].to_broadcast([P, D])).then_inc(loaded, 16)

    @block.vector
    def _(dve):
        chain = [0]

        def linked(ins_):
            chain[0] += 1
            ins_.then_inc(link, 1)
            dve.wait_ge(link, chain[0])

        for k in range(DC):
            g = k // 2
            src = hT[:, k, :]
            for step in range(g + 1):
                sh = 2 ** step
                dst = (sa, sb_)[step % 2]
                lo = 2 * sh - 1
                linked(nc.vector.tensor_tensor(dst[:, lo:L], src[:, lo:L], src[:, lo - sh:L - sh], ALU.add))
                src = dst[:, :]
            nc.vector.scalar_tensor_tensor(out=dT[:, k, N_META:L], in0=src[:, N_META:L], scalar=1.0 / POOL_WINDOWS[g],
                                           in1=hT[:, k, N_META:L], op0=ALU.mult, op1=ALU.subtract).then_inc(diff, 1)
            dve.wait_ge(diff, k + 1)
        dve.wait_ge(loaded, 32)
        for i in range(2 * (NT - 1)):
            m = 1 + i // 2
            cols = slice((i % 2) * 512, (i % 2 + 1) * 512)
            dve.wait_ge(psum, i + 1)
            if i >= 2:
                dve.wait_ge(added, i - 1)
            nc.vector.tensor_tensor(tmp[:, i % 2, :], banks[:, i % 8, :], scale[:, cols], ALU.mult).then_inc(scaled, 1)
            dve.wait_ge(scaled, i + 1)
            nc.vector.scalar_tensor_tensor(out=y[:, m, cols], in0=y[:, m, cols], scalar=ALPHA, in1=tmp[:, i % 2, :],
                                           op0=ALU.mult, op1=ALU.add).then_inc(added, 1)

    @block.tensor
    def _(pe):
        pe.wait_ge(loaded, 32)
        pe.wait_ge(diff, DC)
        for i in range(2 * (NT - 1)):
            t0 = TILES[1 + i // 2][0]
            if i >= 8:
                pe.wait_ge(scaled, i - 7)
            for gg in range(2):
                g = 2 * (i % 2) + gg
                for k in range(2):
                    last = nc.tensor.matmul(banks[:, i % 8, gg * PG:(gg + 1) * PG], dT[:, 2 * g + k, t0:t0 + P],
                                            w[:, g, k, :], start=(k == 0), stop=(k == 1))
            last.then_inc(psum, 1)


def kernel(**inputs):
    import numpy as np
    import concourse.bacc as bacc
    from concourse.bass_utils import run_bass_kernel_spmd

    nc = bacc.Bacc("TRN2", target_bir_lowering=False, num_devices=1)
    arrays, ins = {}, {}
    for name, a in inputs.items():
        arrays[f"in_{name}"] = np.ascontiguousarray(a)
        ins[name] = nc.dram_tensor(f"in_{name}", a.shape, mybir.dt.from_np(arrays[f"in_{name}"].dtype),
                                   kind="ExternalInput").ap()
    out = nc.dram_tensor("out_0", (1, SEQ, D), F32, kind="ExternalOutput").ap()
    build(nc, ins, out)
    r = run_bass_kernel_spmd(nc, [arrays], core_ids=[0])
    return r.results[0]["out_0"]
```

```python
from contextlib import ExitStack, contextmanager

import concourse.bass as bass
from concourse import mybir

F32 = mybir.dt.float32
F32R = mybir.dt.float32r
I32 = mybir.dt.int32
U8 = mybir.dt.uint8
ALU = mybir.AluOpType
ACT = mybir.ActivationFunctionType

P = 128
D = 1024
DC = D // P
SEQ = 1024
N_META = 16
L = SEQ + N_META
A_HEADS = 8
HD = 64
A_WIDTH = A_HEADS * HD
Q_RANK = 256
QC = Q_RANK // P
IDX_HEADS = 16
IDX_WIDTH = IDX_HEADS * HD
TOPK = 256
D_FF = 2816
FF_TILES = D_FF // P
DEPTH = 2
ALPHA = (2 * DEPTH) ** 0.25
LN_EPS = 1e-5
POOL_WINDOWS = (2, 4, 8, 16)
PG = D // len(POOL_WINDOWS)

COL_CQ, COL_KA, COL_VA = 0, Q_RANK, Q_RANK + A_WIDTH
COL_KI = COL_VA + A_WIDTH
COL_WI = COL_KI + HD
COL_QB = COL_WI + IDX_HEADS
COL_ZF, COL_IB, COL_GB = COL_QB + A_WIDTH, COL_QB + 2 * A_WIDTH, COL_QB + 3 * A_WIDTH

TILES = [(0, N_META)] + [(N_META + P * i, P) for i in range(SEQ // P)]
NT = len(TILES)
CHUNKS3 = [(0, 352), (352, 344), (696, 344)]
NKEYS = [t0 + n for t0, n in TILES]
SC_OFF = [sum(NKEYS[:m]) for m in range(NT)]
SC_COLS = sum(NKEYS)
FIRST_TOPK = 2
MASKED = -1.0e30
TAKEN = -3.0e38
TAKEN_BELOW = -2.0e38


def key_chunks(n):
    k = -(-n // 512)
    w = -(-n // k // 8) * 8
    return [(a, min(w, n - a)) for a in range(0, n, w)]


def build(nc, ins, out):
    x, meta, w_in = ins["x"][0], ins["meta_tokens"], ins["w_in"][0]
    w_in_v = w_in.rearrange("(k p) f -> p k f", p=P)

    with ExitStack() as top:
        sems = []

        def sem(name):
            sems.append(nc.alloc_semaphore(name=name))
            return sems[-1]

        @contextmanager
        def stage():
            with ExitStack() as c:
                yield c
            nc.clear_and_free_semaphores(sems)
            nc.all_engine_barrier()
            sems.clear()

        def sb(ctx, name, shape, dt=F32):
            return ctx.enter_context(nc.sbuf_tensor(name, shape, dt))

        qz_dram = nc.dram_tensor("qz_scratch", [2, 4, P, L], F32, kind="Internal").ap()
        vg_dram = nc.dram_tensor("vg_scratch", [2, L, A_WIDTH], F32, kind="Internal").ap()

        banks = top.enter_context(nc.psum_tensor("banks", [P, 8, 512], F32))
        ident = sb(top, "ident", [P, P])

        with ExitStack() as heads:
            with ExitStack() as mixer:
                score = sb(mixer, "score", [P, SC_COLS])
                cqT = sb(mixer, "cqT", [P, QC, L])
                kaT = sb(mixer, "kaT", [P, 4, L])
                va = sb(mixer, "va", [P, NT, A_WIDTH])
                with stage() as c:
                    projection(nc, c, sem, sb, banks, ident, x, meta, w_in_v, ins, score, cqT, kaT, va, qz_dram, vg_dram)
                oT = heads.enter_context(nc.sbuf_tensor("oT", [P, DC, L], F32, side="right"))
                with stage() as c:
                    mixers(nc, c, sem, sb, banks, ident, ins, score, cqT, kaT, va, oT, qz_dram, vg_dram)
            y = sb(top, "y", [P, NT, D])
            hH = sb(top, "hH", [P, DC, L], F32R)
            hL = sb(top, "hL", [P, DC, L], F32R)
            with stage() as c:
                out_projection(nc, c, sem, sb, banks, ident, x, meta, ins, oT, y, hH, hL)
        with stage() as c:
            ffn(nc, c, sem, sb, banks, ident, "f0", y, hH, hL, list(range(NT)), CHUNKS3,
                ins["w_gate"][0], ins["w_up"][0], ins["w_down"][0])
        with stage() as c:
            pool_mixer(nc, c, sem, sb, banks, ident, ins, y, hH, hL)
        with stage() as c:
            ffn(nc, c, sem, sb, banks, ident, "f1", y, hH, hL, list(range(1, NT)), [(N_META, 512), (N_META + 512, 512)],
                ins["w_gate"][1], ins["w_up"][1], ins["w_down"][1], final=(ins["ln_ffn_g"][1], ins["ln_ffn_b"][1], out))


def projection(nc, c, sem, sb, banks, ident, x, meta, w_in_v, ins, score, cqT, kaT, va, qz_dram, vg_dram):
    NX = 3
    IC = Q_RANK + HD + IDX_HEADS
    CK = Q_RANK + 2 * HD
    SW = 256
    xt = va[:, :, :].rearrange("p m f -> p (m f)")[:, 0:NX * D].rearrange("p (s d) -> p s d", s=NX)
    cqk = kaT[:, :, :].rearrange("p f t -> p (f t)")[:, 0:NT * CK].rearrange("p (m f) -> p m f", m=NT)
    w_idx = score[:, SC_OFF[FIRST_TOPK]:SC_OFF[FIRST_TOPK] + DC * IC].rearrange("p (k f) -> p k f", k=DC)
    hH = sb(c, "hH0", [P, DC, L], F32R)
    hL = sb(c, "hL0", [P, DC, L], F32R)
    SLAB = DC * SW
    shared = sb(c, "shared", [P, 3 * SLAB], F32R)
    w_idxH, w_idxL = (shared[:, i * DC * IC:(i + 1) * DC * IC].rearrange("p (k f) -> p k f", k=DC) for i in range(2))
    qiT = shared[:, 0:2 * IDX_HEADS * P].rearrange("p (s h t) -> p s h t", s=2, h=IDX_HEADS)
    with ExitStack() as first:
        w_qi = sb(first, "w_qi", [P, QC, IDX_WIDTH])
    slab0L = sb(c, "slab0L", [P, DC, SW], F32R)
    slab0H, slab1H, slab1L = (shared[:, i * SLAB:(i + 1) * SLAB].rearrange("p (k f) -> p k f", k=DC) for i in (2, 0, 1))
    slabH, slabL = (slab0H, slab1H), (slab0L[:, :, :], slab1L)
    cq_gain = sb(c, "cq_gain_sb", [P, QC])
    ki_gb = sb(c, "ki_gb", [P, 2])
    squares = sb(c, "squares", [P, Q_RANK])
    wi = sb(c, "wi", [P, NT, IDX_HEADS])
    bn6 = sb(c, "bn6", [P, NT, 6])
    var = sb(c, "var", [P, NT, 2])
    sumsq = sb(c, "sumsq", [P, NT, 1])
    std = sb(c, "std_p", [P, NT, 2])
    rstd = sb(c, "rstd_p", [P, NT, 2])
    mv = sb(c, "mv_p", [P, NT, 2])
    kiT = sb(c, "kiT", [P, 2, P])
    kiH = sb(c, "kiH", [P, L], F32R)
    kiL = sb(c, "kiL", [P, L], F32R)
    qi_raw = sb(c, "qi_raw", [P, 2, 4, P])
    NR = 4
    relu = sb(c, "relu", [P, NR, 512])
    top8 = sb(c, "top8", [P, NT, 8])
    mark = sb(c, "round_mark", [P, 2])
    slab = sb(c, "slab", [P, 2, DC, SW])
    NS = NR
    stage = relu

    s_x = [sem(f"x_loaded{i}") for i in range(NX)]
    w_loaded, small_loaded = sem("w_loaded"), sem("small_loaded")
    slab_loaded = [sem("slab_loaded0"), sem("slab_loaded1")]
    ident_zero, ident_done = sem("ident_zero"), sem("ident_done")
    x_transposed, hT_act, hT_dve = sem("x_transposed"), sem("hT_act"), sem("hT_dve")
    idx_psum, idx_act, idx_dve = sem("idx_psum"), sem("idx_act"), sem("idx_dve")
    stats, std_done, normed = sem("stats"), sem("std_done"), sem("normed")
    cq_psum, cqT_done = sem("cq_psum"), sem("cqT_done")
    qi_psum, qi_done = sem("qi_psum"), sem("qi_done")
    ki_raw, qi_lo = sem("ki_raw"), sem("qi_lo")
    sc_psum, relu_done, acc_done = sem("sc_psum"), sem("relu_done"), sem("acc_done")
    causal_done, topk_step, mask_done, mask_all = sem("causal_done"), sem("topk_step"), sem("mask_done"), sem("mask_all")
    slab_psum, slab_out, slab_hi, slab_lo = sem("slab_psum"), sem("slab_out"), sem("slab_hi"), sem("slab_lo")
    idx_hi, idx_lo = sem("w_idx_hi"), sem("w_idx_lo")
    stored = [sem(f"stored{i}") for i in range(NS)]
    link = sem("dve_link")

    SLABS = [(col + SW * half, fm, dest, half) for col, fm, dest in (
        (COL_KA, True, "ka"), (COL_VA, False, "va"), (COL_ZF, True, 1), (COL_QB, True, 0), (COL_IB, False, 0),
        (COL_GB, False, 1)) for half in range(512 // SW)]
    slab_units = []
    for j, (_, fm, dest, half) in enumerate(SLABS):
        if fm:
            slab_units += [(j, fm, dest, ft, a, n) for ft in range(SW // P) for a, n in CHUNKS3]
        else:
            slab_units += [(j, fm, dest, m, *TILES[m]) for m in range(NT)]
    last_unit = {j: max(i for i, u in enumerate(slab_units) if u[0] == j) for j in range(len(SLABS))}

    TM = list(range(FIRST_TOPK, NT))
    EARLY = TM[:-1]
    units, order = [], []
    for i, m in enumerate(TM):
        if i == 0:
            order.append(("qi", m))
        if i + 1 < len(TM):
            order.append(("qi", TM[i + 1]))
        first = len(units)
        units += [(m, 2 * ft + b, a, n) for ft in range(8) for a, n in key_chunks(NKEYS[m]) for b in range(2)]
        order.append(("sc", m, first, len(units)))
    last_of_tile = {m: max(i for i, u in enumerate(units) if u[0] == m) for m in TM}

    def score_bank(n):
        return 2 + 3 * (n % 2) + (n // 2) % 3

    block = c.enter_context(nc.Block())

    @block.sync
    def _(sp):
        for m, (t0, n) in enumerate(TILES):
            if m >= NX:
                sp.wait_ge(x_transposed, m - NX + 1)
            src = meta if m == 0 else x[t0 - N_META:t0 - N_META + n, :]
            sp.dma_start(xt[0:n, m % NX, :], src).then_inc(s_x[m % NX], 16)
            if m == 2:
                sp.dma_start(w_idx[:, :, 0:Q_RANK], w_in_v[:, :, 0:Q_RANK]).then_inc(w_loaded, 16)
                sp.dma_start(w_idx[:, :, Q_RANK:IC], w_in_v[:, :, COL_KI:COL_QB]).then_inc(w_loaded, 16)
        sp.dma_start(w_qi[:, :, :], ins["w_uq_idx"][0].rearrange("(k p) f -> p k f", p=P)).then_inc(w_loaded, 16)
        for k in range(QC):
            sp.dma_start(cq_gain[:, k:k + 1], ins["cq_gain"][0, k * P:(k + 1) * P].rearrange("(p a) -> p a", a=1))\
              .then_inc(small_loaded, 16)
        for b in range(2):
            for i, name in enumerate(("kidx_gain", "kidx_bias")):
                sp.dma_start(ki_gb[HD * b:HD * (b + 1), i:i + 1], ins[name][0].rearrange("(p a) -> p a", a=1))\
                  .then_inc(small_loaded, 16)
        for j, (col, _, _, _) in enumerate(SLABS):
            if j >= 2:
                sp.wait_ge(slab_hi, j - 1)
                sp.wait_ge(slab_lo, j - 1)
            sp.dma_start(slab[:, j % 2, :, :], w_in_v[:, :, col:col + SW]).then_inc(slab_loaded[j % 2], 16)

    @block.gpsimd
    def _(pool):
        nc.gpsimd.memset(ident[:, :], 0.0).then_inc(ident_zero, 1)
        pool.wait_ge(ident_zero, 1)
        nc.gpsimd.affine_select(out=ident[:, :], in_=ident[:, :], compare_op=ALU.not_equal, fill=1.0, base=0,
                                pattern=[[-1, P]], channel_multiplier=1).then_inc(ident_done, 1)
        nc.gpsimd.memset(score[:, 0:SC_OFF[FIRST_TOPK]], 0.0).then_inc(ident_zero, 1)
        pool.wait_ge(ident_zero, 2)

        def causal(m, signal):
            n = TILES[m][1]
            at = score[0:n, SC_OFF[m] + NKEYS[m] - n:SC_OFF[m] + NKEYS[m]]
            nc.gpsimd.affine_select(out=at, in_=at, compare_op=ALU.is_ge, fill=MASKED, base=0, pattern=[[-1, n]],
                                    channel_multiplier=1).then_inc(signal, 1)

        for m in range(FIRST_TOPK):
            causal(m, mask_all)
        pool.wait_ge(idx_hi, 1)
        nc.gpsimd.tensor_tensor(w_idxL, w_idx, w_idxH.bitcast(F32), ALU.subtract).then_inc(idx_lo, 1)
        pool.wait_ge(idx_lo, 1)
        pool.wait_ge(mask_all, FIRST_TOPK)
        nqi = 0
        for what in order:
            if what[0] == "qi":
                pool.wait_ge(qi_done, nqi + 1)
                raw = qi_raw[:, :, :, :].rearrange("p b f t -> p (b f) t")
                hi = qiT[:, what[1] % 2, :, :].rearrange("p (f two) t -> p two f t", two=2)
                for b in range(2):
                    r, other = slice(HD * b, HD * (b + 1)), slice(HD * (1 - b), HD * (2 - b))
                    nc.gpsimd.tensor_tensor(hi[other, b], raw[r], hi[r, b].bitcast(F32), ALU.subtract).then_inc(qi_lo, 1)
                    pool.wait_ge(qi_lo, 2 * nqi + b + 1)
                nqi += 1
            else:
                pool.wait_ge(acc_done, last_of_tile[what[1]] + 1)
                causal(what[1], causal_done)
                pool.wait_ge(causal_done, TM.index(what[1]) + 1)
        for j in range(len(SLABS)):
            pool.wait_ge(slab_hi, j + 1)
            if j >= 2:
                pool.wait_ge(slab_psum, last_unit[j - 2] + 1)
            nc.gpsimd.tensor_tensor(slabL[j % 2], slab[:, j % 2, :, :], slabH[j % 2].bitcast(F32), ALU.subtract)\
              .then_inc(slab_lo, 1)
        for i, m in enumerate(EARLY):
            pool.wait_ge(mask_done, i + 1)
            causal(m, mask_all)
        pool.wait_ge(mask_all, FIRST_TOPK + len(EARLY))
        pool.wait_ge(causal_done, len(TM))

    @block.tensor
    def _(pe):
        pe.wait_ge(ident_done, 1)
        for m, (t0, n) in enumerate(TILES):
            pe.wait_ge(s_x[m % NX], 16 * (m // NX + 1))
            if m >= 2:
                pe.wait_ge(hT_act, m - 1)
                pe.wait_ge(hT_dve, m - 1)
            for k in range(DC):
                bank = 2 * (m % 2) + k // 4
                last = nc.tensor.transpose(banks[:, bank, (k % 4) * P:(k % 4) * P + n], xt[0:n, m % NX, k * P:(k + 1) * P],
                                           ident[0:n, 0:n])
            last.then_inc(x_transposed, 1)
        pe.wait_ge(idx_lo, 1)
        for m, (t0, n) in enumerate(TILES):
            pe.wait_ge(hT_act, m + 1)
            pe.wait_ge(hT_dve, m + 1)
            if m >= 2:
                pe.wait_ge(idx_dve, m - 1)
            for k in range(DC):
                for part, (h, w) in enumerate(((hL, w_idxH), (hH, w_idxL), (hH, w_idxH))):
                    last = nc.tensor.matmul(banks[0:n, 4 + m % 2, 0:IC], h[:, k, t0:t0 + n], w[:, k, :],
                                            start=(k == 0 and part == 0), stop=(k == DC - 1 and part == 2))
            last.then_inc(idx_psum, 1)
        for m, (t0, n) in enumerate(TILES):
            pe.wait_ge(normed, m + 1)
            if m >= 2:
                pe.wait_ge(cqT_done, m - 1)
            for j in range(3):
                last = nc.tensor.transpose(banks[:, 6 + m % 2, j * P:j * P + n], cqk[0:n, m, j * P:(j + 1) * P],
                                           ident[0:n, 0:n])
            last.then_inc(cq_psum, 1)
        pe.wait_ge(cqT_done, NT)
        pe.wait_ge(w_loaded, 48)
        nqi = 0
        for what in order:
            if what[0] == "qi":
                t0, n = TILES[what[1]]
                if nqi:
                    pe.wait_ge(qi_done, nqi)
                for ft in range(8):
                    for k in range(QC):
                        last = nc.tensor.matmul(banks[:, ft // 4, (ft % 4) * P:(ft % 4 + 1) * P],
                                                w_qi[:, k, ft * P:(ft + 1) * P], cqT[:, k, t0:t0 + n],
                                                start=(k == 0), stop=(k == QC - 1))
                last.then_inc(qi_psum, 1)
                nqi += 1
            else:
                _, m, a, b = what
                pe.wait_ge(qi_lo, 2 * TM.index(m) + 2)
                for i in range(a, b):
                    _, h, k0, kn = units[i]
                    if i >= 6:
                        pe.wait_ge(relu_done, i - 5)
                    nc.tensor.matmul(banks[:, score_bank(i), 0:kn], qiT[:, m % 2, h, :], kiL[:, k0:k0 + kn],
                                     start=True, stop=False)
                    nc.tensor.matmul(banks[:, score_bank(i), 0:kn], qiT[:, m % 2, h, :], kiH[:, k0:k0 + kn],
                                     start=False, stop=True).then_inc(sc_psum, 1)
        pe.wait_ge(relu_done, len(units))
        for i, (j, fm, dest, idx, a, n) in enumerate(slab_units):
            pe.wait_ge(slab_lo, j + 1)
            if i >= 8:
                pe.wait_ge(slab_out, i - 7)
            H, Lo = slabH[j % 2], slabL[j % 2]
            for k in range(DC):
                for part, (h, w) in enumerate(((hL, H), (hH, Lo), (hH, H))):
                    first, stop = k == 0 and part == 0, k == DC - 1 and part == 2
                    if fm:
                        last = nc.tensor.matmul(banks[:, i % 8, 0:n], w[:, k, idx * P:(idx + 1) * P], h[:, k, a:a + n],
                                                start=first, stop=stop)
                    else:
                        last = nc.tensor.matmul(banks[0:n, i % 8, 0:SW], h[:, k, a:a + n], w[:, k, :],
                                                start=first, stop=stop)
            last.then_inc(slab_psum, 1)

    @block.scalar
    def _(act):
        for m, (t0, n) in enumerate(TILES):
            act.wait_ge(x_transposed, m + 1)
            for half in range(2):
                src = banks[:, 2 * (m % 2) + half, :].rearrange("p (k t) -> p k t", k=4)[:, :, 0:n]
                last = nc.scalar.activation(hH[:, 4 * half:4 * half + 4, t0:t0 + n], src, ACT.Copy)
            last.then_inc(hT_act, 1)
            if m == 3:
                act.wait_ge(w_loaded, 32)
                nc.scalar.activation(w_idxH, w_idx, ACT.Copy).then_inc(idx_hi, 1)
        act.wait_ge(link, 1)
        for m, (t0, n) in enumerate(TILES):
            act.wait_ge(idx_dve, m + 1)
            if m:
                act.wait_ge(idx_act, m)
            nc.scalar.activation(squares[0:n, :], cqk[0:n, m, 0:Q_RANK], ACT.Square,
                                 accum_out=sumsq[0:n, m, :]).then_inc(idx_act, 1)
        act.wait_ge(stats, 1)
        nc.scalar.activation(std[:, :, :], var[:, :, :], ACT.Sqrt).then_inc(std_done, 1)
        nqi = 0
        for what in order:
            if what[0] == "qi":
                act.wait_ge(qi_psum, nqi + 1)
                src = banks[:, 0:2, :].rearrange("p b t -> p (b t)").rearrange("p (f t) -> p f t", f=8)
                hi = qiT[:, what[1] % 2, :, :].rearrange("p (f two) t -> p two f t", two=2)
                if nqi:
                    act.wait_ge(qi_lo, 2 * nqi)
                for b in range(2):
                    r = slice(HD * b, HD * (b + 1))
                    nc.scalar.activation(hi[r, b], src[r], ACT.Copy)
                nc.scalar.activation(qi_raw[:, :, :, :].rearrange("p b f t -> p (b f) t"), src, ACT.Copy)\
                  .then_inc(qi_done, 1)
                nqi += 1
            else:
                for i in range(what[2], what[3]):
                    kn = units[i][3]
                    act.wait_ge(sc_psum, i + 1)
                    if i >= NR:
                        act.wait_ge(acc_done, i - NR + 1)
                    nc.scalar.activation(relu[:, i % NR, 0:kn], banks[:, score_bank(i), 0:kn], ACT.Relu)\
                      .then_inc(relu_done, 1)
        def split(j):
            act.wait_ge(slab_loaded[j % 2], 16 * (j // 2 + 1))
            if j >= 2:
                act.wait_ge(slab_psum, last_unit[j - 2] + 1)
            nc.scalar.activation(slabH[j % 2], slab[:, j % 2, :, :], ACT.Copy).then_inc(slab_hi, 1)

        act.wait_ge(sc_psum, len(units))
        act.wait_ge(acc_done, len(units))
        split(0)
        split(1)
        staged = 0
        for i, (j, fm, dest, idx, a, n) in enumerate(slab_units):
            half = SLABS[j][3]
            act.wait_ge(slab_psum, i + 1)
            if dest == "ka":
                nc.scalar.activation(kaT[:, half * SW // P + idx, a:a + n], banks[:, i % 8, 0:n], ACT.Copy)\
                  .then_inc(slab_out, 1)
            elif dest == "va":
                nc.scalar.activation(va[0:n, idx, half * SW:(half + 1) * SW], banks[0:n, i % 8, 0:SW], ACT.Copy)\
                  .then_inc(slab_out, 1)
            else:
                s = staged % NS
                if staged >= NS:
                    act.wait_ge(stored[s], 16 * (staged // NS))
                if fm:
                    src, dst, to = (banks[:, i % 8, 0:n], stage[:, s, 0:n],
                                    qz_dram[dest, half * SW // P + idx, :, a:a + n])
                else:
                    src, dst, to = (banks[0:n, i % 8, 0:SW], stage[0:n, s, 0:SW],
                                    vg_dram[dest, a:a + n, half * SW:(half + 1) * SW])
                nc.scalar.activation(dst, src, ACT.Silu if (not fm and dest == 1) else ACT.Copy).then_inc(slab_out, 1)
                act.wait_ge(slab_out, i + 1)
                act.dma_start(to, dst).then_inc(stored[s], 16)
                staged += 1
            if i == last_unit[j] and j + 2 < len(SLABS):
                split(j + 2)
        for s in range(NS):
            act.wait_ge(stored[s], 16 * ((staged - s + NS - 1) // NS))

    @block.vector
    def _(dve):
        chain = [0]

        def linked(ins_):
            chain[0] += 1
            ins_.then_inc(link, 1)
            dve.wait_ge(link, chain[0])

        linked(nc.vector.memset(sumsq[:, :, :], 1.0))
        linked(nc.vector.memset(var[:, :, :], 1.0))
        linked(nc.vector.memset(mv[:, :, :], 1.0))
        for m, (t0, n) in enumerate(TILES):
            dve.wait_ge(x_transposed, m + 1)
            dve.wait_ge(hT_act, m + 1)
            for half in range(2):
                src = banks[:, 2 * (m % 2) + half, :].rearrange("p (k t) -> p k t", k=4)[:, :, 0:n]
                at = slice(4 * half, 4 * half + 4)
                last = nc.vector.tensor_tensor(hL[:, at, t0:t0 + n], src, hH[:, at, t0:t0 + n].bitcast(F32), ALU.subtract)
            last.then_inc(hT_dve, 1)
        for m, (t0, n) in enumerate(TILES):
            dve.wait_ge(idx_psum, m + 1)
            bank = banks[0:n, 4 + m % 2, :]
            nc.vector.tensor_copy(cqk[0:n, m, 0:Q_RANK + HD], bank[:, 0:Q_RANK + HD])
            nc.vector.bn_stats(bn6[0:n, m, :], bank[:, Q_RANK:Q_RANK + HD])
            nc.vector.tensor_scalar(wi[0:n, m, :], bank[:, Q_RANK + HD:IC], IDX_HEADS ** -0.5 * HD ** -0.5, None,
                                    ALU.mult).then_inc(idx_dve, 1)
        dve.wait_ge(idx_dve, NT)
        for m, (t0, n) in enumerate(TILES):
            last = nc.vector.bn_aggr(mv[0:n, m, :], bn6[0:n, m, :])
        linked(last)
        dve.wait_ge(idx_act, NT)
        linked(nc.vector.tensor_scalar(var[:, :, 0:1], sumsq[:, :, :], 1.0 / Q_RANK, LN_EPS, ALU.mult, ALU.add))
        nc.vector.tensor_scalar(var[:, :, 1:2], mv[:, :, 1:2], LN_EPS, None, ALU.add).then_inc(stats, 1)
        dve.wait_ge(std_done, 1)
        linked(nc.vector.reciprocal(rstd[:, :, :], std[:, :, :]))
        dve.wait_ge(idx_dve, NT)
        for m, (t0, n) in enumerate(TILES):
            k0 = Q_RANK
            nc.vector.tensor_scalar(cqk[0:n, m, k0 + HD:k0 + 2 * HD], cqk[0:n, m, k0:k0 + HD], mv[0:n, m, 0:1],
                                    rstd[0:n, m, 1:2], ALU.subtract, ALU.mult)
            linked(nc.vector.tensor_scalar(cqk[0:n, m, 0:k0], cqk[0:n, m, 0:k0], rstd[0:n, m, 0:1], None, ALU.mult))
            nc.vector.tensor_scalar(cqk[0:n, m, k0:k0 + HD], cqk[0:n, m, k0:k0 + HD], mv[0:n, m, 0:1],
                                    rstd[0:n, m, 1:2], ALU.subtract, ALU.mult).then_inc(normed, 1)
        dve.wait_ge(small_loaded, 16 * (QC + 4))
        for m, (t0, n) in enumerate(TILES):
            dve.wait_ge(cq_psum, m + 1)
            bank = banks[:, 6 + m % 2, :]
            for k in range(QC):
                nc.vector.tensor_scalar(cqT[:, k, t0:t0 + n], bank[:, k * P:k * P + n], cq_gain[:, k:k + 1], None,
                                        ALU.mult)
            raw = kiT[:, m % 2, 0:n]
            nc.vector.tensor_scalar(raw, bank[:, QC * P:QC * P + n], ki_gb[:, 0:1], ki_gb[:, 1:2],
                                    ALU.mult, ALU.add).then_inc(ki_raw, 1)
            dve.wait_ge(ki_raw, 2 * m + 1)
            nc.vector.tensor_copy(kiH[:, t0:t0 + n], raw).then_inc(ki_raw, 1)
            dve.wait_ge(ki_raw, 2 * m + 2)
            nc.vector.tensor_tensor(kiL[:, t0:t0 + n], raw, kiH[:, t0:t0 + n].bitcast(F32), ALU.subtract)\
              .then_inc(cqT_done, 1)
        for i, (m, h, a, n) in enumerate(units):
            dve.wait_ge(relu_done, i + 1)
            at = score[:, SC_OFF[m] + a:SC_OFF[m] + a + n]
            if h == 0:
                nc.vector.tensor_scalar(at, relu[:, i % NR, 0:n], wi[:, m, h:h + 1], None, ALU.mult)\
                  .then_inc(acc_done, 1)
            else:
                dve.wait_ge(acc_done, i)
                nc.vector.scalar_tensor_tensor(out=at, in0=relu[:, i % NR, 0:n], scalar=wi[:, m, h:h + 1], in1=at,
                                               op0=ALU.mult, op1=ALU.add).then_inc(acc_done, 1)
        NM = len(EARLY)
        FREE = 1
        dve.wait_ge(causal_done, NM)
        dve.sem_inc(topk_step, FREE)
        with dve.Fori(0, TOPK // 8) as r:
            for i, m in enumerate(EARLY):
                at = score[:, SC_OFF[m]:SC_OFF[m] + NKEYS[m]]
                if i == 0:
                    dve.wait_ge(topk_step, FREE + r * (2 * NM))
                    nc.vector.memset(mark[:, 0:1], 0.0)
                nc.vector.max(top8[:, m, :], at).then_inc(topk_step, 1)
            for i, m in enumerate(EARLY):
                at = score[:, SC_OFF[m]:SC_OFF[m] + NKEYS[m]]
                if i == 0:
                    dve.wait_ge(topk_step, FREE + r * (2 * NM) + NM)
                    nc.vector.memset(mark[:, 1:2], 0.0)
                nc.vector.match_replace(at, top8[:, m, :], at, TAKEN).then_inc(topk_step, 1)
        dve.wait_ge(topk_step, FREE + TOPK // 8 * 2 * NM)
        for m in EARLY:
            at = score[:, SC_OFF[m]:SC_OFF[m] + NKEYS[m]]
            nc.vector.tensor_scalar(at, at, TAKEN_BELOW, MASKED, ALU.is_ge, ALU.mult).then_inc(mask_done, 1)


def mixers(nc, c, sem, sb, banks, ident, ins, score, cqT, kaT, va, oT, qz_dram, vg_dram):
    W = 4 * P
    PAD_Z = 80.0
    LEVELS = 7
    STEPS = LEVELS + 1
    LOG0, T_LO, T_HI, PV, SHARED, GRAM = 0, 2, 3, 4, 5, 6
    PER_BANK = 4

    w_qa = sb(c, "w_qa", [P, QC, A_WIDTH])
    qaT = sb(c, "qaT", [P, 2, A_HEADS, P])
    probs = sb(c, "probs", [P, 2, L])
    pT = sb(c, "pT", [P, 2, NT, P])
    nmax = sb(c, "nmax", [P, 2, 3])
    sums = sb(c, "sums", [P, 2, A_HEADS])
    rsums = sb(c, "rsums", [P, 2, A_HEADS])
    o_tok = sb(c, "o_tok", [P, 2, A_WIDTH])
    REL0 = TILES[-1][0]
    rel_f, rel_i = probs[0:2, 0, :], probs[0:2, 1, :].bitcast(I32)
    rel = sb(c, "rel", [2, L], F32R)
    qpos_i = sb(c, "qpos_i", [2, P], I32)
    qpos = sb(c, "qpos", [2, P])
    alibi = sb(c, "alibi", [2, A_HEADS, P], F32R)
    zt = sb(c, "zt", [P, 2, W])
    qt = sb(c, "qt", [P, 2, W])
    vt = sb(c, "vt", [P, 2, A_WIDTH])
    gt = sb(c, "gt", [P, 2, A_WIDTH])
    u = sb(c, "u", [P, W])
    lnw = sb(c, "lnw", [P, W])
    key_arg = sb(c, "key_arg", [P, W])
    key = sb(c, "key", [P, 2, W])
    b = sb(c, "b", [P, 2, W])
    keep = sb(c, "keep", [P, W])
    ex = sb(c, "ex", [P, 2, W])
    xl = sb(c, "xl", [P, 2, W])
    xq = sb(c, "xq", [P, 2, W])
    eb = sb(c, "eb", [P, W])
    qe = sb(c, "qe", [P, 2, W])
    kd = sb(c, "kd", [P, W])
    elast = sb(c, "elast", [P, 2, 4])
    k_tok = eb
    added = sb(c, "state_added", [P, W])
    S = sb(c, "S", [P, 2, 8, P])
    state = sb(c, "state", [P, 4, P])
    it_s, it_t, xor, shifted, after = (xl[:, 0:2, :].rearrange("p a t -> p (a t)")[:, i * P:(i + 1) * P].bitcast(I32)
                                       for i in range(5))
    masks = sb(c, "masks", [P, STEPS, P], U8)
    gain = sb(c, "gain", [P, A_WIDTH])
    sq = key_arg
    on = sb(c, "on", [P, A_WIDTH])
    ssum = sb(c, "ssum", [P, 8])
    top8 = sb(c, "late_top8", [P, 8])
    rsh = sb(c, "rsh", [P, 8])

    w_loaded, iotas, rel_done, alibi_done = sem("wqa_loaded"), sem("iotas"), sem("rel_done"), sem("alibi_done")
    qk_done, qk_tail, nmax_raw, nmax_tail, nmax_done = (sem("qk_done"), sem("qk_tail"), sem("nmax_raw"),
                                                        sem("nmax_tail"), sem("nmax_done"))
    exp_done, t_psum, t_last, t_act, t_act_last, t_dve, pv_done = (sem("exp_done"), sem("t_psum"), sem("t_last"),
                                                                   sem("t_act"), sem("t_act_last"), sem("t_dve"), sem("pv_done"))
    rs_done, otok_done = sem("rs_done"), sem("otok_done")
    zq_loaded, vg_loaded = [sem("zq_loaded0"), sem("zq_loaded1")], [sem("vg_loaded0"), sem("vg_loaded1")]
    gain_loaded, pads, iota_done, gated = sem("gain_loaded"), sem("pads"), sem("iota_done"), sem("gated")
    vlink = sem("vector_link")
    abs_done, u_done, ln_done, key_in = sem("abs_done"), sem("u_done"), sem("ln_done"), sem("key_in")
    logf_done, b_done, key_done, kd_in, kd_done, eb_done, ke_done = (
        sem("logf_done"), sem("b_done"), sem("key_done"), sem("kd_in"), sem("kd_done"), sem("eb_done"),
        sem("ke_done"))
    ex_in, ex_out, x_done, gram_psum, gram_read = (sem("ex_in"), sem("ex_out"), sem("x_done"), sem("gram_psum"),
                                                   sem("gram_read"))
    state_done, sq_done, ssum_done, lnv_done, rsh_done, on_done = (
        sem("state_done"), sem("sq_done"), sem("ssum_done"), sem("lnv_done"), sem("rsh_done"), sem("on_done"))
    shared_psum, shared_done = sem("shared_psum"), sem("shared_done")
    x_part = sem("x_part")
    taken, late_mask, late_causal = sem("taken"), sem("late_mask"), sem("late_causal")

    units = [(m, h) for m in range(NT) for h in range(A_HEADS)]
    NU = len(units)
    steps = units + [(NT, h) for h in range(STEPS)]
    logits = banks[:, LOG0:LOG0 + 2, :].rearrange("p b t -> p (b t)")
    assert STEPS == A_HEADS and NKEYS[-2] <= 1024 < NKEYS[-1] and NT == 2 * PER_BANK + 1

    def shared_job(m, h):
        jobs = {1: ("out", m - 1), 2: ("kT", m), 3: ("state", m), 4: ("qa", m + 1), 5: ("ot_rec", m - 1),
                6: ("ot_att", m - 1)}
        return jobs[h] if h in jobs and 0 <= jobs[h][1] < NT else None

    shared = [("qa", 0)] + [j for j in (shared_job(*s) for s in steps) if j]
    nth = {j: i + 1 for i, j in enumerate(shared)}

    late = score[:, SC_OFF[NT - 1]:SC_OFF[NT - 1] + NKEYS[NT - 1]]
    ROUNDS = TOPK // 8
    LATE0, LATE1 = 1, NU - A_HEADS - 3
    late_rounds = {i: [r for r in range(ROUNDS) if LATE0 + r * (LATE1 - LATE0) // ROUNDS == i] for i in range(NU)}

    def levels_to(m, h):
        return m * LEVELS + h

    def dve_turns(i):
        return sum(m >= PER_BANK for m, _ in units[:i + 1])

    def tails(i):
        return sum(m == NT - 1 for m, _ in units[:i + 1])

    def halves(ap, l):
        return ap.rearrange("p (n two h) -> p n two h", two=2, h=2 ** l)

    def four(ap):
        return ap.rearrange("p (f t) -> p f t", f=4)

    block = c.enter_context(nc.Block())

    @block.sync
    def _(sp):
        sp.dma_start(w_qa[:, :, :], ins["w_uq"][0].rearrange("(k p) f -> p k f", p=P)).then_inc(w_loaded, 16)
        sp.dma_start(gain[:, :], ins["onorm_gain"][0:1, :].to_broadcast([P, A_WIDTH])).then_inc(gain_loaded, 16)
        sp.wait_ge(pads, 4)
        for m, (t0, n) in enumerate(TILES):
            s = m % 2
            r = slice(P - n, P)
            if m >= 2:
                sp.wait_ge(ke_done, m - 1)
                sp.wait_ge(x_done, levels_to(m - 2, LEVELS))
                sp.wait_ge(gram_psum, STEPS * (m - 2) + 1)
            for w, dst in ((1, zt), (0, qt)):
                sp.dma_start(four(dst[:, s, :])[:, :, r], qz_dram[w, :, :, t0:t0 + n].rearrange("f p t -> p f t"))\
                  .then_inc(zq_loaded[s], 16)
            if m >= 2:
                sp.wait_ge(shared_psum, nth["out", m - 2])
                sp.wait_ge(on_done, m - 1)
            for w, dst in ((0, vt), (1, gt)):
                sp.dma_start(dst[r, s, :], vg_dram[w, t0:t0 + n, :]).then_inc(vg_loaded[s], 16)

    @block.gpsimd
    def _(pool):
        nc.gpsimd.memset(zt[:, 0, :], PAD_Z).then_inc(pads, 1)
        for dst in (qt, vt, gt):
            nc.gpsimd.memset(dst[:, 0, :], 0.0).then_inc(pads, 1)
        nc.gpsimd.memset(xq[:, :, :], 0.0).then_inc(pads, 1)
        nc.gpsimd.memset(qaT[:, :, :, :], 0.0).then_inc(pads, 1)
        nc.gpsimd.iota(it_s, pattern=[[0, P]], base=0, channel_multiplier=1).then_inc(iota_done, 1)
        nc.gpsimd.iota(it_t, pattern=[[1, P]], base=0, channel_multiplier=0).then_inc(iota_done, 1)
        nc.gpsimd.iota(rel_i, pattern=[[1, L]], base=-REL0, channel_multiplier=0).then_inc(iotas, 1)
        nc.gpsimd.iota(qpos_i[:, :], pattern=[[-1, P]], base=0, channel_multiplier=0).then_inc(iotas, 1)
        pool.wait_ge(iotas, 2)
        nc.gpsimd.tensor_copy(rel_f, rel_i).then_inc(iotas, 1)
        nc.gpsimd.tensor_copy(qpos[:, :], qpos_i[:, :]).then_inc(iotas, 1)
        pool.wait_ge(iotas, 4)
        nc.gpsimd.affine_select(out=rel_f, in_=rel_f, compare_op=ALU.is_ge, fill=1.0, base=0,
                                pattern=[[0, L]], channel_multiplier=-1).then_inc(rel_done, 1)
        nc.gpsimd.affine_select(out=qpos[:, :], in_=qpos[:, :], compare_op=ALU.is_gt, fill=1.0, base=0,
                                pattern=[[0, P]], channel_multiplier=1).then_inc(rel_done, 1)
        pool.wait_ge(gain_loaded, 16)
        pool.wait_ge(pads, 6)

        def decayed(m, h):
            l, i = h - 1, levels_to(m, h) - 1
            pool.wait_ge(key_done, m + 1)
            pool.wait_ge(ex_out, i + 1)
            if i >= 2:
                pool.wait_ge(gram_psum, (i - 2) // LEVELS * STEPS + (i - 2) % LEVELS + 2)
            e, xo = halves(ex[:, i % 2, :], l), halves(xl[:, i % 2, :], l)
            nc.gpsimd.tensor_tensor(xo[:, :, 0, :], e[:, :, 0, :], halves(key[:, m % 2, :], l)[:, :, 0, :], ALU.mult)\
              .then_inc(x_part, 1)
            for par in range(2):
                r = slice(HD * par, HD * (par + 1))
                later = [a[r].rearrange("p (f n two t) -> p f n two t", f=4, two=2, t=2 ** l)[:, :, :, 1, :]
                         for a in (ex[:, i % 2, :], qt[:, m % 2, :])]
                to = xq[r, i % 2, :].rearrange("p (f two n t) -> p two f n t", f=4, two=2, t=2 ** l)[:, par]
                pool.wait_ge(x_part, 2 * i + par + 1)
                nc.gpsimd.tensor_tensor(to, later[0], later[1], ALU.mult).then_inc(x_done if par else x_part, 1)
            pool.wait_ge(x_done, i + 1)

        pool.wait_ge(zq_loaded[0], 32)
        decayed(0, 1)
        for i, (m, h) in enumerate(steps):
            if i + 2 < NU and steps[i + 2][1]:
                decayed(*steps[i + 2])
            if h == 0 and m < NT:
                pool.wait_ge(vg_loaded[m % 2], 32 * (m // 2 + 1))
                nc.gpsimd.tensor_tensor(gt[:, m % 2, :], gt[:, m % 2, :], gain[:, :], ALU.mult).then_inc(gated, 1)
            if i == LATE1 + 1:
                pool.wait_ge(late_mask, 1)
                nc.gpsimd.affine_select(out=late[:, NKEYS[-1] - P:NKEYS[-1]], in_=late[:, NKEYS[-1] - P:NKEYS[-1]],
                                        compare_op=ALU.is_ge, fill=MASKED, base=0, pattern=[[-1, P]],
                                        channel_multiplier=1).then_inc(late_causal, 1)
            if h == 2 and m:
                pool.wait_ge(shared_done, nth["out", m - 1])
                if m >= 2:
                    pool.wait_ge(ssum_done, 2 * (m - 1))
                pool.wait_ge(key_done, min(m + 1, NT))
                nc.gpsimd.tensor_tensor(sq[:, :], on[:, :], on[:, :], ALU.mult).then_inc(sq_done, 1)

    @block.tensor
    def _(pe):
        pe.wait_ge(w_loaded, 16)
        pe.wait_ge(alibi_done, 1)

        def on_shared(what, m):
            n_use = nth[what, m]
            if n_use > 1:
                pe.wait_ge(shared_done, n_use - 1)
            s = m % 2
            t0, n = TILES[m]
            if what == "qa":
                for ft in range(4):
                    for k in range(QC):
                        last = nc.tensor.matmul(banks[:, SHARED, ft * P:ft * P + n], w_qa[:, k, ft * P:(ft + 1) * P],
                                                cqT[:, k, t0:t0 + n], start=(k == 0), stop=(k == QC - 1))
            if what == "kT":
                pe.wait_ge(ke_done, m + 1)
                for f in range(4):
                    last = nc.tensor.transpose(banks[:, SHARED, f * P:(f + 1) * P], kd[:, f * P:(f + 1) * P], ident[:, :])
            if what == "state":
                pe.wait_ge(vg_loaded[s], 32 * (m // 2 + 1))
                for f in range(4):
                    last = nc.tensor.matmul(banks[:, SHARED, f * P:(f + 1) * P], k_tok[:, f * P:(f + 1) * P],
                                            vt[:, s, f * P:(f + 1) * P], start=True, stop=True)
            if what == "out":
                pe.wait_ge(gram_read, STEPS * (m + 1))
                if m:
                    pe.wait_ge(state_done, m)
                for f in range(4):
                    nc.tensor.matmul(banks[:, SHARED, f * P:(f + 1) * P], qe[:, s, f * P:(f + 1) * P], state[:, f, :],
                                     start=True, stop=False, skip_group_check=True)
                    for par in range(2):
                        h = 2 * f + par
                        last = nc.tensor.matmul(banks[:, SHARED, h * HD:(h + 1) * HD], S[:, s, h, :],
                                                vt[:, s, h * HD:(h + 1) * HD], start=False, stop=(par == 1),
                                                skip_group_check=True)
            if what == "ot_rec":
                pe.wait_ge(on_done, m + 1)
                for f in range(4):
                    last = nc.tensor.transpose(banks[:, SHARED, f * P:(f + 1) * P], on[:, f * P:(f + 1) * P], ident[:, :])
            if what == "ot_att":
                pe.wait_ge(otok_done, m + 1)
                for f in range(4):
                    last = nc.tensor.transpose(banks[:, SHARED, f * P:f * P + n], o_tok[0:n, s, f * P:(f + 1) * P],
                                               ident[0:n, 0:n])
            last.then_inc(shared_psum, 1)

        def scores_of(m, h, a, kn, at):
            t0, n = TILES[m]
            nc.tensor.matmul(logits[0:n, at:at + kn], alibi[:, h, 0:n], rel[:, REL0 - t0 + a:REL0 - t0 + a + kn],
                             start=True, stop=False)
            return nc.tensor.matmul(logits[0:n, at:at + kn], qaT[:, m % 2, h, 0:n], kaT[:, h // 2, a:a + kn],
                                    start=False, stop=True)

        def qk(i):
            m, h = units[i]
            if h == 0:
                pe.wait_ge(shared_done, nth["qa", m])
            if i:
                pe.wait_ge(nmax_raw, i)
                if tails(i - 1):
                    pe.wait_ge(nmax_tail, tails(i - 1))
            for a in range(0, min(NKEYS[m], 1024), 512):
                last = scores_of(m, h, a, min(512, NKEYS[m] - a), a)
            last.then_inc(qk_done, 1)

        def qk_rest(i):
            m, h = units[i]
            pe.wait_ge(nmax_raw, i + 1)
            scores_of(m, h, 1024, NKEYS[m] - 1024, 0).then_inc(qk_tail, 1)

        def gram(i):
            m, h = units[i]
            if i >= 2 if h >= 2 else i:
                pe.wait_ge(gram_read, i - 1 if h >= 2 else i)
            if h == 0:
                pe.wait_ge(key_done, m + 1)
                for f in range(4):
                    for par in range(2):
                        r, t = slice(HD * par, HD * (par + 1)), slice(f * P, (f + 1) * P)
                        last = nc.tensor.matmul(banks[:, GRAM + par, t], key[r, m % 2, t], qt[r, m % 2, t],
                                                start=True, stop=True)
            else:
                j = levels_to(m, h) - 1
                pe.wait_ge(x_done, j + 1)
                for f in range(4):
                    t = slice(f * P, (f + 1) * P)
                    last = nc.tensor.matmul(banks[:, GRAM + h % 2, t], xl[:, j % 2, t], xq[:, j % 2, t],
                                            start=True, stop=True)
            last.then_inc(gram_psum, 1)

        def turn(i):
            m, h = units[i]
            n = TILES[m][1]
            pe.wait_ge(exp_done, i + 1)
            if i:
                pe.wait_ge(t_act, i)
                if dve_turns(i - 1):
                    pe.wait_ge(t_dve, dve_turns(i - 1))
                if tails(i - 1):
                    pe.wait_ge(t_act_last, tails(i - 1))
            for j in range(min(m + 1, 2 * PER_BANK)):
                k0, kn = TILES[j]
                last = nc.tensor.transpose(banks[0:kn, T_LO + j // PER_BANK, j % PER_BANK * P:j % PER_BANK * P + n],
                                           probs[0:n, i % 2, k0:k0 + kn], ident[0:n, 0:n])
            last.then_inc(t_psum, 1)

        def turn_rest(i):
            m, h = units[i]
            k0, kn = TILES[m]
            pe.wait_ge(t_act, i + 1)
            nc.tensor.transpose(banks[0:kn, T_LO, 0:P], probs[:, i % 2, k0:k0 + kn], ident[:, :]).then_inc(t_last, 1)

        def pv(i):
            m, h = units[i]
            n = TILES[m][1]
            pe.wait_ge(t_act, i + 1)
            if m >= PER_BANK:
                pe.wait_ge(t_dve, dve_turns(i))
            if m == NT - 1:
                pe.wait_ge(t_act_last, tails(i))
            if h == 0 and m:
                pe.wait_ge(otok_done, m)
            for j in range(m + 1):
                kn = TILES[j][1]
                last = nc.tensor.matmul(banks[0:n, PV, h * HD:(h + 1) * HD], pT[0:kn, i % 2, j, 0:n],
                                        va[0:kn, j, h * HD:(h + 1) * HD], start=(j == 0), stop=(j == m))
            last.then_inc(pv_done, 1)

        on_shared("qa", 0)
        for i, (m, h) in enumerate(steps):
            if i < NU:
                qk(i)
                gram(i)
                if m == NT - 1:
                    qk_rest(i)
            if shared_job(m, h):
                on_shared(*shared_job(m, h))
            if 1 <= i <= NU:
                turn(i - 1)
            if 2 <= i <= NU + 1:
                pv(i - 2)
            if 1 <= i <= NU and units[i - 1][0] == NT - 1:
                turn_rest(i - 1)

    @block.scalar
    def _(act):
        act.preload_act_table_set("natural_log_exp_and_others")

        def exps(i):
            m, h = units[i]
            n = TILES[m][1]
            act.wait_ge(nmax_done, i + 1)
            if h == 0 and m >= 2:
                act.wait_ge(rs_done, m - 1)
            at = probs[0:n, i % 2, 0:NKEYS[m]]
            nc.scalar.activation(at, at, ACT.Exp, bias=nmax[0:n, i % 2, 2:3], accum_out=sums[0:n, m % 2, h:h + 1])\
              .then_inc(exp_done, 1)

        def turned(i):
            m, h = units[i]
            n = TILES[m][1]
            act.wait_ge(t_psum, i + 1)
            if i >= 2:
                act.wait_ge(pv_done, i - 1)
            last = nc.scalar.activation(pT[0:N_META, i % 2, 0, 0:n], banks[0:N_META, T_LO, 0:n], ACT.Copy)
            if m:
                k = min(PER_BANK - 1, m)
                last = nc.scalar.activation(pT[:, i % 2, 1:1 + k, 0:n],
                                            banks[:, T_LO, P:(1 + k) * P].rearrange("p (f t) -> p f t", f=k)[:, :, 0:n],
                                            ACT.Copy)
            last.then_inc(t_act, 1)

        def turned_rest(i):
            act.wait_ge(t_last, tails(i))
            nc.scalar.activation(pT[:, i % 2, NT - 1, :], banks[:, T_LO, 0:P], ACT.Copy).then_inc(t_act_last, 1)

        def level_exp(m, h):
            i = levels_to(m, h) - 1
            act.wait_ge(ex_in, i + 1)
            nc.scalar.activation(ex[:, i % 2, :], ex[:, i % 2, :], ACT.Exp).then_inc(ex_out, 1)

        def gates(m, stage):
            z = zt[:, m % 2, :]
            if stage == 2:
                act.wait_ge(zq_loaded[m % 2], 32 * (m // 2 + 1))
                if m:
                    act.wait_ge(ln_done, m)
                nc.scalar.activation(u[:, :], z, ACT.Abs).then_inc(abs_done, 1)
                act.wait_ge(abs_done, m + 1)
                nc.scalar.activation(u[:, :], u[:, :], ACT.Exp, scale=-1.0).then_inc(u_done, 1)
            if stage == 3:
                act.wait_ge(u_done, m + 1)
                if m:
                    act.wait_ge(b_done, m)
                nc.scalar.activation(lnw[:, :], u[:, :], ACT.Ln, bias=1.0).then_inc(ln_done, 1)
            if stage == 4:
                act.wait_ge(key_in, m + 1)
                if m >= 2:
                    act.wait_ge(gram_psum, STEPS * (m - 2) + 1)
                    act.wait_ge(x_done, levels_to(m - 2, LEVELS))
                    act.wait_ge(ke_done, m - 1)
                nc.scalar.activation(key[:, m % 2, :], key_arg[:, :], ACT.Exp, scale=-1.0).then_inc(key_done, 1)
            if stage == 5:
                act.wait_ge(kd_in, m + 1)
                nc.scalar.activation(kd[:, :], kd[:, :], ACT.Exp).then_inc(kd_done, 1)
                if m:
                    act.wait_ge(ke_done, m)
                nc.scalar.activation(eb[:, :], b[:, m % 2, :], ACT.Exp).then_inc(eb_done, 1)

        def off_shared(what, m):
            act.wait_ge(shared_psum, nth[what, m])
            t0, n = TILES[m]
            src = banks[:, SHARED, :]
            if what == "qa":
                if m == 0:
                    act.wait_ge(pads, 6)
                for par in range(2):
                    r = slice(HD * par, HD * (par + 1))
                    to = qaT[r, m % 2, :, 0:n].rearrange("p (f two) t -> p two f t", two=2)[:, par]
                    ins_ = nc.scalar.activation(to, four(src)[r, :, 0:n], ACT.Copy, scale=HD ** -0.5)
            if what == "kT":
                ins_ = nc.scalar.activation(k_tok[:, :], src, ACT.Copy)
            if what == "state":
                if m:
                    act.wait_ge(state_done, m)
                ins_ = nc.scalar.activation(added[:, :], src, ACT.Copy)
            if what == "out":
                ins_ = nc.scalar.activation(on[:, :], src, ACT.Copy)
            if what == "ot_rec":
                ins_ = nc.scalar.activation(oT[:, 4:8, t0:t0 + n], four(src)[:, :, P - n:P], ACT.Copy)
            if what == "ot_att":
                ins_ = nc.scalar.activation(oT[:, 0:4, t0:t0 + n], four(src)[:, :, 0:n], ACT.Copy)
            ins_.then_inc(shared_done, 1)

        off_shared("qa", 0)
        for stage in (2, 3, 4, 5):
            gates(0, stage)
        level_exp(0, 1)
        for i, (m, h) in enumerate(steps):
            if i < NU:
                exps(i)
            if i + 2 < NU and steps[i + 2][1]:
                level_exp(*steps[i + 2])
            if m + 1 < NT:
                gates(m + 1, h)
            if shared_job(m, h):
                off_shared(*shared_job(m, h))
            if 1 <= i <= NU:
                turned(i - 1)
                if units[i - 1][0] == NT - 1:
                    turned_rest(i - 1)
            if h == 3 and 1 <= m:
                act.wait_ge(ssum_done, 2 * m)
                nc.scalar.activation(rsh[:, :], ssum[:, :], ACT.Ln).then_inc(lnv_done, 1)
                act.wait_ge(lnv_done, m)
                nc.scalar.activation(rsh[:, :], rsh[:, :], ACT.Exp, scale=-0.5).then_inc(rsh_done, 1)

    @block.vector
    def _(dve):
        chain = [0]

        def linked(ins_):
            chain[0] += 1
            ins_.then_inc(vlink, 1)
            dve.wait_ge(vlink, chain[0])

        dve.wait_ge(rel_done, 2)
        linked(nc.vector.tensor_copy(rel[:, :], rel_f))
        for h in range(A_HEADS):
            last = nc.vector.tensor_scalar(alibi[:, h, :], qpos[:, :], 2.0 ** (-8.0 * (h + 1) / A_HEADS), None, ALU.mult)
        last.then_inc(alibi_done, 1)
        dve.wait_ge(iota_done, 2)
        linked(nc.vector.tensor_tensor(xor, it_s, it_t, ALU.bitwise_xor))
        linked(nc.vector.tensor_tensor(after, it_t, it_s, ALU.is_gt))
        for l in range(LEVELS):
            linked(nc.vector.tensor_scalar(shifted, xor, l, None, ALU.logical_shift_right))
            linked(nc.vector.scalar_tensor_tensor(out=masks[:, l, :], in0=shifted, scalar=1.0, in1=after,
                                                  op0=ALU.is_equal, op1=ALU.mult))
        linked(nc.vector.tensor_scalar(masks[:, LEVELS, :], xor, 0.0, None, ALU.is_equal))
        linked(nc.vector.memset(xl[:, :, :], 0.0))
        linked(nc.vector.memset(keep[:, :], 1.0))
        linked(nc.vector.memset(four(keep[:, :])[:, :, 0:1], 0.0))
        linked(nc.vector.memset(S[:, :, :, :], 0.0))
        linked(nc.vector.memset(state[:, :, :], 0.0))

        def masked(i):
            m, h = units[i]
            n = TILES[m][1]
            N = min(NKEYS[m], 1024)
            if m == NT - 1:
                dve.wait_ge(late_causal, 1)
            dve.wait_ge(qk_done, i + 1)
            if i >= 2:
                dve.wait_ge(t_psum, i - 1)
                if tails(i - 2):
                    dve.wait_ge(t_last, tails(i - 2))
                dve.wait_ge(exp_done, i - 1)

            def part(at, src, init, out, signal):
                nc.vector.tensor_tensor_reduce(out=probs[0:n, i % 2, at], in0=src,
                                               in1=score[0:n, SC_OFF[m] + at.start:SC_OFF[m] + at.stop], scale=1.0,
                                               scalar=init, op0=ALU.add, op1=ALU.max,
                                               accum_out=nmax[0:n, i % 2, out:out + 1]).then_inc(signal, 1)

            part(slice(0, N), logits[0:n, 0:N], TAKEN, 0, nmax_raw)
            dve.wait_ge(nmax_raw, i + 1)
            peak = 0
            if m == NT - 1:
                dve.wait_ge(qk_tail, tails(i))
                part(slice(N, NKEYS[m]), logits[0:n, 0:NKEYS[m] - N], nmax[0:n, i % 2, 0:1], 1, nmax_tail)
                dve.wait_ge(nmax_tail, tails(i))
                peak = 1
            nc.vector.tensor_scalar(nmax[0:n, i % 2, 2:3], nmax[0:n, i % 2, peak:peak + 1], -1.0, None, ALU.mult)\
              .then_inc(nmax_done, 1)

        def turned(i):
            m, h = units[i]
            n = TILES[m][1]
            if m >= PER_BANK:
                dve.wait_ge(t_psum, i + 1)
                if i >= 2:
                    dve.wait_ge(pv_done, i - 1)
                k = min(m + 1 - PER_BANK, PER_BANK)
                nc.vector.tensor_copy(pT[:, i % 2, PER_BANK:PER_BANK + k, 0:n],
                                      banks[:, T_HI, 0:k * P].rearrange("p (f t) -> p f t", f=k)).then_inc(t_dve, 1)

        def normed(m):
            n = TILES[m][1]
            dve.wait_ge(exp_done, A_HEADS * (m + 1))
            nc.vector.reciprocal(rsums[0:n, m % 2, :], sums[0:n, m % 2, :]).then_inc(rs_done, 1)
            dve.wait_ge(rs_done, m + 1)
            dve.wait_ge(pv_done, A_HEADS * (m + 1))
            if m >= 2:
                dve.wait_ge(shared_psum, nth["ot_att", m - 2])
            nc.vector.tensor_tensor(o_tok[0:n, m % 2, :].rearrange("p (h e) -> p h e", h=A_HEADS),
                                    banks[0:n, PV, :].rearrange("p (h e) -> p h e", h=A_HEADS),
                                    rsums[0:n, m % 2, :].rearrange("p (h e) -> p h e", e=1).to_broadcast([n, A_HEADS, HD]),
                                    ALU.mult).then_inc(otok_done, 1)

        def gates(m, stage):
            s = m % 2
            z = zt[:, s, :]
            if stage == 4:
                dve.wait_ge(ln_done, m + 1)
                if m:
                    dve.wait_ge(key_done, m)
                nc.vector.scalar_tensor_tensor(out=key_arg[:, :], in0=z, scalar=0.0, in1=lnw[:, :], op0=ALU.max,
                                               op1=ALU.add).then_inc(key_in, 1)
                dve.wait_ge(key_in, m + 1)
                nc.vector.scalar_tensor_tensor(out=lnw[:, :], in0=z, scalar=0.0, in1=lnw[:, :], op0=ALU.min,
                                               op1=ALU.subtract).then_inc(logf_done, 1)
                dve.wait_ge(logf_done, m + 1)
                nc.vector.tensor_tensor_scan(b[:, s, :], keep[:, :], lnw[:, :], 0.0, ALU.mult, ALU.add)\
                  .then_inc(b_done, 1)
            if stage == 5:
                dve.wait_ge(b_done, m + 1)
                if m:
                    dve.wait_ge(shared_psum, nth["kT", m - 1])
                b3 = four(b[:, s, :])
                nc.vector.tensor_tensor(four(kd[:, :]), b3[:, :, P - 1:P].to_broadcast([P, 4, P]), b3, ALU.subtract)\
                  .then_inc(kd_in, 1)
            if stage == 6:
                dve.wait_ge(eb_done, m + 1)
                dve.wait_ge(key_done, m + 1)
                nc.vector.tensor_copy(elast[:, s, :], four(eb[:, :])[:, :, P - 1])
                nc.vector.tensor_tensor(qe[:, s, :], qt[:, s, :], eb[:, :], ALU.mult)
                nc.vector.tensor_tensor(kd[:, :], key[:, s, :], kd[:, :], ALU.mult).then_inc(ke_done, 1)

        def exponents(m, h):
            l, i = h - 1, levels_to(m, h) - 1
            if i >= 2:
                dve.wait_ge(x_done, i - 1)
            bl, el = halves(b[:, m % 2, :], l), halves(ex[:, i % 2, :], l)
            ref = bl[:, :, 0, 2 ** l - 1:2 ** l].to_broadcast([P, W // 2 ** (l + 1), 2 ** l])
            nc.vector.tensor_tensor(el[:, :, 0, :], ref, bl[:, :, 0, :], ALU.subtract)
            nc.vector.tensor_tensor(el[:, :, 1, :], bl[:, :, 1, :], ref, ALU.subtract).then_inc(ex_in, 1)

        def scores_of(i):
            m, h = units[i]
            dve.wait_ge(gram_psum, i + 1)
            if i:
                dve.wait_ge(gram_read, i)
            if h == 0:
                mask = masks[:, LEVELS, :].rearrange("p (f t) -> p f t", f=1).to_broadcast([P, 4, P])
                for par in range(2):
                    at = S[:, m % 2, :, :].rearrange("p (f two) t -> p two f t", two=2)[:, par, :, :]
                    last = nc.vector.copy_predicated(at, mask, four(banks[:, GRAM + par, :]))
            else:
                l = h - 1
                mask = halves(masks[:, l, :], l)[:, :, 1, :].rearrange("p (a n) t -> p a n t", a=1)\
                    .to_broadcast([P, 8, P // 2 ** h, 2 ** l])
                at = S[:, m % 2, :, :].rearrange("p h (n two t) -> p h n two t", two=2, t=2 ** l)[:, :, :, 1, :]
                last = nc.vector.copy_predicated(at, mask, banks[:, GRAM + h % 2, :]
                                                 .rearrange("p (h n t) -> p h n t", h=8, t=2 ** l))
            last.then_inc(gram_read, 1)

        def next_state(m):
            dve.wait_ge(shared_done, nth["out", m])
            for f in range(4):
                for par in range(2):
                    r = slice(HD * par, HD * (par + 1))
                    last = nc.vector.scalar_tensor_tensor(out=state[r, f, r], in0=state[r, f, r],
                                                          scalar=elast[r, m % 2, f:f + 1],
                                                          in1=added[r, f * P + HD * par:f * P + HD * (par + 1)],
                                                          op0=ALU.mult, op1=ALU.add)
            last.then_inc(state_done, 1)

        for stage in (4, 5, 6):
            gates(0, stage)
        exponents(0, 1)
        for i, (m, h) in enumerate(steps):
            if i < NU:
                masked(i)
            for r in late_rounds.get(i, ()):
                if r:
                    dve.wait_ge(taken, 2 * r)
                nc.vector.max(top8[:, :], late).then_inc(taken, 1)
            if i + 2 < NU and steps[i + 2][1]:
                exponents(*steps[i + 2])
            if m + 1 < NT:
                gates(m + 1, h)
            if i < NU:
                if h == 0 and m >= 2:
                    dve.wait_ge(shared_psum, nth["out", m - 2])
                scores_of(i)
            if 1 <= i <= NU:
                turned(i - 1)
            for r in late_rounds.get(i, ()):
                dve.wait_ge(taken, 2 * r + 1)
                nc.vector.match_replace(late, top8[:, :], late, TAKEN).then_inc(taken, 1)
            if i == LATE1:
                dve.wait_ge(taken, 2 * ROUNDS)
                nc.vector.tensor_scalar(late, late, TAKEN_BELOW, MASKED, ALU.is_ge, ALU.mult).then_inc(late_mask, 1)
            if h == 2 and m:
                normed(m - 1)
                next_state(m - 1)
            if h == 3 and m:
                dve.wait_ge(sq_done, m)
                if m >= 2:
                    dve.wait_ge(rsh_done, m - 1)
                nc.vector.tensor_reduce(ssum[:, :], sq[:, :].rearrange("p (h e) -> p h e", h=8),
                                        mybir.AxisListType.X, ALU.add).then_inc(ssum_done, 1)
                dve.wait_ge(ssum_done, 2 * m - 1)
                nc.vector.tensor_scalar(ssum[:, :], ssum[:, :], 1.0 / HD, LN_EPS, ALU.mult, ALU.add).then_inc(ssum_done, 1)
            if h == 4 and m:
                dve.wait_ge(rsh_done, m)
                on8 = on[:, :].rearrange("p (h e) -> p h e", h=8)
                linked(nc.vector.tensor_tensor(on8, on8, rsh[:, :].rearrange("p (h e) -> p h e", e=1)
                                               .to_broadcast([P, 8, HD]), ALU.mult))
                dve.wait_ge(gated, m)
                nc.vector.tensor_tensor(on[:, :], on[:, :], gt[:, (m - 1) % 2, :], ALU.mult).then_inc(on_done, 1)


class NormSteps:

    def __init__(self, nc, c, sem, sb, banks, ident, tag, y, tiles, t_banks=(), split=None):
        self.nc, self.banks, self.ident, self.y, self.tiles, self.t_banks, self.split = (
            nc, banks, ident, y, tiles, t_banks, split)
        self.gb = sb(c, f"{tag}_g", [P, D])
        self.bb = sb(c, f"{tag}_b", [P, D])
        self.bn6 = sb(c, f"{tag}_bn6", [P, NT, 2, 6])
        self.mv = sb(c, f"{tag}_mv", [P, NT, 2])
        self.std = sb(c, f"{tag}_std", [P, NT])
        self.rstd = sb(c, f"{tag}_rstd", [P, NT])
        self.shift = sb(c, f"{tag}_shift", [P, NT])
        self.gb_loaded, self.bn, self.var, self.rooted, self.inverted, self.shifted, self.scaled, self.gained, self.biased = (
            sem(f"{tag}_{k}") for k in ("gb_loaded", "bn", "var", "rooted", "inverted", "shifted", "scaled", "gained", "biased"))
        if split:
            self.turned, self.hi, self.lo = sem(f"{tag}_turned"), sem(f"{tag}_hi"), sem(f"{tag}_lo")

    def load(self, sp, g_row, b_row):
        for dst, row in ((self.gb, g_row), (self.bb, b_row)):
            sp.dma_start(dst[:, :], row.rearrange("(a n) -> a n", a=1).to_broadcast([P, D])).then_inc(self.gb_loaded, 16)

    def stats(self, dve, j):
        m = self.tiles[j]
        n = TILES[m][1]
        self.nc.vector.bn_stats(self.bn6[0:n, m, 0, :], self.y[0:n, m, 0:512])
        self.nc.vector.bn_stats(self.bn6[0:n, m, 1, :], self.y[0:n, m, 512:D]).then_inc(self.bn, 1)
        dve.wait_ge(self.bn, 2 * j + 1)
        self.nc.vector.bn_aggr(self.mv[0:n, m, :], self.bn6[0:n, m, :, :].rearrange("p a b -> p (a b)")).then_inc(self.bn, 1)
        dve.wait_ge(self.bn, 2 * j + 2)
        self.nc.vector.tensor_scalar(self.mv[0:n, m, 1:2], self.mv[0:n, m, 1:2], LN_EPS, None, ALU.add).then_inc(self.var, 1)

    def root(self, act, j):
        m = self.tiles[j]
        n = TILES[m][1]
        act.wait_ge(self.var, j + 1)
        self.nc.scalar.activation(self.std[0:n, m:m + 1], self.mv[0:n, m, 1:2], ACT.Sqrt).then_inc(self.rooted, 1)

    def factors(self, dve, j):
        m = self.tiles[j]
        n = TILES[m][1]
        dve.wait_ge(self.rooted, j + 1)
        self.nc.vector.reciprocal(self.rstd[0:n, m:m + 1], self.std[0:n, m:m + 1]).then_inc(self.inverted, 1)
        dve.wait_ge(self.inverted, j + 1)
        self.nc.vector.tensor_scalar(self.shift[0:n, m:m + 1], self.mv[0:n, m, 0:1], self.rstd[0:n, m:m + 1], -1.0, ALU.mult, ALU.mult)\
          .then_inc(self.shifted, 1)

    def scale(self, act, j):
        m = self.tiles[j]
        n = TILES[m][1]
        act.wait_ge(self.shifted, j + 1)
        self.nc.scalar.activation(self.y[0:n, m, :], self.y[0:n, m, :], ACT.Identity, bias=self.shift[0:n, m:m + 1],
                             scale=self.rstd[0:n, m:m + 1]).then_inc(self.scaled, 1)

    def gains(self, dve, j):
        m = self.tiles[j]
        n = TILES[m][1]
        if j == 0:
            dve.wait_ge(self.gb_loaded, 32)
        dve.wait_ge(self.scaled, j + 1)
        self.nc.vector.tensor_tensor(self.y[0:n, m, :], self.y[0:n, m, :], self.gb[0:n, :], ALU.mult).then_inc(self.gained, 1)

    def bias(self, pool, j):
        m = self.tiles[j]
        n = TILES[m][1]
        pool.wait_ge(self.gained, j + 1)
        self.nc.gpsimd.tensor_tensor(self.y[0:n, m, :], self.y[0:n, m, :], self.bb[0:n, :], ALU.add).then_inc(self.biased, 1)

    def bank_of(self, i):
        return self.t_banks[i % len(self.t_banks)]

    def turn(self, pe, j):
        m = self.tiles[j]
        n = TILES[m][1]
        pe.wait_ge(self.biased, j + 1)
        for q in range(2):
            i = 2 * j + q
            if i >= len(self.t_banks):
                pe.wait_ge(self.lo, i - len(self.t_banks) + 1)
            for k in range(4):
                kk = 4 * q + k
                last = self.nc.tensor.transpose(self.banks[:, self.bank_of(i), k * P:k * P + n], self.y[0:n, m, kk * P:(kk + 1) * P],
                                           self.ident[0:n, 0:n])
            last.then_inc(self.turned, 1)

    def high(self, act, j):
        t0, n = TILES[self.tiles[j]]
        for q in range(2):
            i = 2 * j + q
            act.wait_ge(self.turned, i + 1)
            src = self.banks[:, self.bank_of(i), :].rearrange("p (k t) -> p k t", k=4)[:, :, 0:n]
            self.nc.scalar.activation(self.split[0][:, 4 * q:4 * q + 4, t0:t0 + n], src, ACT.Copy).then_inc(self.hi, 1)

    def low(self, dve, j):
        t0, n = TILES[self.tiles[j]]
        for q in range(2):
            i = 2 * j + q
            dve.wait_ge(self.hi, i + 1)
            src = self.banks[:, self.bank_of(i), :].rearrange("p (k t) -> p k t", k=4)[:, :, 0:n]
            at = slice(4 * q, 4 * q + 4)
            self.nc.vector.tensor_tensor(self.split[1][:, at, t0:t0 + n], src, self.split[0][:, at, t0:t0 + n].bitcast(F32),
                                    ALU.subtract).then_inc(self.lo, 1)


def out_projection(nc, c, sem, sb, banks, ident, x, meta, ins, oT, y, hH, hL):
    w = sb(c, "w_out_sb", [P, DC, D])
    loaded_w, done, added = sem("w_out_loaded"), sem("op_psum"), sem("op_added")
    h_loaded = [sem(f"op_h{i}") for i in range(3)]
    tiles = list(range(NT))
    norm = NormSteps(nc, c, sem, sb, banks, ident, "n0", y, tiles, (4, 5, 6, 7), (hH, hL))
    NB = 4
    block = c.enter_context(nc.Block())

    @block.sync
    def _(sp):
        w_v = ins["w_out"][0].rearrange("(k p) f -> p k f", p=P)
        for k in range(0, DC, 2):
            sp.dma_start(w[:, k:k + 2, :], w_v[:, k:k + 2, :]).then_inc(loaded_w, 16)
        for m, (t0, n) in enumerate(TILES):
            src = meta if m == 0 else x[t0 - N_META:t0 - N_META + n, :]
            if m >= 3:
                sp.wait_ge(h_loaded[m % 3], 16 * (m // 3))
            sp.dma_start(y[0:n, m, :], src).then_inc(h_loaded[m % 3], 16)
            if m == 2:
                norm.load(sp, ins["ln_mix_g"][0], ins["ln_mix_b"][0])

    @block.gpsimd
    def _(pool):
        for j in range(NT):
            norm.bias(pool, j)

    @block.tensor
    def _(pe):
        pe.wait_ge(loaded_w, 16 * (DC // 2))
        for T in range(NT + 4):
            if T >= 4:
                norm.turn(pe, T - 4)
            for i in (2 * T, 2 * T + 1) if T < NT else ():
                t0, n = TILES[T]
                if i >= NB:
                    pe.wait_ge(added, i - NB + 1)
                for k in range(DC):
                    last = nc.tensor.matmul(banks[0:n, i % NB, :], oT[:, k, t0:t0 + n],
                                            w[:, k, (i % 2) * 512:(i % 2 + 1) * 512], start=(k == 0), stop=(k == DC - 1))
                last.then_inc(done, 1)

    @block.scalar
    def _(act):
        for T in range(NT + 4):
            if T >= 4:
                norm.high(act, T - 4)
            if 1 <= T <= NT:
                norm.scale(act, T - 1)
            if T < NT:
                norm.root(act, T)

    @block.vector
    def _(dve):
        for T in range(NT + 4):
            if T >= 4:
                norm.low(dve, T - 4)
            if 2 <= T <= NT + 1:
                norm.gains(dve, T - 2)
            if 1 <= T <= NT:
                norm.factors(dve, T - 1)
            if T < NT:
                n = TILES[T][1]
                dve.wait_ge(h_loaded[T % 3], 16 * (T // 3 + 1))
                for i in (2 * T, 2 * T + 1):
                    dve.wait_ge(done, i + 1)
                    at = y[0:n, T, (i % 2) * 512:(i % 2 + 1) * 512]
                    nc.vector.scalar_tensor_tensor(out=at, in0=at, scalar=ALPHA, in1=banks[0:n, i % NB, :], op0=ALU.mult,
                                                   op1=ALU.add).then_inc(added, 1)
                dve.wait_ge(added, 2 * T + 2)
                norm.stats(dve, T)


def pool_mixer(nc, c, sem, sb, banks, ident, ins, y, hH, hL):
    NW = len(POOL_WINDOWS)
    TAIL = 32
    w = sb(c, "w_pool_sb", [P, NW, 2, PG])
    scale = sb(c, "pool_scale_sb", [P, NW, PG])
    band = sb(c, "band", [P, NW, P])
    band_tail = sb(c, "band_tail", [P, NW, P])
    band_meta = sb(c, "band_meta", [N_META, NW, P])
    dT = sb(c, "dT", [P, 2, DC, P])
    loaded, w_ready, made, made_all, d_psum, d_act, d_dve, psum, added = (
        sem("pool_loaded"), sem("pool_w"), sem("band_made"), sem("bands_done"), sem("d_psum"), sem("d_act"),
        sem("d_dve"), sem("pool_psum"), sem("pool_added"))
    n1 = NormSteps(nc, c, sem, sb, banks, ident, "n1", y, list(range(NT)))
    n2 = NormSteps(nc, c, sem, sb, banks, ident, "n2", y, list(range(1, NT)), (4, 5, 6, 7), (hH, hL))
    NP = NT - 1
    END = NP + 8
    block = c.enter_context(nc.Block())

    @block.sync
    def _(sp):
        n1.load(sp, ins["ln_ffn_g"][0], ins["ln_ffn_b"][0])
        sp.dma_start(w[:, :, :, :], ins["w_pool"][0].rearrange("g (k p) f -> p g k f", p=P)).then_inc(loaded, 16)
        sp.dma_start(scale[:, :, :].rearrange("p g f -> p (g f)"), ins["pool_scale"].to_broadcast([P, D]))\
          .then_inc(loaded, 16)
        n2.load(sp, ins["ln_mix_g"][1], ins["ln_mix_b"][1])

    @block.gpsimd
    def _(pool):
        count = 0
        for g, win in enumerate(POOL_WINDOWS):
            for mat, rows, base in ((band, P, 0), (band_tail, P, P), (band_meta, N_META, N_META)):
                at = mat[0:rows, g, :]
                nc.gpsimd.memset(at, 1.0 / win).then_inc(made, 1)
                count += 1
                pool.wait_ge(made, count)
                nc.gpsimd.affine_select(out=at, in_=at, compare_op=ALU.is_gt, fill=0.0, base=win - base,
                                        pattern=[[-1, P]], channel_multiplier=1).then_inc(made, 1)
                count += 1
                pool.wait_ge(made, count)
                if base == 0:
                    nc.gpsimd.affine_select(out=at, in_=at, compare_op=ALU.is_ge, fill=0.0, base=0,
                                            pattern=[[1, P]], channel_multiplier=-1).then_inc(made, 1)
                    count += 1
                    pool.wait_ge(made, count)
                    nc.gpsimd.tensor_tensor(at, at, ident[:, :], ALU.subtract).then_inc(made_all, 1)
        pool.wait_ge(loaded, 32)
        for k in range(2):
            nc.gpsimd.tensor_tensor(w[:, :, k, :], w[:, :, k, :], scale[:, :, :], ALU.mult).then_inc(w_ready, 1)
        for T in range(END):
            if 0 <= T - 7 < NP:
                n2.bias(pool, T - 7)
            if 0 <= T - 2 < NT:
                n1.bias(pool, T - 2)

    @block.tensor
    def _(pe):
        pe.wait_ge(made_all, NW)
        pe.wait_ge(made, 3 * 2 * NW + NW)
        pe.wait_ge(w_ready, 2)
        for T in range(END):
            if 0 <= T - 8 < NP:
                n2.turn(pe, T - 8)
            j = T - 5
            if 0 <= j < NP:
                pe.wait_ge(d_act, j + 1)
                pe.wait_ge(d_dve, j + 1)
                if j:
                    pe.wait_ge(added, 2 * j)
                for g in range(NW):
                    for k in range(2):
                        last = nc.tensor.matmul(banks[:, 2 + g // 2, g % 2 * PG:(g % 2 + 1) * PG],
                                                dT[:, j % 2, 2 * g + k, :], w[:, g, k, :], start=(k == 0), stop=(k == 1))
                last.then_inc(psum, 1)
            j = T - 4
            if 0 <= j < NP:
                m = j + 1
                pe.wait_ge(n1.biased, m + 1)
                if j:
                    pe.wait_ge(d_act, j)
                    pe.wait_ge(d_dve, j)
                for k in range(DC):
                    at = banks[:, k // 4, k % 4 * P:(k % 4 + 1) * P]
                    cols = slice(k * P, (k + 1) * P)
                    g = k // 2
                    nc.tensor.matmul(at, y[:, m, cols], band[:, g, :], start=True, stop=False)
                    if m == 1:
                        last = nc.tensor.matmul(at, y[0:N_META, 0, cols], band_meta[:, g, :], start=False, stop=True)
                    else:
                        last = nc.tensor.matmul(at, y[P - TAIL:P, m - 1, cols], band_tail[P - TAIL:P, g, :],
                                                start=False, stop=True)
                last.then_inc(d_psum, 1)

    @block.scalar
    def _(act):
        for T in range(END):
            if 0 <= T - 8 < NP:
                n2.high(act, T - 8)
            if 0 <= T - 6 < NP:
                n2.scale(act, T - 6)
            if 0 <= T - 5 < NP:
                n2.root(act, T - 5)
            j = T - 4
            if 0 <= j < NP:
                act.wait_ge(d_psum, j + 1)
                if j >= 2:
                    act.wait_ge(psum, j - 1)
                nc.scalar.activation(dT[:, j % 2, 0:4, :], banks[:, 0, :].rearrange("p (k t) -> p k t", k=4), ACT.Copy)\
                  .then_inc(d_act, 1)
            if 0 <= T - 1 < NT:
                n1.scale(act, T - 1)
            if T < NT:
                n1.root(act, T)

    @block.vector
    def _(dve):
        for T in range(END):
            if 0 <= T - 8 < NP:
                n2.low(dve, T - 8)
            if 0 <= T - 7 < NP:
                n2.gains(dve, T - 7)
            if 0 <= T - 6 < NP:
                n2.factors(dve, T - 6)
            j = T - 5
            if 0 <= j < NP:
                m = j + 1
                dve.wait_ge(psum, j + 1)
                if m + 1 < NT:
                    dve.wait_ge(d_psum, j + 2)
                for half in range(2):
                    at = y[:, m, half * 512:(half + 1) * 512]
                    nc.vector.scalar_tensor_tensor(out=at, in0=at, scalar=ALPHA, in1=banks[:, 2 + half, :],
                                                   op0=ALU.mult, op1=ALU.add).then_inc(added, 1)
                dve.wait_ge(added, 2 * j + 2)
                n2.stats(dve, j)
            j = T - 4
            if 0 <= j < NP:
                dve.wait_ge(d_psum, j + 1)
                if j >= 2:
                    dve.wait_ge(psum, j - 1)
                nc.vector.tensor_copy(dT[:, j % 2, 4:8, :], banks[:, 1, :].rearrange("p (k t) -> p k t", k=4))\
                  .then_inc(d_dve, 1)
            if 0 <= T - 2 < NT:
                n1.gains(dve, T - 2)
            if 0 <= T - 1 < NT:
                n1.factors(dve, T - 1)
            if T < NT:
                n1.stats(dve, T)


def ffn(nc, c, sem, sb, banks, ident, tag, y, hH, hL, tiles, chunks, w_gate, w_up, w_down, final=None):
    NCH = len(chunks)
    CW = max(n for _, n in chunks)
    NU = 2 * NCH
    NJ = 2 * len(tiles)
    wg = w_gate.rearrange("(k p) f -> p k f", p=P)
    wu = w_up.rearrange("(k p) f -> p k f", p=P)
    wd = w_down.rearrange("(i u p) f -> i p u f", u=2, p=P)
    raw = sb(c, f"{tag}_raw", [P, 2, DC, P])
    wH = sb(c, f"{tag}_wH", [P, 2, 2, DC, P], F32R)
    wL = sb(c, f"{tag}_wL", [P, 2, 2, DC, P], F32R)
    draw = sb(c, f"{tag}_draw", [P, 2, D])
    dH = sb(c, f"{tag}_dH", [P, 2, D], F32R)
    dL = sb(c, f"{tag}_dL", [P, 2, D], F32R)
    hidH = sb(c, f"{tag}_hidH", [P, 2, L], F32R)
    hidL = sb(c, f"{tag}_hidL", [P, 2, L], F32R)
    silu = sb(c, f"{tag}_silu", [P, 2, CW])
    hid = sb(c, f"{tag}_hid", [P, 2, CW])

    s = {k: sem(f"{tag}_{k}") for k in ("alpha", "raw", "w_hi", "w_lo", "draw", "d_hi", "d_lo", "gu_psum",
                                        "silu", "hid", "hid_hi", "hid_lo", "d_psum", "added")}
    FREE = 1
    ITERS = FF_TILES // 2
    NF = len(tiles)
    if final:
        norm = NormSteps(nc, c, sem, sb, banks, ident, f"{tag}_norm", y, tiles)
        stored = sem(f"{tag}_stored")
    block = c.enter_context(nc.Block())

    @block.sync
    def _(sp):
        if final:
            norm.load(sp, final[0], final[1])
        with sp.Fori(0, ITERS) as i:
            for u in range(2):
                sp.wait_ge(s["w_hi"], FREE + 2 * i + u)
                sp.wait_ge(s["w_lo"], FREE + 2 * i + u)
                for g, w in enumerate((wg, wu)):
                    sp.dma_start(raw[:, g, :, :], w[:, :, bass.ds((2 * i + u) * P, P)]).then_inc(s["raw"], 16)
                if u == 0:
                    sp.wait_ge(s["d_hi"], FREE + i)
                    sp.wait_ge(s["d_lo"], FREE + i)
                    sp.dma_start(draw[:, :, :], wd[bass.ds(i, 1), :, :, :].rearrange("a p u f -> p (a u) f"))\
                      .then_inc(s["draw"], 16)
        if final:
            for j, m in enumerate(tiles):
                t0, n = TILES[m]
                sp.wait_ge(norm.biased, j + 1)
                sp.dma_start(final[2][0, t0 - N_META:t0 - N_META + n, :], y[0:n, m, :]).then_inc(stored, 16)
            sp.wait_ge(stored, 16 * NF)

    @block.gpsimd
    def _(pool):
        pool.sem_inc(s["w_lo"], FREE)
        pool.sem_inc(s["d_lo"], FREE)
        for m in tiles:
            n = TILES[m][1]
            nc.gpsimd.tensor_scalar(y[0:n, m, :], y[0:n, m, :], ALPHA, 1.0, ALU.mult, ALU.mult).then_inc(s["alpha"], 1)
        with pool.Fori(0, ITERS) as i:
            for u in range(2):
                pool.wait_ge(s["w_hi"], FREE + 2 * i + u + 1)
                pool.wait_ge(s["gu_psum"], FREE + NU * i)
                nc.gpsimd.tensor_tensor(wL[:, u, :, :, :].rearrange("p g k f -> p (g k f)"),
                                        raw[:, :, :, :].rearrange("p g k f -> p (g k f)"),
                                        wH[:, u, :, :, :].rearrange("p g k f -> p (g k f)").bitcast(F32),
                                        ALU.subtract).then_inc(s["w_lo"], 1)
            pool.wait_ge(s["d_hi"], FREE + i + 1)
            nc.gpsimd.tensor_tensor(dL[:, :, :].rearrange("p u f -> p (u f)"), draw[:, :, :].rearrange("p u f -> p (u f)"),
                                    dH[:, :, :].rearrange("p u f -> p (u f)").bitcast(F32), ALU.subtract)\
              .then_inc(s["d_lo"], 1)
        if final:
            for j in range(NF):
                norm.bias(pool, j)

    @block.scalar
    def _(act):
        act.sem_inc(s["w_hi"], FREE)
        act.sem_inc(s["d_hi"], FREE)
        with act.Fori(0, ITERS) as i:
            act.wait_ge(s["gu_psum"], FREE + NU * i)
            for u in range(2):
                act.wait_ge(s["raw"], 32 * (2 * i + u + 1))
                nc.scalar.activation(wH[:, u, :, :, :], raw[:, :, :, :], ACT.Copy).then_inc(s["w_hi"], 1)
            act.wait_ge(s["draw"], 16 * (i + 1))
            act.wait_ge(s["d_psum"], FREE + NJ * i)
            nc.scalar.activation(dH[:, :, :], draw[:, :, :], ACT.Copy).then_inc(s["d_hi"], 1)

            def gate(q):
                n = chunks[q % NCH][1]
                act.wait_ge(s["gu_psum"], FREE + NU * i + q + 1)
                nc.scalar.activation(silu[:, q % 2, 0:n], banks[:, 2 * (q % 2), 0:n], ACT.Silu).then_inc(s["silu"], 1)

            def high(q):
                a, n = chunks[q % NCH]
                act.wait_ge(s["hid"], FREE + NU * i + q + 1)
                nc.scalar.activation(hidH[:, q // NCH, a:a + n], hid[:, q % 2, 0:n], ACT.Copy).then_inc(s["hid_hi"], 1)

            for q in range(NU):
                gate(q)
                high(q)
        if final:
            for T in range(NF + 1):
                if T >= 1:
                    norm.scale(act, T - 1)
                if T < NF:
                    norm.root(act, T)

    @block.vector
    def _(dve):
        dve.sem_inc(s["hid"], FREE)
        dve.sem_inc(s["added"], FREE)
        with dve.Fori(0, ITERS) as i:
            for q in range(NU):
                a, n = chunks[q % NCH]
                dve.wait_ge(s["silu"], NU * i + q + 1)
                nc.vector.tensor_tensor(hid[:, q % 2, 0:n], silu[:, q % 2, 0:n], banks[:, 2 * (q % 2) + 1, 0:n], ALU.mult)\
                  .then_inc(s["hid"], 1)
                dve.wait_ge(s["hid_hi"], NU * i + q + 1)
                nc.vector.tensor_tensor(hidL[:, q // NCH, a:a + n], hid[:, q % 2, 0:n],
                                        hidH[:, q // NCH, a:a + n].bitcast(F32), ALU.subtract).then_inc(s["hid_lo"], 1)
            dve.wait_ge(s["alpha"], len(tiles))
            dve.wait_ge(s["added"], FREE + NJ * i)
            for j in range(NJ):
                m = tiles[j // 2]
                n = TILES[m][1]
                dve.wait_ge(s["d_psum"], FREE + NJ * i + j + 1)
                at = y[0:n, m, (j % 2) * 512:(j % 2 + 1) * 512]
                nc.vector.tensor_tensor(at, at, banks[0:n, 4 + j % 4, :], ALU.add).then_inc(s["added"], 1)
        if final:
            dve.wait_ge(s["added"], FREE + NJ * ITERS)
            for T in range(NF + 2):
                if T >= 2:
                    norm.gains(dve, T - 2)
                if 1 <= T <= NF:
                    norm.factors(dve, T - 1)
                if T < NF:
                    norm.stats(dve, T)

    @block.tensor
    def _(pe):
        pe.sem_inc(s["gu_psum"], FREE)
        pe.sem_inc(s["d_psum"], FREE)
        with pe.Fori(0, ITERS) as i:
            for q in range(NU):
                u, (a, n) = q // NCH, chunks[q % NCH]
                if q % NCH == 0:
                    pe.wait_ge(s["w_hi"], FREE + 2 * i + u + 1)
                    pe.wait_ge(s["w_lo"], FREE + 2 * i + u + 1)
                if q >= 2:
                    pe.wait_ge(s["hid"], FREE + NU * i + q - 1)
                else:
                    pe.wait_ge(s["hid"], FREE + NU * i)
                for g in range(2):
                    for k in range(DC):
                        for part, (w, h) in enumerate(((wH, hL), (wL, hH), (wH, hH))):
                            last = nc.tensor.matmul(banks[:, 2 * (q % 2) + g, 0:n], w[:, u, g, k, :], h[:, k, a:a + n],
                                                    start=(k == 0 and part == 0), stop=(k == DC - 1 and part == 2))
                last.then_inc(s["gu_psum"], 1)
            pe.wait_ge(s["d_lo"], FREE + i + 1)
            pe.wait_ge(s["hid_lo"], NU * i + NCH)
            for j0 in range(0, NJ, 4):
                for u in range(2):
                    if j0 == 0 and u == 1:
                        pe.wait_ge(s["hid_lo"], NU * (i + 1))
                    for j in range(j0, min(j0 + 4, NJ)):
                        t0, n = TILES[tiles[j // 2]]
                        if u == 0:
                            pe.wait_ge(s["added"], FREE + NJ * i + max(j - 3, 0))
                        for part, (w, h) in enumerate(((dH, hidL), (dL, hidH), (dH, hidH))):
                            last = nc.tensor.matmul(banks[0:n, 4 + j % 4, :], h[:, u, t0:t0 + n],
                                                    w[:, u, (j % 2) * 512:(j % 2 + 1) * 512],
                                                    start=(u == 0 and part == 0), stop=(u == 1 and part == 2))
                        if u == 1:
                            last.then_inc(s["d_psum"], 1)


def kernel(**inputs):
    import numpy as np
    import concourse.bacc as bacc
    from concourse.bass_utils import run_bass_kernel_spmd

    nc = bacc.Bacc("TRN2", target_bir_lowering=False, num_devices=1)
    arrays, ins = {}, {}
    for name, a in inputs.items():
        arrays[f"in_{name}"] = np.ascontiguousarray(a)
        ins[name] = nc.dram_tensor(f"in_{name}", a.shape, mybir.dt.from_np(arrays[f"in_{name}"].dtype),
                                   kind="ExternalInput").ap()
    out = nc.dram_tensor("out_0", (1, SEQ, D), F32, kind="ExternalOutput").ap()
    build(nc, ins, out)
    r = run_bass_kernel_spmd(nc, [arrays], core_ids=[0])
    return r.results[0]["out_0"]
```

```python
from contextlib import ExitStack, contextmanager

import concourse.bass as bass
from concourse import mybir

F32 = mybir.dt.float32
F32R = mybir.dt.float32r
I32 = mybir.dt.int32
U8 = mybir.dt.uint8
ALU = mybir.AluOpType
ACT = mybir.ActivationFunctionType

P = 128
D = 1024
DC = D // P
SEQ = 1024
N_META = 16
L = SEQ + N_META
A_HEADS = 8
HD = 64
A_WIDTH = A_HEADS * HD
Q_RANK = 256
QC = Q_RANK // P
IDX_HEADS = 16
IDX_WIDTH = IDX_HEADS * HD
TOPK = 256
D_FF = 2816
FF_TILES = D_FF // P
DEPTH = 2
ALPHA = (2 * DEPTH) ** 0.25
LN_EPS = 1e-5
POOL_WINDOWS = (2, 4, 8, 16)
PG = D // len(POOL_WINDOWS)

COL_CQ, COL_KA, COL_VA = 0, Q_RANK, Q_RANK + A_WIDTH
COL_KI = COL_VA + A_WIDTH
COL_WI = COL_KI + HD
COL_QB = COL_WI + IDX_HEADS
COL_ZF, COL_IB, COL_GB = COL_QB + A_WIDTH, COL_QB + 2 * A_WIDTH, COL_QB + 3 * A_WIDTH

TILES = [(0, N_META)] + [(N_META + P * i, P) for i in range(SEQ // P)]
NT = len(TILES)
CHUNKS3 = [(0, 352), (352, 344), (696, 344)]
NKEYS = [t0 + n for t0, n in TILES]
SC_OFF = [sum(NKEYS[:m]) for m in range(NT)]
SC_COLS = sum(NKEYS)
FIRST_TOPK = 2
MASKED = -1.0e30
TAKEN = -3.0e38
TAKEN_BELOW = -2.0e38


def key_chunks(n):
    k = -(-n // 512)
    w = -(-n // k // 8) * 8
    return [(a, min(w, n - a)) for a in range(0, n, w)]


def build(nc, ins, out):
    x, meta, w_in = ins["x"][0], ins["meta_tokens"], ins["w_in"][0]
    w_in_v = w_in.rearrange("(k p) f -> p k f", p=P)

    with ExitStack() as top:
        sems = []

        def sem(name):
            sems.append(nc.alloc_semaphore(name=name))
            return sems[-1]

        @contextmanager
        def stage():
            with ExitStack() as c:
                yield c
            nc.clear_and_free_semaphores(sems)
            nc.all_engine_barrier()
            sems.clear()

        def sb(ctx, name, shape, dt=F32):
            return ctx.enter_context(nc.sbuf_tensor(name, shape, dt))

        qz_dram = nc.dram_tensor("qz_scratch", [2, 4, P, L], F32, kind="Internal").ap()
        vg_dram = nc.dram_tensor("vg_scratch", [2, L, A_WIDTH], F32, kind="Internal").ap()

        banks = top.enter_context(nc.psum_tensor("banks", [P, 8, 512], F32))
        ident = sb(top, "ident", [P, P])

        with ExitStack() as heads:
            with ExitStack() as mixer:
                score = sb(mixer, "score", [P, SC_COLS])
                cqT = sb(mixer, "cqT", [P, QC, L])
                kaT = sb(mixer, "kaT", [P, 4, L])
                va = sb(mixer, "va", [P, NT, A_WIDTH])
                with stage() as c:
                    projection(nc, c, sem, sb, banks, ident, x, meta, w_in_v, ins, score, cqT, kaT, va, qz_dram, vg_dram)
                oT = heads.enter_context(nc.sbuf_tensor("oT", [P, DC, L], F32, side="right"))
                with stage() as c:
                    mixers(nc, c, sem, sb, banks, ident, ins, score, cqT, kaT, va, oT, qz_dram, vg_dram)
            y = sb(top, "y", [P, NT, D])
            hH = sb(top, "hH", [P, DC, L], F32R)
            hL = sb(top, "hL", [P, DC, L], F32R)
            with stage() as c:
                out_projection(nc, c, sem, sb, banks, ident, x, meta, ins, oT, y, hH, hL)
        with stage() as c:
            ffn(nc, c, sem, sb, banks, ident, "f0", y, hH, hL, list(range(NT)), CHUNKS3,
                ins["w_gate"][0], ins["w_up"][0], ins["w_down"][0])
        with stage() as c:
            pool_mixer(nc, c, sem, sb, banks, ident, ins, y, hH, hL)
        with stage() as c:
            ffn(nc, c, sem, sb, banks, ident, "f1", y, hH, hL, list(range(1, NT)), [(N_META, 512), (N_META + 512, 512)],
                ins["w_gate"][1], ins["w_up"][1], ins["w_down"][1], final=(ins["ln_ffn_g"][1], ins["ln_ffn_b"][1], out))


def projection(nc, c, sem, sb, banks, ident, x, meta, w_in_v, ins, score, cqT, kaT, va, qz_dram, vg_dram):
    NX = 3
    IC = Q_RANK + HD + IDX_HEADS
    CK = Q_RANK + 2 * HD
    SW = 256
    xt = va[:, :, :].rearrange("p m f -> p (m f)")[:, 0:NX * D].rearrange("p (s d) -> p s d", s=NX)
    cqk = kaT[:, :, :].rearrange("p f t -> p (f t)")[:, 0:NT * CK].rearrange("p (m f) -> p m f", m=NT)
    w_idx = score[:, SC_OFF[FIRST_TOPK]:SC_OFF[FIRST_TOPK] + DC * IC].rearrange("p (k f) -> p k f", k=DC)
    hH = sb(c, "hH0", [P, DC, L], F32R)
    hL = sb(c, "hL0", [P, DC, L], F32R)
    SLAB = DC * SW
    shared = sb(c, "shared", [P, 3 * SLAB], F32R)
    w_idxH, w_idxL = (shared[:, i * DC * IC:(i + 1) * DC * IC].rearrange("p (k f) -> p k f", k=DC) for i in range(2))
    with ExitStack() as first:
        w_qi = sb(first, "w_qi", [P, QC, IDX_WIDTH])
        qiT = sb(first, "qiT", [P, 2, IDX_HEADS, P], F32R)
    slab1L = sb(c, "slab1L", [P, DC, SW], F32R)
    slab = sb(c, "slab", [P, 2, DC, SW])
    slab0H, slab0L, slab1H = (shared[:, i * SLAB:(i + 1) * SLAB].rearrange("p (k f) -> p k f", k=DC) for i in range(3))
    slabH, slabL = (slab0H, slab1H), (slab0L, slab1L[:, :, :])
    slab_first = va[:, :, :].rearrange("p m f -> p (m f)")[:, 0:2 * SLAB].rearrange("p (s k f) -> p s k f", s=2, k=DC)

    def slab_raw(j):
        return slab_first[:, j, :, :] if j < 2 else slab[:, j % 2, :, :]

    cq_gain = sb(c, "cq_gain_sb", [P, QC])
    ki_gb = sb(c, "ki_gb", [P, 2])
    squares = sb(c, "squares", [P, Q_RANK])
    wi = sb(c, "wi", [P, NT, IDX_HEADS])
    bn6 = sb(c, "bn6", [P, NT, 6])
    var = sb(c, "var", [P, NT, 2])
    sumsq = sb(c, "sumsq", [P, NT, 1])
    std = sb(c, "std_p", [P, NT, 2])
    rstd = sb(c, "rstd_p", [P, NT, 2])
    mv = sb(c, "mv_p", [P, NT, 2])
    kiT = sb(c, "kiT", [P, 2, P])
    kiH = sb(c, "kiH", [P, L], F32R)
    kiL = sb(c, "kiL", [P, L], F32R)
    qi_raw = sb(c, "qi_raw", [P, 2, 4, P])
    NR = 4
    relu = sb(c, "relu", [P, NR, 512])
    top8 = sb(c, "top8", [P, NT, 8])
    mark = sb(c, "round_mark", [P, 2])
    NS = NR
    stage = relu

    s_x = [sem(f"x_loaded{i}") for i in range(NX)]
    w_loaded, w_qi_loaded, small_loaded = sem("w_loaded"), sem("w_qi_loaded"), sem("small_loaded")
    slab_loaded = [sem("slab_loaded0"), sem("slab_loaded1")]
    ident_zero, ident_done = sem("ident_zero"), sem("ident_done")
    x_transposed, hT_act, hT_dve = sem("x_transposed"), sem("hT_act"), sem("hT_dve")
    idx_psum, idx_act, idx_dve = sem("idx_psum"), sem("idx_act"), sem("idx_dve")
    stats, std_done, normed = sem("stats"), sem("std_done"), sem("normed")
    cq_psum, cqT_done = sem("cq_psum"), sem("cqT_done")
    qi_psum, qi_done = sem("qi_psum"), sem("qi_done")
    ki_raw, qi_lo = sem("ki_raw"), sem("qi_lo")
    sc_psum, relu_done, acc_done = sem("sc_psum"), sem("relu_done"), sem("acc_done")
    causal_done, topk_step, mask_done, mask_all = sem("causal_done"), sem("topk_step"), sem("mask_done"), sem("mask_all")
    slab_psum, slab_out, slab_hi, slab_lo = sem("slab_psum"), sem("slab_out"), sem("slab_hi"), sem("slab_lo")
    idx_hi, idx_lo = sem("w_idx_hi"), sem("w_idx_lo")
    stored = [sem(f"stored{i}") for i in range(NS)]
    link = sem("dve_link")

    SLABS = [(col + SW * half, fm, dest, half) for col, fm, dest in (
        (COL_KA, True, "ka"), (COL_VA, False, "va"), (COL_ZF, True, 1), (COL_QB, True, 0), (COL_IB, False, 0),
        (COL_GB, False, 1)) for half in range(512 // SW)]
    slab_units = []
    for j, (_, fm, dest, half) in enumerate(SLABS):
        if fm:
            slab_units += [(j, fm, dest, ft, a, n) for ft in range(SW // P) for a, n in CHUNKS3]
        else:
            slab_units += [(j, fm, dest, m, *TILES[m]) for m in range(NT)]
    last_unit = {j: max(i for i, u in enumerate(slab_units) if u[0] == j) for j in range(len(SLABS))}

    TM = list(range(FIRST_TOPK, NT))
    EARLY = TM[:-1]
    NQ = len(TM)
    nth_q = {m: i for i, m in enumerate(TM)}
    units = [(m, h, a, n) for m in TM for h in range(IDX_HEADS) for a, n in key_chunks(NKEYS[m])]
    last_of_tile = {m: max(i for i, u in enumerate(units) if u[0] == m) for m in TM}

    order, PARTS = [], 5

    def take(what, m, first=0, *rest):
        if first <= m < NT:
            order.append((what, m, *rest))

    for T in range(NT + 3):
        if T == NT + 2:
            order += [("split", 0), ("split", 1)]
        take("cq", T - 2)
        take("sc", T - 3, FIRST_TOPK, 0)
        take("x", T)
        take("sc", T - 3, FIRST_TOPK, 1)
        take("idx", T - 1)
        take("sc", T - 3, FIRST_TOPK, 2)
        take("stats", T - 1)
        take("qi", T - 2, FIRST_TOPK, 0)
        take("norm", T - 1)
        take("sc", T - 3, FIRST_TOPK, 3)
        take("qi", T - 2, FIRST_TOPK, 1)
        take("sc", T - 3, FIRST_TOPK, 4)

    def units_of(m, part):
        mine = [i for i, u in enumerate(units) if u[0] == m]
        return mine[len(mine) * part // PARTS:len(mine) * (part + 1) // PARTS]

    SB = 4

    def score_bank(n):
        return 4 + n % SB

    block = c.enter_context(nc.Block())

    @block.sync
    def _(sp):
        for m, (t0, n) in enumerate(TILES):
            if m >= NX:
                sp.wait_ge(x_transposed, m - NX + 1)
            src = meta if m == 0 else x[t0 - N_META:t0 - N_META + n, :]
            sp.dma_start(xt[0:n, m % NX, :], src).then_inc(s_x[m % NX], 16)
            if m == 0:
                sp.dma_start(w_idx[:, :, 0:Q_RANK], w_in_v[:, :, 0:Q_RANK]).then_inc(w_loaded, 16)
                sp.dma_start(w_idx[:, :, Q_RANK:IC], w_in_v[:, :, COL_KI:COL_QB]).then_inc(w_loaded, 16)
            if m == 2:
                for k in range(QC):
                    sp.dma_start(cq_gain[:, k:k + 1],
                                 ins["cq_gain"][0, k * P:(k + 1) * P].rearrange("(p a) -> p a", a=1))\
                      .then_inc(small_loaded, 16)
                for b in range(2):
                    for i, name in enumerate(("kidx_gain", "kidx_bias")):
                        sp.dma_start(ki_gb[HD * b:HD * (b + 1), i:i + 1], ins[name][0].rearrange("(p a) -> p a", a=1))\
                          .then_inc(small_loaded, 16)
                sp.dma_start(w_qi[:, :, :], ins["w_uq_idx"][0].rearrange("(k p) f -> p k f", p=P)).then_inc(w_qi_loaded, 16)
        for j, (col, _, _, _) in enumerate(SLABS):
            if j == 0:
                sp.wait_ge(x_transposed, NT)
            elif j == 2:
                sp.wait_ge(sc_psum, len(units))
            elif j >= 4:
                sp.wait_ge(slab_hi, j - 1)
                sp.wait_ge(slab_lo, j - 1)
            sp.dma_start(slab_raw(j), w_in_v[:, :, col:col + SW]).then_inc(slab_loaded[j % 2], 16)

    @block.gpsimd
    def _(pool):
        nc.gpsimd.memset(ident[:, :], 0.0).then_inc(ident_zero, 1)
        pool.wait_ge(ident_zero, 1)
        nc.gpsimd.affine_select(out=ident[:, :], in_=ident[:, :], compare_op=ALU.not_equal, fill=1.0, base=0,
                                pattern=[[-1, P]], channel_multiplier=1).then_inc(ident_done, 1)
        nc.gpsimd.memset(score[:, 0:SC_OFF[FIRST_TOPK]], 0.0).then_inc(ident_zero, 1)
        pool.wait_ge(ident_zero, 2)

        def causal(m, signal):
            n = TILES[m][1]
            at = score[0:n, SC_OFF[m] + NKEYS[m] - n:SC_OFF[m] + NKEYS[m]]
            nc.gpsimd.affine_select(out=at, in_=at, compare_op=ALU.is_ge, fill=MASKED, base=0, pattern=[[-1, n]],
                                    channel_multiplier=1).then_inc(signal, 1)

        for m in range(FIRST_TOPK):
            causal(m, mask_all)
        pool.wait_ge(idx_hi, 1)
        nc.gpsimd.tensor_tensor(w_idxL[:, 0:DC // 2, :], w_idx[:, 0:DC // 2, :], w_idxH[:, 0:DC // 2, :].bitcast(F32),
                                ALU.subtract).then_inc(idx_lo, 1)
        pool.wait_ge(idx_lo, 2)
        pool.wait_ge(mask_all, FIRST_TOPK)

        def split(j):
            pool.wait_ge(slab_hi, j + 1)
            if j >= 2:
                pool.wait_ge(slab_psum, last_unit[j - 2] + 1)
            else:
                pool.wait_ge(qi_psum, 2 * NQ)
            nc.gpsimd.tensor_tensor(slabL[j % 2], slab_raw(j), slabH[j % 2].bitcast(F32), ALU.subtract).then_inc(slab_lo, 1)

        for what, m, *part in order:
            if what == "qi":
                half = part[0]
                nqi = 2 * nth_q[m] + half
                pool.wait_ge(qi_done, nqi + 1)
                hi = qiT[:, m % 2, 8 * half:8 * half + 8, :].rearrange("p (f two) t -> p two f t", two=2)
                for b in range(2):
                    r, other = slice(HD * b, HD * (b + 1)), slice(HD * (1 - b), HD * (2 - b))
                    nc.gpsimd.tensor_tensor(hi[other, b], qi_raw[r, half], hi[r, b].bitcast(F32), ALU.subtract)\
                      .then_inc(qi_lo, 1)
                    pool.wait_ge(qi_lo, 2 * nqi + b + 1)
            elif what == "sc" and part[0] == PARTS - 1:
                pool.wait_ge(acc_done, last_of_tile[m] + 1)
                causal(m, causal_done)
                pool.wait_ge(causal_done, nth_q[m] + 1)
            elif what == "split":
                split(m)
        for j in range(2, len(SLABS)):
            split(j)
        for i, m in enumerate(EARLY):
            pool.wait_ge(mask_done, i + 1)
            causal(m, mask_all)
        pool.wait_ge(mask_all, FIRST_TOPK + len(EARLY))
        pool.wait_ge(causal_done, len(TM))

    @block.tensor
    def _(pe):
        pe.wait_ge(ident_done, 1)
        for what, m, *part in order:
            if what == "split":
                continue
            t0, n = TILES[m]
            if what == "x":
                pe.wait_ge(s_x[m % NX], 16 * (m // NX + 1))
                if m:
                    pe.wait_ge(hT_dve, m)
                if m - 3 >= FIRST_TOPK:
                    pe.wait_ge(qi_done, 2 * nth_q[m - 3] + 2)
                for k in range(DC):
                    last = nc.tensor.transpose(banks[:, k // 4, (k % 4) * P:(k % 4) * P + n],
                                               xt[0:n, m % NX, k * P:(k + 1) * P], ident[0:n, 0:n])
                last.then_inc(x_transposed, 1)
            if what == "idx":
                if m == 0:
                    pe.wait_ge(idx_lo, 2)
                pe.wait_ge(hT_dve, m + 1)
                if m:
                    pe.wait_ge(idx_dve, m)
                for k in range(DC):
                    for part, (h, w) in enumerate(((hL, w_idxH), (hH, w_idxL), (hH, w_idxH))):
                        last = nc.tensor.matmul(banks[0:n, 2, 0:IC], h[:, k, t0:t0 + n], w[:, k, :],
                                                start=(k == 0 and part == 0), stop=(k == DC - 1 and part == 2))
                last.then_inc(idx_psum, 1)
            if what == "cq":
                pe.wait_ge(normed, m + 1)
                if m:
                    pe.wait_ge(cqT_done, m)
                for j in range(3):
                    last = nc.tensor.transpose(banks[:, 3, j * P:j * P + n], cqk[0:n, m, j * P:(j + 1) * P],
                                               ident[0:n, 0:n])
                last.then_inc(cq_psum, 1)
            if what == "qi":
                half = part[0]
                nqi = 2 * nth_q[m] + half
                if nqi == 0:
                    pe.wait_ge(w_qi_loaded, 16)
                pe.wait_ge(cqT_done, m + 1)
                pe.wait_ge(hT_dve, min(m + 3, NT))
                if nqi >= 2:
                    pe.wait_ge(qi_done, nqi - 1)
                for f in range(4):
                    ft = 4 * half + f
                    for k in range(QC):
                        last = nc.tensor.matmul(banks[:, half, f * P:(f + 1) * P],
                                                w_qi[:, k, ft * P:(ft + 1) * P], cqT[:, k, t0:t0 + n],
                                                start=(k == 0), stop=(k == QC - 1))
                last.then_inc(qi_psum, 1)
            if what == "sc":
                pe.wait_ge(qi_lo, 4 * nth_q[m] + 4)
                for i in units_of(m, part[0]):
                    _, h, k0, kn = units[i]
                    if i >= SB:
                        pe.wait_ge(relu_done, i - SB + 1)
                    nc.tensor.matmul(banks[:, score_bank(i), 0:kn], qiT[:, m % 2, h, :], kiL[:, k0:k0 + kn],
                                     start=True, stop=False)
                    nc.tensor.matmul(banks[:, score_bank(i), 0:kn], qiT[:, m % 2, h, :], kiH[:, k0:k0 + kn],
                                     start=False, stop=True).then_inc(sc_psum, 1)
        pe.wait_ge(relu_done, len(units))
        for i, (j, fm, dest, idx, a, n) in enumerate(slab_units):
            pe.wait_ge(slab_lo, j + 1)
            if i >= 8:
                pe.wait_ge(slab_out, i - 7)
            H, Lo = slabH[j % 2], slabL[j % 2]
            for k in range(DC):
                for part, (h, w) in enumerate(((hL, H), (hH, Lo), (hH, H))):
                    first, stop = k == 0 and part == 0, k == DC - 1 and part == 2
                    if fm:
                        last = nc.tensor.matmul(banks[:, i % 8, 0:n], w[:, k, idx * P:(idx + 1) * P], h[:, k, a:a + n],
                                                start=first, stop=stop)
                    else:
                        last = nc.tensor.matmul(banks[0:n, i % 8, 0:SW], h[:, k, a:a + n], w[:, k, :],
                                                start=first, stop=stop)
            last.then_inc(slab_psum, 1)

    @block.scalar
    def _(act):
        def split(j):
            act.wait_ge(slab_loaded[j % 2], 16 * (j // 2 + 1))
            if j >= 2:
                act.wait_ge(slab_psum, last_unit[j - 2] + 1)
            else:
                act.wait_ge(idx_psum, NT)
            nc.scalar.activation(slabH[j % 2], slab_raw(j), ACT.Copy).then_inc(slab_hi, 1)

        for what, m, *part in order:
            if what == "split":
                split(m)
                continue
            t0, n = TILES[m]
            if what == "x":
                act.wait_ge(x_transposed, m + 1)
                for half in range(2):
                    src = banks[:, half, :].rearrange("p (k t) -> p k t", k=4)[:, :, 0:n]
                    last = nc.scalar.activation(hH[:, 4 * half:4 * half + 4, t0:t0 + n], src, ACT.Copy)
                last.then_inc(hT_act, 1)
                if m == 0:
                    act.wait_ge(w_loaded, 32)
                    nc.scalar.activation(w_idxH, w_idx, ACT.Copy).then_inc(idx_hi, 1)
            if what == "idx":
                if m == 0:
                    act.wait_ge(link, 1)
                act.wait_ge(idx_dve, m + 1)
                if m:
                    act.wait_ge(idx_act, m)
                nc.scalar.activation(squares[0:n, :], cqk[0:n, m, 0:Q_RANK], ACT.Square,
                                     accum_out=sumsq[0:n, m, :]).then_inc(idx_act, 1)
            if what == "stats":
                act.wait_ge(stats, m + 1)
                nc.scalar.activation(std[:, m, :], var[:, m, :], ACT.Sqrt).then_inc(std_done, 1)
            if what == "qi":
                half = part[0]
                nqi = 2 * nth_q[m] + half
                act.wait_ge(qi_psum, nqi + 1)
                src = banks[:, half, :].rearrange("p (f t) -> p f t", f=4)
                hi = qiT[:, m % 2, 8 * half:8 * half + 8, :].rearrange("p (f two) t -> p two f t", two=2)
                if nqi >= 2:
                    act.wait_ge(qi_lo, 2 * (nqi - 1))
                for b in range(2):
                    r = slice(HD * b, HD * (b + 1))
                    nc.scalar.activation(hi[r, b], src[r], ACT.Copy)
                nc.scalar.activation(qi_raw[:, half, :, :], src, ACT.Copy).then_inc(qi_done, 1)
            if what == "sc":
                for i in units_of(m, part[0]):
                    kn = units[i][3]
                    act.wait_ge(sc_psum, i + 1)
                    if i >= NR:
                        act.wait_ge(acc_done, i - NR + 1)
                    nc.scalar.activation(relu[:, i % NR, 0:kn], banks[:, score_bank(i), 0:kn], ACT.Relu)\
                      .then_inc(relu_done, 1)
        act.wait_ge(acc_done, len(units))
        staged = 0
        for i, (j, fm, dest, idx, a, n) in enumerate(slab_units):
            half = SLABS[j][3]
            act.wait_ge(slab_psum, i + 1)
            if dest == "ka":
                nc.scalar.activation(kaT[:, half * SW // P + idx, a:a + n], banks[:, i % 8, 0:n], ACT.Copy)\
                  .then_inc(slab_out, 1)
            elif dest == "va":
                nc.scalar.activation(va[0:n, idx, half * SW:(half + 1) * SW], banks[0:n, i % 8, 0:SW], ACT.Copy)\
                  .then_inc(slab_out, 1)
            else:
                s = staged % NS
                if staged >= NS:
                    act.wait_ge(stored[s], 16 * (staged // NS))
                if fm:
                    src, dst, to = (banks[:, i % 8, 0:n], stage[:, s, 0:n],
                                    qz_dram[dest, half * SW // P + idx, :, a:a + n])
                else:
                    src, dst, to = (banks[0:n, i % 8, 0:SW], stage[0:n, s, 0:SW],
                                    vg_dram[dest, a:a + n, half * SW:(half + 1) * SW])
                nc.scalar.activation(dst, src, ACT.Silu if (not fm and dest == 1) else ACT.Copy).then_inc(slab_out, 1)
                act.wait_ge(slab_out, i + 1)
                act.dma_start(to, dst).then_inc(stored[s], 16)
                staged += 1
            if i == last_unit[j] and j + 2 < len(SLABS):
                split(j + 2)
        for s in range(NS):
            act.wait_ge(stored[s], 16 * ((staged - s + NS - 1) // NS))

    @block.vector
    def _(dve):
        chain = [0]

        def linked(ins_):
            chain[0] += 1
            ins_.then_inc(link, 1)
            dve.wait_ge(link, chain[0])

        linked(nc.vector.memset(sumsq[:, :, :], 1.0))
        linked(nc.vector.memset(var[:, :, :], 1.0))
        linked(nc.vector.memset(mv[:, :, :], 1.0))
        for what, m, *part in order:
            if what == "split":
                continue
            t0, n = TILES[m]
            if what == "x":
                dve.wait_ge(hT_act, m + 1)
                for half in range(2):
                    src = banks[:, half, :].rearrange("p (k t) -> p k t", k=4)[:, :, 0:n]
                    at = slice(4 * half, 4 * half + 4)
                    last = nc.vector.tensor_tensor(hL[:, at, t0:t0 + n], src, hH[:, at, t0:t0 + n].bitcast(F32),
                                                   ALU.subtract)
                last.then_inc(hT_dve, 1)
                if m == 0:
                    dve.wait_ge(idx_hi, 1)
                    at = slice(DC // 2, DC)
                    nc.vector.tensor_tensor(w_idxL[:, at, :], w_idx[:, at, :], w_idxH[:, at, :].bitcast(F32),
                                            ALU.subtract).then_inc(idx_lo, 1)
            if what == "idx":
                dve.wait_ge(idx_psum, m + 1)
                bank = banks[0:n, 2, :]
                nc.vector.tensor_copy(cqk[0:n, m, 0:Q_RANK + HD], bank[:, 0:Q_RANK + HD])
                nc.vector.bn_stats(bn6[0:n, m, :], bank[:, Q_RANK:Q_RANK + HD])
                nc.vector.tensor_scalar(wi[0:n, m, :], bank[:, Q_RANK + HD:IC], IDX_HEADS ** -0.5 * HD ** -0.5, None,
                                        ALU.mult).then_inc(idx_dve, 1)
            if what == "stats":
                dve.wait_ge(idx_dve, m + 1)
                linked(nc.vector.bn_aggr(mv[0:n, m, :], bn6[0:n, m, :]))
                dve.wait_ge(idx_act, m + 1)
                linked(nc.vector.tensor_scalar(var[:, m, 0:1], sumsq[:, m, :], 1.0 / Q_RANK, LN_EPS, ALU.mult, ALU.add))
                nc.vector.tensor_scalar(var[:, m, 1:2], mv[:, m, 1:2], LN_EPS, None, ALU.add).then_inc(stats, 1)
            if what == "norm":
                dve.wait_ge(std_done, m + 1)
                linked(nc.vector.reciprocal(rstd[:, m, :], std[:, m, :]))
                k0 = Q_RANK
                nc.vector.tensor_scalar(cqk[0:n, m, k0 + HD:k0 + 2 * HD], cqk[0:n, m, k0:k0 + HD], mv[0:n, m, 0:1],
                                        rstd[0:n, m, 1:2], ALU.subtract, ALU.mult)
                linked(nc.vector.tensor_scalar(cqk[0:n, m, 0:k0], cqk[0:n, m, 0:k0], rstd[0:n, m, 0:1], None, ALU.mult))
                nc.vector.tensor_scalar(cqk[0:n, m, k0:k0 + HD], cqk[0:n, m, k0:k0 + HD], mv[0:n, m, 0:1],
                                        rstd[0:n, m, 1:2], ALU.subtract, ALU.mult).then_inc(normed, 1)
            if what == "cq":
                if m == 0:
                    dve.wait_ge(small_loaded, 16 * (QC + 4))
                dve.wait_ge(cq_psum, m + 1)
                bank = banks[:, 3, :]
                for k in range(QC):
                    nc.vector.tensor_scalar(cqT[:, k, t0:t0 + n], bank[:, k * P:k * P + n], cq_gain[:, k:k + 1], None,
                                            ALU.mult)
                raw = kiT[:, m % 2, 0:n]
                nc.vector.tensor_scalar(raw, bank[:, QC * P:QC * P + n], ki_gb[:, 0:1], ki_gb[:, 1:2],
                                        ALU.mult, ALU.add).then_inc(ki_raw, 1)
                dve.wait_ge(ki_raw, 2 * m + 1)
                nc.vector.tensor_copy(kiH[:, t0:t0 + n], raw).then_inc(ki_raw, 1)
                dve.wait_ge(ki_raw, 2 * m + 2)
                nc.vector.tensor_tensor(kiL[:, t0:t0 + n], raw, kiH[:, t0:t0 + n].bitcast(F32), ALU.subtract)\
                  .then_inc(cqT_done, 1)
            if what == "sc":
                for i in units_of(m, part[0]):
                    _, h, a, kn = units[i]
                    dve.wait_ge(relu_done, i + 1)
                    at = score[:, SC_OFF[m] + a:SC_OFF[m] + a + kn]
                    if i == 0:
                        dve.wait_ge(idx_lo, 2)
                    if h == 0:
                        nc.vector.tensor_scalar(at, relu[:, i % NR, 0:kn], wi[:, m, h:h + 1], None, ALU.mult)\
                          .then_inc(acc_done, 1)
                    else:
                        dve.wait_ge(acc_done, i - len(key_chunks(NKEYS[m])) + 1)
                        nc.vector.scalar_tensor_tensor(out=at, in0=relu[:, i % NR, 0:kn], scalar=wi[:, m, h:h + 1],
                                                       in1=at, op0=ALU.mult, op1=ALU.add).then_inc(acc_done, 1)
        NM = len(EARLY)
        FREE = 1
        dve.wait_ge(causal_done, NM)
        dve.sem_inc(topk_step, FREE)
        with dve.Fori(0, TOPK // 8) as r:
            for i, m in enumerate(EARLY):
                at = score[:, SC_OFF[m]:SC_OFF[m] + NKEYS[m]]
                if i == 0:
                    dve.wait_ge(topk_step, FREE + r * (2 * NM))
                    nc.vector.memset(mark[:, 0:1], 0.0)
                nc.vector.max(top8[:, m, :], at).then_inc(topk_step, 1)
            for i, m in enumerate(EARLY):
                at = score[:, SC_OFF[m]:SC_OFF[m] + NKEYS[m]]
                if i == 0:
                    dve.wait_ge(topk_step, FREE + r * (2 * NM) + NM)
                    nc.vector.memset(mark[:, 1:2], 0.0)
                nc.vector.match_replace(at, top8[:, m, :], at, TAKEN).then_inc(topk_step, 1)
        dve.wait_ge(topk_step, FREE + TOPK // 8 * 2 * NM)
        for m in EARLY:
            at = score[:, SC_OFF[m]:SC_OFF[m] + NKEYS[m]]
            nc.vector.tensor_scalar(at, at, TAKEN_BELOW, MASKED, ALU.is_ge, ALU.mult).then_inc(mask_done, 1)


def mixers(nc, c, sem, sb, banks, ident, ins, score, cqT, kaT, va, oT, qz_dram, vg_dram):
    W = 4 * P
    PAD_Z = 80.0
    LEVELS = 7
    STEPS = LEVELS + 1
    LOG0, T_LO, T_HI, PV, SHARED, GRAM = 0, 2, 3, 4, 5, 6
    PER_BANK = 4

    w_qa = sb(c, "w_qa", [P, QC, A_WIDTH])
    qaT = sb(c, "qaT", [P, 2, A_HEADS, P])
    probs = sb(c, "probs", [P, 2, L])
    pT = sb(c, "pT", [P, 2, NT, P])
    nmax = sb(c, "nmax", [P, 2, 3])
    sums = sb(c, "sums", [P, 2, A_HEADS])
    rsums = sb(c, "rsums", [P, 2, A_HEADS])
    o_tok = sb(c, "o_tok", [P, 2, A_WIDTH])
    REL0 = TILES[-1][0]
    rel_f, rel_i = probs[0:2, 0, :], probs[0:2, 1, :].bitcast(I32)
    rel = sb(c, "rel", [2, L], F32R)
    qpos_i = sb(c, "qpos_i", [2, P], I32)
    qpos = sb(c, "qpos", [2, P])
    alibi = sb(c, "alibi", [2, A_HEADS, P], F32R)
    zt = sb(c, "zt", [P, 2, W])
    qt = sb(c, "qt", [P, 2, W])
    vt = sb(c, "vt", [P, 2, A_WIDTH])
    gt = sb(c, "gt", [P, 2, A_WIDTH])
    u = sb(c, "u", [P, W])
    lnw = sb(c, "lnw", [P, W])
    key_arg = sb(c, "key_arg", [P, W])
    key = sb(c, "key", [P, 2, W])
    b = sb(c, "b", [P, 2, W])
    keep = sb(c, "keep", [P, W])
    ex = sb(c, "ex", [P, 2, W])
    xl = sb(c, "xl", [P, 2, W])
    xq = sb(c, "xq", [P, 2, W])
    eb = sb(c, "eb", [P, W])
    qe = sb(c, "qe", [P, 2, W])
    kd = sb(c, "kd", [P, W])
    elast = sb(c, "elast", [P, 2, 4])
    k_tok = eb
    added = sb(c, "state_added", [P, W])
    S = sb(c, "S", [P, 2, 8, P])
    state = sb(c, "state", [P, 4, P])
    it_s, it_t, xor, shifted, after = (xl[:, 0:2, :].rearrange("p a t -> p (a t)")[:, i * P:(i + 1) * P].bitcast(I32)
                                       for i in range(5))
    masks = sb(c, "masks", [P, STEPS, P], U8)
    gain = sb(c, "gain", [P, A_WIDTH])
    sq = key_arg
    on = sb(c, "on", [P, A_WIDTH])
    ssum = sb(c, "ssum", [P, 8])
    top8 = sb(c, "late_top8", [P, 8])
    rsh = sb(c, "rsh", [P, 8])

    w_loaded, iotas, rel_done, alibi_done = sem("wqa_loaded"), sem("iotas"), sem("rel_done"), sem("alibi_done")
    qk_done, qk_tail, nmax_raw, nmax_tail, nmax_done = (sem("qk_done"), sem("qk_tail"), sem("nmax_raw"),
                                                        sem("nmax_tail"), sem("nmax_done"))
    exp_done, t_psum, t_last, t_act, t_act_last, t_dve, pv_done = (sem("exp_done"), sem("t_psum"), sem("t_last"),
                                                                   sem("t_act"), sem("t_act_last"), sem("t_dve"), sem("pv_done"))
    rs_done, otok_done = sem("rs_done"), sem("otok_done")
    zq_loaded, vg_loaded = [sem("zq_loaded0"), sem("zq_loaded1")], [sem("vg_loaded0"), sem("vg_loaded1")]
    gain_loaded, pads, iota_done, gated = sem("gain_loaded"), sem("pads"), sem("iota_done"), sem("gated")
    vlink = sem("vector_link")
    abs_done, u_done, ln_done, key_in = sem("abs_done"), sem("u_done"), sem("ln_done"), sem("key_in")
    logf_done, b_done, key_done, kd_in, kd_done, eb_done, ke_done = (
        sem("logf_done"), sem("b_done"), sem("key_done"), sem("kd_in"), sem("kd_done"), sem("eb_done"),
        sem("ke_done"))
    ex_in, ex_out, x_done, gram_psum, gram_read = (sem("ex_in"), sem("ex_out"), sem("x_done"), sem("gram_psum"),
                                                   sem("gram_read"))
    state_done, sq_done, ssum_done, lnv_done, rsh_done, on_done = (
        sem("state_done"), sem("sq_done"), sem("ssum_done"), sem("lnv_done"), sem("rsh_done"), sem("on_done"))
    shared_psum, shared_done = sem("shared_psum"), sem("shared_done")
    x_part = sem("x_part")
    taken, late_mask, late_causal = sem("taken"), sem("late_mask"), sem("late_causal")

    units = [(m, h) for m in range(NT) for h in range(A_HEADS)]
    NU = len(units)
    steps = units + [(NT, h) for h in range(STEPS)]
    logits = banks[:, LOG0:LOG0 + 2, :].rearrange("p b t -> p (b t)")
    assert STEPS == A_HEADS and NKEYS[-2] <= 1024 < NKEYS[-1] and NT == 2 * PER_BANK + 1

    def shared_job(m, h):
        jobs = {1: ("out", m - 1), 2: ("kT", m), 3: ("state", m), 4: ("qa", m + 1), 5: ("ot_rec", m - 1),
                6: ("ot_att", m - 1)}
        return jobs[h] if h in jobs and 0 <= jobs[h][1] < NT else None

    shared = [("qa", 0)] + [j for j in (shared_job(*s) for s in steps) if j]
    nth = {j: i + 1 for i, j in enumerate(shared)}

    late = score[:, SC_OFF[NT - 1]:SC_OFF[NT - 1] + NKEYS[NT - 1]]
    ROUNDS = TOPK // 8
    LATE0, LATE1 = 1, NU - A_HEADS - 3
    late_rounds = {i: [r for r in range(ROUNDS) if LATE0 + r * (LATE1 - LATE0) // ROUNDS == i] for i in range(NU)}

    def levels_to(m, h):
        return m * LEVELS + h

    def dve_turns(i):
        return sum(m >= PER_BANK for m, _ in units[:i + 1])

    def tails(i):
        return sum(m == NT - 1 for m, _ in units[:i + 1])

    def halves(ap, l):
        return ap.rearrange("p (n two h) -> p n two h", two=2, h=2 ** l)

    def four(ap):
        return ap.rearrange("p (f t) -> p f t", f=4)

    block = c.enter_context(nc.Block())

    @block.sync
    def _(sp):
        sp.dma_start(w_qa[:, :, :], ins["w_uq"][0].rearrange("(k p) f -> p k f", p=P)).then_inc(w_loaded, 16)
        sp.dma_start(gain[:, :], ins["onorm_gain"][0:1, :].to_broadcast([P, A_WIDTH])).then_inc(gain_loaded, 16)
        sp.wait_ge(pads, 2)
        for m, (t0, n) in enumerate(TILES):
            s = m % 2
            r = slice(P - n, P)
            if m >= 2:
                sp.wait_ge(ke_done, m - 1)
                sp.wait_ge(x_done, levels_to(m - 2, LEVELS))
                sp.wait_ge(gram_psum, STEPS * (m - 2) + 1)
            for w, dst in ((1, zt), (0, qt)):
                sp.dma_start(four(dst[:, s, :])[:, :, r], qz_dram[w, :, :, t0:t0 + n].rearrange("f p t -> p f t"))\
                  .then_inc(zq_loaded[s], 16)
            if m >= 2:
                sp.wait_ge(shared_psum, nth["out", m - 2])
                sp.wait_ge(on_done, m - 1)
            if m == 0:
                sp.wait_ge(pads, 4)
            for w, dst in ((0, vt), (1, gt)):
                sp.dma_start(dst[r, s, :], vg_dram[w, t0:t0 + n, :]).then_inc(vg_loaded[s], 16)

    @block.gpsimd
    def _(pool):
        nc.gpsimd.memset(zt[:, 0, :], PAD_Z).then_inc(pads, 1)
        nc.gpsimd.memset(qt[:, 0, :], 0.0).then_inc(pads, 1)
        nc.gpsimd.iota(it_s, pattern=[[0, P]], base=0, channel_multiplier=1).then_inc(iota_done, 1)
        nc.gpsimd.iota(it_t, pattern=[[1, P]], base=0, channel_multiplier=0).then_inc(iota_done, 1)
        nc.gpsimd.iota(rel_i, pattern=[[1, L]], base=-REL0, channel_multiplier=0).then_inc(iotas, 1)
        nc.gpsimd.iota(qpos_i[:, :], pattern=[[-1, P]], base=0, channel_multiplier=0).then_inc(iotas, 1)
        nc.gpsimd.memset(vt[:, 0, :], 0.0).then_inc(pads, 1)
        nc.gpsimd.memset(gt[:, 0, :], 0.0).then_inc(pads, 1)
        pool.wait_ge(iotas, 4)
        nc.gpsimd.affine_select(out=rel_f, in_=rel_f, compare_op=ALU.is_ge, fill=1.0, base=0,
                                pattern=[[0, L]], channel_multiplier=-1).then_inc(rel_done, 1)
        nc.gpsimd.affine_select(out=qpos[:, :], in_=qpos[:, :], compare_op=ALU.is_gt, fill=1.0, base=0,
                                pattern=[[0, P]], channel_multiplier=1).then_inc(rel_done, 1)
        for dst in (qaT, xq, S, state):
            nc.gpsimd.memset(dst[:], 0.0).then_inc(pads, 1)
        pool.wait_ge(gain_loaded, 16)
        pool.wait_ge(pads, 8)

        def decayed(m, h):
            l, i = h - 1, levels_to(m, h) - 1
            pool.wait_ge(key_done, m + 1)
            pool.wait_ge(ex_out, i + 1)
            if i >= 2:
                pool.wait_ge(gram_psum, (i - 2) // LEVELS * STEPS + (i - 2) % LEVELS + 2)
            e, xo = halves(ex[:, i % 2, :], l), halves(xl[:, i % 2, :], l)
            nc.gpsimd.tensor_tensor(xo[:, :, 0, :], e[:, :, 0, :], halves(key[:, m % 2, :], l)[:, :, 0, :], ALU.mult)\
              .then_inc(x_part, 1)
            for par in range(2):
                r = slice(HD * par, HD * (par + 1))
                later = [a[r].rearrange("p (f n two t) -> p f n two t", f=4, two=2, t=2 ** l)[:, :, :, 1, :]
                         for a in (ex[:, i % 2, :], qt[:, m % 2, :])]
                to = xq[r, i % 2, :].rearrange("p (f two n t) -> p two f n t", f=4, two=2, t=2 ** l)[:, par]
                pool.wait_ge(x_part, 2 * i + par + 1)
                nc.gpsimd.tensor_tensor(to, later[0], later[1], ALU.mult).then_inc(x_done if par else x_part, 1)
            pool.wait_ge(x_done, i + 1)

        pool.wait_ge(zq_loaded[0], 32)
        decayed(0, 1)
        for i, (m, h) in enumerate(steps):
            if i + 2 < NU and steps[i + 2][1]:
                decayed(*steps[i + 2])
            if h == 0 and m < NT:
                pool.wait_ge(vg_loaded[m % 2], 32 * (m // 2 + 1))
                nc.gpsimd.tensor_tensor(gt[:, m % 2, :], gt[:, m % 2, :], gain[:, :], ALU.mult).then_inc(gated, 1)
            if i == LATE1 + 1:
                pool.wait_ge(late_mask, 1)
                nc.gpsimd.affine_select(out=late[:, NKEYS[-1] - P:NKEYS[-1]], in_=late[:, NKEYS[-1] - P:NKEYS[-1]],
                                        compare_op=ALU.is_ge, fill=MASKED, base=0, pattern=[[-1, P]],
                                        channel_multiplier=1).then_inc(late_causal, 1)
            if h == 2 and m:
                pool.wait_ge(shared_done, nth["out", m - 1])
                if m >= 2:
                    pool.wait_ge(ssum_done, 2 * (m - 1))
                pool.wait_ge(key_done, min(m + 1, NT))
                nc.gpsimd.tensor_tensor(sq[:, :], on[:, :], on[:, :], ALU.mult).then_inc(sq_done, 1)

    @block.tensor
    def _(pe):
        pe.wait_ge(w_loaded, 16)

        def on_shared(what, m):
            n_use = nth[what, m]
            if n_use > 1:
                pe.wait_ge(shared_done, n_use - 1)
            s = m % 2
            t0, n = TILES[m]
            if what == "qa":
                for ft in range(4):
                    for k in range(QC):
                        last = nc.tensor.matmul(banks[:, SHARED, ft * P:ft * P + n], w_qa[:, k, ft * P:(ft + 1) * P],
                                                cqT[:, k, t0:t0 + n], start=(k == 0), stop=(k == QC - 1))
            if what == "kT":
                pe.wait_ge(ke_done, m + 1)
                for f in range(4):
                    last = nc.tensor.transpose(banks[:, SHARED, f * P:(f + 1) * P], kd[:, f * P:(f + 1) * P], ident[:, :])
            if what == "state":
                pe.wait_ge(vg_loaded[s], 32 * (m // 2 + 1))
                for f in range(4):
                    last = nc.tensor.matmul(banks[:, SHARED, f * P:(f + 1) * P], k_tok[:, f * P:(f + 1) * P],
                                            vt[:, s, f * P:(f + 1) * P], start=True, stop=True)
            if what == "out":
                pe.wait_ge(gram_read, STEPS * (m + 1))
                if m:
                    pe.wait_ge(state_done, m)
                for f in range(4):
                    nc.tensor.matmul(banks[:, SHARED, f * P:(f + 1) * P], qe[:, s, f * P:(f + 1) * P], state[:, f, :],
                                     start=True, stop=False, skip_group_check=True)
                    for par in range(2):
                        h = 2 * f + par
                        last = nc.tensor.matmul(banks[:, SHARED, h * HD:(h + 1) * HD], S[:, s, h, :],
                                                vt[:, s, h * HD:(h + 1) * HD], start=False, stop=(par == 1),
                                                skip_group_check=True)
            if what == "ot_rec":
                pe.wait_ge(on_done, m + 1)
                for f in range(4):
                    last = nc.tensor.transpose(banks[:, SHARED, f * P:(f + 1) * P], on[:, f * P:(f + 1) * P], ident[:, :])
            if what == "ot_att":
                pe.wait_ge(otok_done, m + 1)
                for f in range(4):
                    last = nc.tensor.transpose(banks[:, SHARED, f * P:f * P + n], o_tok[0:n, s, f * P:(f + 1) * P],
                                               ident[0:n, 0:n])
            last.then_inc(shared_psum, 1)

        def scores_of(m, h, a, kn, at):
            t0, n = TILES[m]
            nc.tensor.matmul(logits[0:n, at:at + kn], alibi[:, h, 0:n], rel[:, REL0 - t0 + a:REL0 - t0 + a + kn],
                             start=True, stop=False)
            return nc.tensor.matmul(logits[0:n, at:at + kn], qaT[:, m % 2, h, 0:n], kaT[:, h // 2, a:a + kn],
                                    start=False, stop=True)

        def qk(i):
            m, h = units[i]
            if h == 0:
                pe.wait_ge(shared_done, nth["qa", m])
            if i == 0:
                pe.wait_ge(alibi_done, 1)
            if i:
                pe.wait_ge(nmax_raw, i)
                if tails(i - 1):
                    pe.wait_ge(nmax_tail, tails(i - 1))
            for a in range(0, min(NKEYS[m], 1024), 512):
                last = scores_of(m, h, a, min(512, NKEYS[m] - a), a)
            last.then_inc(qk_done, 1)

        def qk_rest(i):
            m, h = units[i]
            pe.wait_ge(nmax_raw, i + 1)
            scores_of(m, h, 1024, NKEYS[m] - 1024, 0).then_inc(qk_tail, 1)

        def gram(i):
            m, h = units[i]
            if i:
                pe.wait_ge(gram_read, i - 1 if h >= 2 else i)
            if h == 0:
                pe.wait_ge(key_done, m + 1)
                for f in range(4):
                    for par in range(2):
                        r, t = slice(HD * par, HD * (par + 1)), slice(f * P, (f + 1) * P)
                        last = nc.tensor.matmul(banks[:, GRAM + par, t], key[r, m % 2, t], qt[r, m % 2, t],
                                                start=True, stop=True)
            else:
                j = levels_to(m, h) - 1
                pe.wait_ge(x_done, j + 1)
                for f in range(4):
                    t = slice(f * P, (f + 1) * P)
                    last = nc.tensor.matmul(banks[:, GRAM + h % 2, t], xl[:, j % 2, t], xq[:, j % 2, t],
                                            start=True, stop=True)
            last.then_inc(gram_psum, 1)

        def turn(i):
            m, h = units[i]
            n = TILES[m][1]
            pe.wait_ge(exp_done, i + 1)
            if i:
                pe.wait_ge(t_act, i)
                if dve_turns(i - 1):
                    pe.wait_ge(t_dve, dve_turns(i - 1))
                if tails(i - 1):
                    pe.wait_ge(t_act_last, tails(i - 1))
            for j in range(min(m + 1, 2 * PER_BANK)):
                k0, kn = TILES[j]
                last = nc.tensor.transpose(banks[0:kn, T_LO + j // PER_BANK, j % PER_BANK * P:j % PER_BANK * P + n],
                                           probs[0:n, i % 2, k0:k0 + kn], ident[0:n, 0:n])
            last.then_inc(t_psum, 1)

        def turn_rest(i):
            m, h = units[i]
            k0, kn = TILES[m]
            pe.wait_ge(t_act, i + 1)
            nc.tensor.transpose(banks[0:kn, T_LO, 0:P], probs[:, i % 2, k0:k0 + kn], ident[:, :]).then_inc(t_last, 1)

        def pv(i):
            m, h = units[i]
            n = TILES[m][1]
            pe.wait_ge(t_act, i + 1)
            if m >= PER_BANK:
                pe.wait_ge(t_dve, dve_turns(i))
            if m == NT - 1:
                pe.wait_ge(t_act_last, tails(i))
            if h == 0 and m:
                pe.wait_ge(otok_done, m)
            for j in range(m + 1):
                kn = TILES[j][1]
                last = nc.tensor.matmul(banks[0:n, PV, h * HD:(h + 1) * HD], pT[0:kn, i % 2, j, 0:n],
                                        va[0:kn, j, h * HD:(h + 1) * HD], start=(j == 0), stop=(j == m))
            last.then_inc(pv_done, 1)

        on_shared("qa", 0)
        for i, (m, h) in enumerate(steps):
            if i < NU:
                qk(i)
                gram(i)
                if m == NT - 1:
                    qk_rest(i)
            if shared_job(m, h):
                on_shared(*shared_job(m, h))
            if 1 <= i <= NU:
                turn(i - 1)
            if 2 <= i <= NU + 1:
                pv(i - 2)
            if 1 <= i <= NU and units[i - 1][0] == NT - 1:
                turn_rest(i - 1)

    @block.scalar
    def _(act):
        act.preload_act_table_set("natural_log_exp_and_others")

        def exps(i):
            m, h = units[i]
            n = TILES[m][1]
            act.wait_ge(nmax_done, i + 1)
            if h == 0 and m >= 2:
                act.wait_ge(rs_done, m - 1)
            at = probs[0:n, i % 2, 0:NKEYS[m]]
            nc.scalar.activation(at, at, ACT.Exp, bias=nmax[0:n, i % 2, 2:3], accum_out=sums[0:n, m % 2, h:h + 1])\
              .then_inc(exp_done, 1)

        def turned(i):
            m, h = units[i]
            n = TILES[m][1]
            act.wait_ge(t_psum, i + 1)
            if i >= 2:
                act.wait_ge(pv_done, i - 1)
            last = nc.scalar.activation(pT[0:N_META, i % 2, 0, 0:n], banks[0:N_META, T_LO, 0:n], ACT.Copy)
            if m:
                k = min(PER_BANK - 1, m)
                last = nc.scalar.activation(pT[:, i % 2, 1:1 + k, 0:n],
                                            banks[:, T_LO, P:(1 + k) * P].rearrange("p (f t) -> p f t", f=k)[:, :, 0:n],
                                            ACT.Copy)
            last.then_inc(t_act, 1)

        def turned_rest(i):
            act.wait_ge(t_last, tails(i))
            nc.scalar.activation(pT[:, i % 2, NT - 1, :], banks[:, T_LO, 0:P], ACT.Copy).then_inc(t_act_last, 1)

        def level_exp(m, h):
            i = levels_to(m, h) - 1
            act.wait_ge(ex_in, i + 1)
            nc.scalar.activation(ex[:, i % 2, :], ex[:, i % 2, :], ACT.Exp).then_inc(ex_out, 1)

        def gates(m, stage):
            z = zt[:, m % 2, :]
            if stage == 2:
                act.wait_ge(zq_loaded[m % 2], 32 * (m // 2 + 1))
                if m:
                    act.wait_ge(ln_done, m)
                nc.scalar.activation(u[:, :], z, ACT.Abs).then_inc(abs_done, 1)
                act.wait_ge(abs_done, m + 1)
                nc.scalar.activation(u[:, :], u[:, :], ACT.Exp, scale=-1.0).then_inc(u_done, 1)
            if stage == 3:
                act.wait_ge(u_done, m + 1)
                if m:
                    act.wait_ge(b_done, m)
                nc.scalar.activation(lnw[:, :], u[:, :], ACT.Ln, bias=1.0).then_inc(ln_done, 1)
            if stage == 4:
                act.wait_ge(key_in, m + 1)
                if m >= 2:
                    act.wait_ge(gram_psum, STEPS * (m - 2) + 1)
                    act.wait_ge(x_done, levels_to(m - 2, LEVELS))
                    act.wait_ge(ke_done, m - 1)
                nc.scalar.activation(key[:, m % 2, :], key_arg[:, :], ACT.Exp, scale=-1.0).then_inc(key_done, 1)
            if stage == 5:
                act.wait_ge(kd_in, m + 1)
                nc.scalar.activation(kd[:, :], kd[:, :], ACT.Exp).then_inc(kd_done, 1)
                if m:
                    act.wait_ge(ke_done, m)
                nc.scalar.activation(eb[:, :], b[:, m % 2, :], ACT.Exp).then_inc(eb_done, 1)

        def off_shared(what, m):
            act.wait_ge(shared_psum, nth[what, m])
            t0, n = TILES[m]
            src = banks[:, SHARED, :]
            if what == "qa":
                if m == 0:
                    act.wait_ge(pads, 5)
                for par in range(2):
                    r = slice(HD * par, HD * (par + 1))
                    to = qaT[r, m % 2, :, 0:n].rearrange("p (f two) t -> p two f t", two=2)[:, par]
                    ins_ = nc.scalar.activation(to, four(src)[r, :, 0:n], ACT.Copy, scale=HD ** -0.5)
            if what == "kT":
                ins_ = nc.scalar.activation(k_tok[:, :], src, ACT.Copy)
            if what == "state":
                if m:
                    act.wait_ge(state_done, m)
                ins_ = nc.scalar.activation(added[:, :], src, ACT.Copy)
            if what == "out":
                ins_ = nc.scalar.activation(on[:, :], src, ACT.Copy)
            if what == "ot_rec":
                ins_ = nc.scalar.activation(oT[:, 4:8, t0:t0 + n], four(src)[:, :, P - n:P], ACT.Copy)
            if what == "ot_att":
                ins_ = nc.scalar.activation(oT[:, 0:4, t0:t0 + n], four(src)[:, :, 0:n], ACT.Copy)
            ins_.then_inc(shared_done, 1)

        off_shared("qa", 0)
        for stage in (2, 3, 4, 5):
            gates(0, stage)
        level_exp(0, 1)
        for i, (m, h) in enumerate(steps):
            if i < NU:
                exps(i)
            if i + 2 < NU and steps[i + 2][1]:
                level_exp(*steps[i + 2])
            if m + 1 < NT:
                gates(m + 1, h)
            if shared_job(m, h):
                off_shared(*shared_job(m, h))
            if 1 <= i <= NU:
                turned(i - 1)
                if units[i - 1][0] == NT - 1:
                    turned_rest(i - 1)
            if h == 3 and 1 <= m:
                act.wait_ge(ssum_done, 2 * m)
                nc.scalar.activation(rsh[:, :], ssum[:, :], ACT.Ln).then_inc(lnv_done, 1)
                act.wait_ge(lnv_done, m)
                nc.scalar.activation(rsh[:, :], rsh[:, :], ACT.Exp, scale=-0.5).then_inc(rsh_done, 1)

    @block.vector
    def _(dve):
        chain = [0]

        def linked(ins_):
            chain[0] += 1
            ins_.then_inc(vlink, 1)
            dve.wait_ge(vlink, chain[0])

        dve.wait_ge(iotas, 2)
        nc.vector.tensor_copy(rel_f, rel_i).then_inc(iotas, 1)
        nc.vector.tensor_copy(qpos[:, :], qpos_i[:, :]).then_inc(iotas, 1)
        dve.wait_ge(iota_done, 2)
        linked(nc.vector.tensor_tensor(xor, it_s, it_t, ALU.bitwise_xor))
        linked(nc.vector.tensor_tensor(after, it_t, it_s, ALU.is_gt))
        for l in range(LEVELS):
            linked(nc.vector.tensor_scalar(shifted, xor, l, None, ALU.logical_shift_right))
            linked(nc.vector.scalar_tensor_tensor(out=masks[:, l, :], in0=shifted, scalar=1.0, in1=after,
                                                  op0=ALU.is_equal, op1=ALU.mult))
        linked(nc.vector.tensor_scalar(masks[:, LEVELS, :], xor, 0.0, None, ALU.is_equal))
        dve.wait_ge(rel_done, 2)
        linked(nc.vector.tensor_copy(rel[:, :], rel_f))
        for h in range(A_HEADS):
            last = nc.vector.tensor_scalar(alibi[:, h, :], qpos[:, :], 2.0 ** (-8.0 * (h + 1) / A_HEADS), None, ALU.mult)
        last.then_inc(alibi_done, 1)
        linked(nc.vector.memset(xl[:, :, :], 0.0))
        linked(nc.vector.memset(keep[:, :], 1.0))
        linked(nc.vector.memset(four(keep[:, :])[:, :, 0:1], 0.0))

        def masked(i):
            m, h = units[i]
            n = TILES[m][1]
            N = min(NKEYS[m], 1024)
            if m == NT - 1:
                dve.wait_ge(late_causal, 1)
            dve.wait_ge(qk_done, i + 1)
            if i >= 2:
                dve.wait_ge(t_psum, i - 1)
                if tails(i - 2):
                    dve.wait_ge(t_last, tails(i - 2))
                dve.wait_ge(exp_done, i - 1)

            def part(at, src, init, out, signal):
                nc.vector.tensor_tensor_reduce(out=probs[0:n, i % 2, at], in0=src,
                                               in1=score[0:n, SC_OFF[m] + at.start:SC_OFF[m] + at.stop], scale=1.0,
                                               scalar=init, op0=ALU.add, op1=ALU.max,
                                               accum_out=nmax[0:n, i % 2, out:out + 1]).then_inc(signal, 1)

            part(slice(0, N), logits[0:n, 0:N], TAKEN, 0, nmax_raw)
            dve.wait_ge(nmax_raw, i + 1)
            peak = 0
            if m == NT - 1:
                dve.wait_ge(qk_tail, tails(i))
                part(slice(N, NKEYS[m]), logits[0:n, 0:NKEYS[m] - N], nmax[0:n, i % 2, 0:1], 1, nmax_tail)
                dve.wait_ge(nmax_tail, tails(i))
                peak = 1
            nc.vector.tensor_scalar(nmax[0:n, i % 2, 2:3], nmax[0:n, i % 2, peak:peak + 1], -1.0, None, ALU.mult)\
              .then_inc(nmax_done, 1)

        def turned(i):
            m, h = units[i]
            n = TILES[m][1]
            if m >= PER_BANK:
                dve.wait_ge(t_psum, i + 1)
                if i >= 2:
                    dve.wait_ge(pv_done, i - 1)
                k = min(m + 1 - PER_BANK, PER_BANK)
                nc.vector.tensor_copy(pT[:, i % 2, PER_BANK:PER_BANK + k, 0:n],
                                      banks[:, T_HI, 0:k * P].rearrange("p (f t) -> p f t", f=k)).then_inc(t_dve, 1)

        def normed(m):
            n = TILES[m][1]
            dve.wait_ge(exp_done, A_HEADS * (m + 1))
            nc.vector.reciprocal(rsums[0:n, m % 2, :], sums[0:n, m % 2, :]).then_inc(rs_done, 1)
            dve.wait_ge(rs_done, m + 1)
            dve.wait_ge(pv_done, A_HEADS * (m + 1))
            if m >= 2:
                dve.wait_ge(shared_psum, nth["ot_att", m - 2])
            nc.vector.tensor_tensor(o_tok[0:n, m % 2, :].rearrange("p (h e) -> p h e", h=A_HEADS),
                                    banks[0:n, PV, :].rearrange("p (h e) -> p h e", h=A_HEADS),
                                    rsums[0:n, m % 2, :].rearrange("p (h e) -> p h e", e=1).to_broadcast([n, A_HEADS, HD]),
                                    ALU.mult).then_inc(otok_done, 1)

        def gates(m, stage):
            s = m % 2
            z = zt[:, s, :]
            if stage == 4:
                dve.wait_ge(ln_done, m + 1)
                if m:
                    dve.wait_ge(key_done, m)
                nc.vector.scalar_tensor_tensor(out=key_arg[:, :], in0=z, scalar=0.0, in1=lnw[:, :], op0=ALU.max,
                                               op1=ALU.add).then_inc(key_in, 1)
                dve.wait_ge(key_in, m + 1)
                nc.vector.scalar_tensor_tensor(out=lnw[:, :], in0=z, scalar=0.0, in1=lnw[:, :], op0=ALU.min,
                                               op1=ALU.subtract).then_inc(logf_done, 1)
                dve.wait_ge(logf_done, m + 1)
                nc.vector.tensor_tensor_scan(b[:, s, :], keep[:, :], lnw[:, :], 0.0, ALU.mult, ALU.add)\
                  .then_inc(b_done, 1)
            if stage == 5:
                dve.wait_ge(b_done, m + 1)
                if m:
                    dve.wait_ge(shared_psum, nth["kT", m - 1])
                b3 = four(b[:, s, :])
                nc.vector.tensor_tensor(four(kd[:, :]), b3[:, :, P - 1:P].to_broadcast([P, 4, P]), b3, ALU.subtract)\
                  .then_inc(kd_in, 1)
            if stage == 6:
                dve.wait_ge(eb_done, m + 1)
                dve.wait_ge(key_done, m + 1)
                nc.vector.tensor_copy(elast[:, s, :], four(eb[:, :])[:, :, P - 1])
                nc.vector.tensor_tensor(qe[:, s, :], qt[:, s, :], eb[:, :], ALU.mult)
                nc.vector.tensor_tensor(kd[:, :], key[:, s, :], kd[:, :], ALU.mult).then_inc(ke_done, 1)

        def exponents(m, h):
            l, i = h - 1, levels_to(m, h) - 1
            if i >= 2:
                dve.wait_ge(x_done, i - 1)
            bl, el = halves(b[:, m % 2, :], l), halves(ex[:, i % 2, :], l)
            ref = bl[:, :, 0, 2 ** l - 1:2 ** l].to_broadcast([P, W // 2 ** (l + 1), 2 ** l])
            nc.vector.tensor_tensor(el[:, :, 0, :], ref, bl[:, :, 0, :], ALU.subtract)
            nc.vector.tensor_tensor(el[:, :, 1, :], bl[:, :, 1, :], ref, ALU.subtract).then_inc(ex_in, 1)

        def scores_of(i):
            m, h = units[i]
            dve.wait_ge(gram_psum, i + 1)
            if i:
                dve.wait_ge(gram_read, i)
            if h == 0:
                mask = masks[:, LEVELS, :].rearrange("p (f t) -> p f t", f=1).to_broadcast([P, 4, P])
                for par in range(2):
                    at = S[:, m % 2, :, :].rearrange("p (f two) t -> p two f t", two=2)[:, par, :, :]
                    last = nc.vector.copy_predicated(at, mask, four(banks[:, GRAM + par, :]))
            else:
                l = h - 1
                mask = halves(masks[:, l, :], l)[:, :, 1, :].rearrange("p (a n) t -> p a n t", a=1)\
                    .to_broadcast([P, 8, P // 2 ** h, 2 ** l])
                at = S[:, m % 2, :, :].rearrange("p h (n two t) -> p h n two t", two=2, t=2 ** l)[:, :, :, 1, :]
                last = nc.vector.copy_predicated(at, mask, banks[:, GRAM + h % 2, :]
                                                 .rearrange("p (h n t) -> p h n t", h=8, t=2 ** l))
            last.then_inc(gram_read, 1)

        def next_state(m):
            dve.wait_ge(shared_done, nth["out", m])
            for f in range(4):
                for par in range(2):
                    r = slice(HD * par, HD * (par + 1))
                    last = nc.vector.scalar_tensor_tensor(out=state[r, f, r], in0=state[r, f, r],
                                                          scalar=elast[r, m % 2, f:f + 1],
                                                          in1=added[r, f * P + HD * par:f * P + HD * (par + 1)],
                                                          op0=ALU.mult, op1=ALU.add)
            last.then_inc(state_done, 1)

        for stage in (4, 5, 6):
            gates(0, stage)
        dve.wait_ge(pads, 8)
        exponents(0, 1)
        for i, (m, h) in enumerate(steps):
            if i < NU:
                masked(i)
            for r in late_rounds.get(i, ()):
                if r:
                    dve.wait_ge(taken, 2 * r)
                nc.vector.max(top8[:, :], late).then_inc(taken, 1)
            if i + 2 < NU and steps[i + 2][1]:
                exponents(*steps[i + 2])
            if m + 1 < NT:
                gates(m + 1, h)
            if i < NU:
                if h == 0 and m >= 2:
                    dve.wait_ge(shared_psum, nth["out", m - 2])
                scores_of(i)
            if 1 <= i <= NU:
                turned(i - 1)
            for r in late_rounds.get(i, ()):
                dve.wait_ge(taken, 2 * r + 1)
                nc.vector.match_replace(late, top8[:, :], late, TAKEN).then_inc(taken, 1)
            if i == LATE1:
                dve.wait_ge(taken, 2 * ROUNDS)
                nc.vector.tensor_scalar(late, late, TAKEN_BELOW, MASKED, ALU.is_ge, ALU.mult).then_inc(late_mask, 1)
            if h == 2 and m:
                normed(m - 1)
                next_state(m - 1)
            if h == 3 and m:
                dve.wait_ge(sq_done, m)
                if m >= 2:
                    dve.wait_ge(rsh_done, m - 1)
                nc.vector.tensor_reduce(ssum[:, :], sq[:, :].rearrange("p (h e) -> p h e", h=8),
                                        mybir.AxisListType.X, ALU.add).then_inc(ssum_done, 1)
                dve.wait_ge(ssum_done, 2 * m - 1)
                nc.vector.tensor_scalar(ssum[:, :], ssum[:, :], 1.0 / HD, LN_EPS, ALU.mult, ALU.add).then_inc(ssum_done, 1)
            if h == 4 and m:
                dve.wait_ge(rsh_done, m)
                on8 = on[:, :].rearrange("p (h e) -> p h e", h=8)
                linked(nc.vector.tensor_tensor(on8, on8, rsh[:, :].rearrange("p (h e) -> p h e", e=1)
                                               .to_broadcast([P, 8, HD]), ALU.mult))
                dve.wait_ge(gated, m)
                nc.vector.tensor_tensor(on[:, :], on[:, :], gt[:, (m - 1) % 2, :], ALU.mult).then_inc(on_done, 1)


class NormSteps:

    def __init__(self, nc, c, sem, sb, banks, ident, tag, y, tiles, t_banks=(), split=None):
        self.nc, self.banks, self.ident, self.y, self.tiles, self.t_banks, self.split = (
            nc, banks, ident, y, tiles, t_banks, split)
        self.gb = sb(c, f"{tag}_g", [P, D])
        self.bb = sb(c, f"{tag}_b", [P, D])
        self.bn6 = sb(c, f"{tag}_bn6", [P, NT, 2, 6])
        self.mv = sb(c, f"{tag}_mv", [P, NT, 2])
        self.std = sb(c, f"{tag}_std", [P, NT])
        self.rstd = sb(c, f"{tag}_rstd", [P, NT])
        self.shift = sb(c, f"{tag}_shift", [P, NT])
        self.gb_loaded, self.bn, self.var, self.rooted, self.inverted, self.shifted, self.scaled, self.gained, self.biased = (
            sem(f"{tag}_{k}") for k in ("gb_loaded", "bn", "var", "rooted", "inverted", "shifted", "scaled", "gained", "biased"))
        if split:
            self.turned, self.hi, self.lo = sem(f"{tag}_turned"), sem(f"{tag}_hi"), sem(f"{tag}_lo")

    def load(self, sp, g_row, b_row):
        for dst, row in ((self.gb, g_row), (self.bb, b_row)):
            sp.dma_start(dst[:, :], row.rearrange("(a n) -> a n", a=1).to_broadcast([P, D])).then_inc(self.gb_loaded, 16)

    def stats(self, dve, j):
        m = self.tiles[j]
        n = TILES[m][1]
        self.nc.vector.bn_stats(self.bn6[0:n, m, 0, :], self.y[0:n, m, 0:512])
        self.nc.vector.bn_stats(self.bn6[0:n, m, 1, :], self.y[0:n, m, 512:D]).then_inc(self.bn, 1)
        dve.wait_ge(self.bn, 2 * j + 1)
        self.nc.vector.bn_aggr(self.mv[0:n, m, :], self.bn6[0:n, m, :, :].rearrange("p a b -> p (a b)")).then_inc(self.bn, 1)
        dve.wait_ge(self.bn, 2 * j + 2)
        self.nc.vector.tensor_scalar(self.mv[0:n, m, 1:2], self.mv[0:n, m, 1:2], LN_EPS, None, ALU.add).then_inc(self.var, 1)

    def root(self, act, j):
        m = self.tiles[j]
        n = TILES[m][1]
        act.wait_ge(self.var, j + 1)
        self.nc.scalar.activation(self.std[0:n, m:m + 1], self.mv[0:n, m, 1:2], ACT.Sqrt).then_inc(self.rooted, 1)

    def factors(self, dve, j):
        m = self.tiles[j]
        n = TILES[m][1]
        dve.wait_ge(self.rooted, j + 1)
        self.nc.vector.reciprocal(self.rstd[0:n, m:m + 1], self.std[0:n, m:m + 1]).then_inc(self.inverted, 1)
        dve.wait_ge(self.inverted, j + 1)
        self.nc.vector.tensor_scalar(self.shift[0:n, m:m + 1], self.mv[0:n, m, 0:1], self.rstd[0:n, m:m + 1], -1.0, ALU.mult, ALU.mult)\
          .then_inc(self.shifted, 1)

    def scale(self, act, j):
        m = self.tiles[j]
        n = TILES[m][1]
        act.wait_ge(self.shifted, j + 1)
        self.nc.scalar.activation(self.y[0:n, m, :], self.y[0:n, m, :], ACT.Identity, bias=self.shift[0:n, m:m + 1],
                             scale=self.rstd[0:n, m:m + 1]).then_inc(self.scaled, 1)

    def gains(self, dve, j):
        m = self.tiles[j]
        n = TILES[m][1]
        if j == 0:
            dve.wait_ge(self.gb_loaded, 32)
        dve.wait_ge(self.scaled, j + 1)
        self.nc.vector.tensor_tensor(self.y[0:n, m, :], self.y[0:n, m, :], self.gb[0:n, :], ALU.mult).then_inc(self.gained, 1)

    def bias(self, pool, j):
        m = self.tiles[j]
        n = TILES[m][1]
        pool.wait_ge(self.gained, j + 1)
        self.nc.gpsimd.tensor_tensor(self.y[0:n, m, :], self.y[0:n, m, :], self.bb[0:n, :], ALU.add).then_inc(self.biased, 1)

    def bank_of(self, i):
        return self.t_banks[i % len(self.t_banks)]

    def turn(self, pe, j):
        m = self.tiles[j]
        n = TILES[m][1]
        pe.wait_ge(self.biased, j + 1)
        for q in range(2):
            i = 2 * j + q
            if i >= len(self.t_banks):
                pe.wait_ge(self.lo, i - len(self.t_banks) + 1)
            for k in range(4):
                kk = 4 * q + k
                last = self.nc.tensor.transpose(self.banks[:, self.bank_of(i), k * P:k * P + n], self.y[0:n, m, kk * P:(kk + 1) * P],
                                           self.ident[0:n, 0:n])
            last.then_inc(self.turned, 1)

    def high(self, act, j):
        t0, n = TILES[self.tiles[j]]
        for q in range(2):
            i = 2 * j + q
            act.wait_ge(self.turned, i + 1)
            src = self.banks[:, self.bank_of(i), :].rearrange("p (k t) -> p k t", k=4)[:, :, 0:n]
            self.nc.scalar.activation(self.split[0][:, 4 * q:4 * q + 4, t0:t0 + n], src, ACT.Copy).then_inc(self.hi, 1)

    def low(self, dve, j):
        t0, n = TILES[self.tiles[j]]
        for q in range(2):
            i = 2 * j + q
            dve.wait_ge(self.hi, i + 1)
            src = self.banks[:, self.bank_of(i), :].rearrange("p (k t) -> p k t", k=4)[:, :, 0:n]
            at = slice(4 * q, 4 * q + 4)
            self.nc.vector.tensor_tensor(self.split[1][:, at, t0:t0 + n], src, self.split[0][:, at, t0:t0 + n].bitcast(F32),
                                    ALU.subtract).then_inc(self.lo, 1)


def out_projection(nc, c, sem, sb, banks, ident, x, meta, ins, oT, y, hH, hL):
    w = sb(c, "w_out_sb", [P, DC, D])
    done, added = sem("op_psum"), sem("op_added")
    w_loaded = [sem(f"w_out_loaded{i}") for i in range(DC // 2)]
    h_loaded = [sem(f"op_h{i}") for i in range(3)]
    tiles = list(range(NT))
    norm = NormSteps(nc, c, sem, sb, banks, ident, "n0", y, tiles, (4, 5, 6, 7), (hH, hL))
    NB = 4
    block = c.enter_context(nc.Block())

    @block.sync
    def _(sp):
        w_v = ins["w_out"][0].rearrange("(k p) f -> p k f", p=P)
        for k in range(0, DC, 2):
            sp.dma_start(w[:, k:k + 2, :], w_v[:, k:k + 2, :]).then_inc(w_loaded[k // 2], 16)
        for m, (t0, n) in enumerate(TILES):
            src = meta if m == 0 else x[t0 - N_META:t0 - N_META + n, :]
            if m >= 3:
                sp.wait_ge(h_loaded[m % 3], 16 * (m // 3))
            sp.dma_start(y[0:n, m, :], src).then_inc(h_loaded[m % 3], 16)
            if m == 2:
                norm.load(sp, ins["ln_mix_g"][0], ins["ln_mix_b"][0])

    @block.gpsimd
    def _(pool):
        for j in range(NT):
            norm.bias(pool, j)

    @block.tensor
    def _(pe):
        def product(i, ks):
            t0, n = TILES[i // 2]
            if i >= NB and ks[0] == 0:
                pe.wait_ge(added, i - NB + 1)
            for k in ks:
                last = nc.tensor.matmul(banks[0:n, i % NB, :], oT[:, k, t0:t0 + n],
                                        w[:, k, (i % 2) * 512:(i % 2 + 1) * 512], start=(k == 0), stop=(k == DC - 1))
            if ks[-1] == DC - 1:
                last.then_inc(done, 1)

        for k in range(0, DC, 2):
            pe.wait_ge(w_loaded[k // 2], 16)
            for i in range(NB):
                product(i, (k, k + 1))
        for T in range(NT + 4):
            if T >= 4:
                norm.turn(pe, T - 4)
            for i in (2 * T, 2 * T + 1) if T < NT else ():
                if i >= NB:
                    product(i, range(DC))

    @block.scalar
    def _(act):
        for T in range(NT + 4):
            if T >= 4:
                norm.high(act, T - 4)
            if 1 <= T <= NT:
                norm.scale(act, T - 1)
            if T < NT:
                norm.root(act, T)

    @block.vector
    def _(dve):
        for T in range(NT + 4):
            if T >= 4:
                norm.low(dve, T - 4)
            if 2 <= T <= NT + 1:
                norm.gains(dve, T - 2)
            if 1 <= T <= NT:
                norm.factors(dve, T - 1)
            if T < NT:
                n = TILES[T][1]
                dve.wait_ge(h_loaded[T % 3], 16 * (T // 3 + 1))
                for i in (2 * T, 2 * T + 1):
                    dve.wait_ge(done, i + 1)
                    at = y[0:n, T, (i % 2) * 512:(i % 2 + 1) * 512]
                    nc.vector.scalar_tensor_tensor(out=at, in0=at, scalar=ALPHA, in1=banks[0:n, i % NB, :], op0=ALU.mult,
                                                   op1=ALU.add).then_inc(added, 1)
                dve.wait_ge(added, 2 * T + 2)
                norm.stats(dve, T)


def pool_mixer(nc, c, sem, sb, banks, ident, ins, y, hH, hL):
    NW = len(POOL_WINDOWS)
    TAIL = 32
    w = sb(c, "w_pool_sb", [P, NW, 2, PG])
    scale = sb(c, "pool_scale_sb", [P, NW, PG])
    band = sb(c, "band", [P, NW, P])
    band_tail = sb(c, "band_tail", [P, NW, P])
    band_meta = sb(c, "band_meta", [N_META, NW, P])
    dT = sb(c, "dT", [P, 2, DC, P])
    loaded, w_ready, made, made_all, d_psum, d_act, d_dve, psum, added = (
        sem("pool_loaded"), sem("pool_w"), sem("band_made"), sem("bands_done"), sem("d_psum"), sem("d_act"),
        sem("d_dve"), sem("pool_psum"), sem("pool_added"))
    n1 = NormSteps(nc, c, sem, sb, banks, ident, "n1", y, list(range(NT)))
    n2 = NormSteps(nc, c, sem, sb, banks, ident, "n2", y, list(range(1, NT)), (4, 5, 6, 7), (hH, hL))
    NP = NT - 1
    END = NP + 8
    block = c.enter_context(nc.Block())

    @block.sync
    def _(sp):
        n1.load(sp, ins["ln_ffn_g"][0], ins["ln_ffn_b"][0])
        sp.dma_start(w[:, :, :, :], ins["w_pool"][0].rearrange("g (k p) f -> p g k f", p=P)).then_inc(loaded, 16)
        sp.dma_start(scale[:, :, :].rearrange("p g f -> p (g f)"), ins["pool_scale"].to_broadcast([P, D]))\
          .then_inc(loaded, 16)
        n2.load(sp, ins["ln_mix_g"][1], ins["ln_mix_b"][1])

    @block.gpsimd
    def _(pool):
        count = 0
        for g, win in enumerate(POOL_WINDOWS):
            for mat, rows, base in ((band, P, 0), (band_tail, P, P), (band_meta, N_META, N_META)):
                at = mat[0:rows, g, :]
                nc.gpsimd.memset(at, 1.0 / win).then_inc(made, 1)
                count += 1
                pool.wait_ge(made, count)
                nc.gpsimd.affine_select(out=at, in_=at, compare_op=ALU.is_gt, fill=0.0, base=win - base,
                                        pattern=[[-1, P]], channel_multiplier=1).then_inc(made, 1)
                count += 1
                pool.wait_ge(made, count)
                if base == 0:
                    nc.gpsimd.affine_select(out=at, in_=at, compare_op=ALU.is_ge, fill=0.0, base=0,
                                            pattern=[[1, P]], channel_multiplier=-1).then_inc(made, 1)
                    count += 1
                    pool.wait_ge(made, count)
                    nc.gpsimd.tensor_tensor(at, at, ident[:, :], ALU.subtract).then_inc(made_all, 1)
        pool.wait_ge(loaded, 32)
        for k in range(2):
            nc.gpsimd.tensor_tensor(w[:, :, k, :], w[:, :, k, :], scale[:, :, :], ALU.mult).then_inc(w_ready, 1)
        for T in range(END):
            if 0 <= T - 7 < NP:
                n2.bias(pool, T - 7)
            if 0 <= T - 2 < NT:
                n1.bias(pool, T - 2)

    @block.tensor
    def _(pe):
        pe.wait_ge(made_all, NW)
        pe.wait_ge(made, 3 * 2 * NW + NW)
        pe.wait_ge(w_ready, 2)
        for T in range(END):
            if 0 <= T - 8 < NP:
                n2.turn(pe, T - 8)
            j = T - 5
            if 0 <= j < NP:
                pe.wait_ge(d_act, j + 1)
                pe.wait_ge(d_dve, j + 1)
                if j:
                    pe.wait_ge(added, 2 * j)
                for g in range(NW):
                    for k in range(2):
                        last = nc.tensor.matmul(banks[:, 2 + g // 2, g % 2 * PG:(g % 2 + 1) * PG],
                                                dT[:, j % 2, 2 * g + k, :], w[:, g, k, :], start=(k == 0), stop=(k == 1))
                last.then_inc(psum, 1)
            j = T - 4
            if 0 <= j < NP:
                m = j + 1
                pe.wait_ge(n1.biased, m + 1)
                if j:
                    pe.wait_ge(d_act, j)
                    pe.wait_ge(d_dve, j)
                for k in range(DC):
                    at = banks[:, k // 4, k % 4 * P:(k % 4 + 1) * P]
                    cols = slice(k * P, (k + 1) * P)
                    g = k // 2
                    nc.tensor.matmul(at, y[:, m, cols], band[:, g, :], start=True, stop=False)
                    if m == 1:
                        last = nc.tensor.matmul(at, y[0:N_META, 0, cols], band_meta[:, g, :], start=False, stop=True)
                    else:
                        last = nc.tensor.matmul(at, y[P - TAIL:P, m - 1, cols], band_tail[P - TAIL:P, g, :],
                                                start=False, stop=True)
                last.then_inc(d_psum, 1)

    @block.scalar
    def _(act):
        for T in range(END):
            if 0 <= T - 8 < NP:
                n2.high(act, T - 8)
            if 0 <= T - 6 < NP:
                n2.scale(act, T - 6)
            if 0 <= T - 5 < NP:
                n2.root(act, T - 5)
            j = T - 4
            if 0 <= j < NP:
                act.wait_ge(d_psum, j + 1)
                if j >= 2:
                    act.wait_ge(psum, j - 1)
                nc.scalar.activation(dT[:, j % 2, 0:4, :], banks[:, 0, :].rearrange("p (k t) -> p k t", k=4), ACT.Copy)\
                  .then_inc(d_act, 1)
            if 0 <= T - 1 < NT:
                n1.scale(act, T - 1)
            if T < NT:
                n1.root(act, T)

    @block.vector
    def _(dve):
        for T in range(END):
            if 0 <= T - 7 < NP:
                n2.gains(dve, T - 7)
            if 0 <= T - 6 < NP:
                n2.factors(dve, T - 6)
            if 0 <= T - 8 < NP:
                n2.low(dve, T - 8)
            j = T - 5
            if 0 <= j < NP:
                m = j + 1
                dve.wait_ge(psum, j + 1)
                if m + 1 < NT:
                    dve.wait_ge(d_psum, j + 2)
                for half in range(2):
                    at = y[:, m, half * 512:(half + 1) * 512]
                    nc.vector.scalar_tensor_tensor(out=at, in0=at, scalar=ALPHA, in1=banks[:, 2 + half, :],
                                                   op0=ALU.mult, op1=ALU.add).then_inc(added, 1)
                dve.wait_ge(added, 2 * j + 2)
                n2.stats(dve, j)
            j = T - 4
            if 0 <= j < NP:
                dve.wait_ge(d_psum, j + 1)
                if j >= 2:
                    dve.wait_ge(psum, j - 1)
                nc.vector.tensor_copy(dT[:, j % 2, 4:8, :], banks[:, 1, :].rearrange("p (k t) -> p k t", k=4))\
                  .then_inc(d_dve, 1)
            if 0 <= T - 2 < NT:
                n1.gains(dve, T - 2)
            if 0 <= T - 1 < NT:
                n1.factors(dve, T - 1)
            if T < NT:
                n1.stats(dve, T)


def ffn(nc, c, sem, sb, banks, ident, tag, y, hH, hL, tiles, chunks, w_gate, w_up, w_down, final=None):
    NCH = len(chunks)
    CW = max(n for _, n in chunks)
    NU = 2 * NCH
    NJ = 2 * len(tiles)
    wg = w_gate.rearrange("(k p) f -> p k f", p=P)
    wu = w_up.rearrange("(k p) f -> p k f", p=P)
    wd = w_down.rearrange("(i u p) f -> i p u f", u=2, p=P)
    raw = sb(c, f"{tag}_raw", [P, 2, DC, P])
    wH = sb(c, f"{tag}_wH", [P, 2, 2, DC, P], F32R)
    wL = sb(c, f"{tag}_wL", [P, 2, 2, DC, P], F32R)
    draw = sb(c, f"{tag}_draw", [P, 2, D])
    dH = sb(c, f"{tag}_dH", [P, 2, D], F32R)
    dL = sb(c, f"{tag}_dL", [P, 2, D], F32R)
    hidH = sb(c, f"{tag}_hidH", [P, 2, L], F32R)
    hidL = sb(c, f"{tag}_hidL", [P, 2, L], F32R)
    silu = sb(c, f"{tag}_silu", [P, 2, CW])
    hid = sb(c, f"{tag}_hid", [P, 2, CW])

    s = {k: sem(f"{tag}_{k}") for k in ("alpha", "raw", "w_hi", "w_lo", "draw", "d_hi", "d_lo", "gu_psum",
                                        "silu", "hid", "hid_hi", "hid_lo", "d_psum", "added")}
    FREE = 1
    ITERS = FF_TILES // 2
    NF = len(tiles)
    if final:
        norm = NormSteps(nc, c, sem, sb, banks, ident, f"{tag}_norm", y, tiles)
        stored = sem(f"{tag}_stored")
    block = c.enter_context(nc.Block())

    @block.sync
    def _(sp):
        with sp.Fori(0, ITERS) as i:
            for u in range(2):
                sp.wait_ge(s["w_hi"], FREE + 2 * i + u)
                sp.wait_ge(s["w_lo"], FREE + 2 * i + u)
                for g, w in enumerate((wg, wu)):
                    sp.dma_start(raw[:, g, :, :], w[:, :, bass.ds((2 * i + u) * P, P)]).then_inc(s["raw"], 16)
                if u == 0:
                    sp.wait_ge(s["d_hi"], FREE + i)
                    sp.wait_ge(s["d_lo"], FREE + i)
                    sp.dma_start(draw[:, :, :], wd[bass.ds(i, 1), :, :, :].rearrange("a p u f -> p (a u) f"))\
                      .then_inc(s["draw"], 16)
        if final:
            norm.load(sp, final[0], final[1])
            for j, m in enumerate(tiles):
                t0, n = TILES[m]
                sp.wait_ge(norm.biased, j + 1)
                sp.dma_start(final[2][0, t0 - N_META:t0 - N_META + n, :], y[0:n, m, :]).then_inc(stored, 16)
            sp.wait_ge(stored, 16 * NF)

    @block.gpsimd
    def _(pool):
        pool.sem_inc(s["w_lo"], FREE)
        pool.sem_inc(s["d_lo"], FREE)
        with pool.Fori(0, ITERS) as i:
            for u in range(2):
                pool.wait_ge(s["w_hi"], FREE + 2 * i + u + 1)
                pool.wait_ge(s["gu_psum"], FREE + NU * i)
                nc.gpsimd.tensor_tensor(wL[:, u, :, :, :].rearrange("p g k f -> p (g k f)"),
                                        raw[:, :, :, :].rearrange("p g k f -> p (g k f)"),
                                        wH[:, u, :, :, :].rearrange("p g k f -> p (g k f)").bitcast(F32),
                                        ALU.subtract).then_inc(s["w_lo"], 1)
            pool.wait_ge(s["d_hi"], FREE + i + 1)
            nc.gpsimd.tensor_tensor(dL[:, :, :].rearrange("p u f -> p (u f)"), draw[:, :, :].rearrange("p u f -> p (u f)"),
                                    dH[:, :, :].rearrange("p u f -> p (u f)").bitcast(F32), ALU.subtract)\
              .then_inc(s["d_lo"], 1)
        if final:
            for j in range(NF):
                norm.bias(pool, j)

    @block.scalar
    def _(act):
        act.sem_inc(s["w_hi"], FREE)
        act.sem_inc(s["d_hi"], FREE)
        with act.Fori(0, ITERS) as i:
            act.wait_ge(s["gu_psum"], FREE + NU * i)
            for u in range(2):
                act.wait_ge(s["raw"], 32 * (2 * i + u + 1))
                nc.scalar.activation(wH[:, u, :, :, :], raw[:, :, :, :], ACT.Copy).then_inc(s["w_hi"], 1)
            act.wait_ge(s["draw"], 16 * (i + 1))
            act.wait_ge(s["d_psum"], FREE + NJ * i)
            nc.scalar.activation(dH[:, :, :], draw[:, :, :], ACT.Copy).then_inc(s["d_hi"], 1)

            def gate(q):
                n = chunks[q % NCH][1]
                act.wait_ge(s["gu_psum"], FREE + NU * i + q + 1)
                nc.scalar.activation(silu[:, q % 2, 0:n], banks[:, 2 * (q % 2), 0:n], ACT.Silu).then_inc(s["silu"], 1)

            def high(q):
                a, n = chunks[q % NCH]
                act.wait_ge(s["hid"], FREE + NU * i + q + 1)
                nc.scalar.activation(hidH[:, q // NCH, a:a + n], hid[:, q % 2, 0:n], ACT.Copy).then_inc(s["hid_hi"], 1)

            for q in range(NU):
                gate(q)
                high(q)
        if final:
            for T in range(NF + 1):
                if T >= 1:
                    norm.scale(act, T - 1)
                if T < NF:
                    norm.root(act, T)

    @block.vector
    def _(dve):
        dve.sem_inc(s["hid"], FREE)
        dve.sem_inc(s["added"], FREE)
        for m in tiles:
            n = TILES[m][1]
            nc.vector.tensor_scalar(y[0:n, m, :], y[0:n, m, :], ALPHA, None, ALU.mult).then_inc(s["alpha"], 1)

        def iteration(i, then):
            for q in range(NU):
                a, n = chunks[q % NCH]
                dve.wait_ge(s["silu"], NU * i + q + 1)
                nc.vector.tensor_tensor(hid[:, q % 2, 0:n], silu[:, q % 2, 0:n], banks[:, 2 * (q % 2) + 1, 0:n], ALU.mult)\
                  .then_inc(s["hid"], 1)
                dve.wait_ge(s["hid_hi"], NU * i + q + 1)
                nc.vector.tensor_tensor(hidL[:, q // NCH, a:a + n], hid[:, q % 2, 0:n],
                                        hidH[:, q // NCH, a:a + n].bitcast(F32), ALU.subtract).then_inc(s["hid_lo"], 1)
            dve.wait_ge(s["alpha"], len(tiles))
            dve.wait_ge(s["added"], FREE + NJ * i)
            for j in range(NJ):
                m = tiles[j // 2]
                n = TILES[m][1]
                dve.wait_ge(s["d_psum"], FREE + NJ * i + j + 1)
                at = y[0:n, m, (j % 2) * 512:(j % 2 + 1) * 512]
                nc.vector.tensor_tensor(at, at, banks[0:n, 4 + j % 4, :], ALU.add).then_inc(s["added"], 1)
                if j % 2:
                    then(j // 2)

        def norm_beside(T):
            if T < NF:
                dve.wait_ge(s["added"], FREE + NJ * (ITERS - 1) + 2 * T + 2)
                norm.stats(dve, T)
            if 1 <= T <= NF:
                norm.factors(dve, T - 1)
            if T >= 2:
                norm.gains(dve, T - 2)

        LOOPED = ITERS - 1 if final else ITERS
        with dve.Fori(0, LOOPED) as i:
            iteration(i, lambda T: None)
        if final:
            iteration(LOOPED, norm_beside)
            norm_beside(NF)
            norm_beside(NF + 1)

    @block.tensor
    def _(pe):
        pe.sem_inc(s["gu_psum"], FREE)
        pe.sem_inc(s["d_psum"], FREE)
        with pe.Fori(0, ITERS) as i:
            for q in range(NU):
                u, (a, n) = q // NCH, chunks[q % NCH]
                if q % NCH == 0:
                    pe.wait_ge(s["w_hi"], FREE + 2 * i + u + 1)
                    pe.wait_ge(s["w_lo"], FREE + 2 * i + u + 1)
                if q >= 2:
                    pe.wait_ge(s["hid"], FREE + NU * i + q - 1)
                else:
                    pe.wait_ge(s["hid"], FREE + NU * i)
                for g in range(2):
                    for k in range(DC):
                        for part, (w, h) in enumerate(((wH, hL), (wL, hH), (wH, hH))):
                            last = nc.tensor.matmul(banks[:, 2 * (q % 2) + g, 0:n], w[:, u, g, k, :], h[:, k, a:a + n],
                                                    start=(k == 0 and part == 0), stop=(k == DC - 1 and part == 2))
                last.then_inc(s["gu_psum"], 1)
            pe.wait_ge(s["d_lo"], FREE + i + 1)
            pe.wait_ge(s["hid_lo"], NU * i + NCH)
            for j0 in range(0, NJ, 4):
                for u in range(2):
                    if j0 == 0 and u == 1:
                        pe.wait_ge(s["hid_lo"], NU * (i + 1))
                    for j in range(j0, min(j0 + 4, NJ)):
                        t0, n = TILES[tiles[j // 2]]
                        if u == 0:
                            pe.wait_ge(s["added"], FREE + NJ * i + max(j - 3, 0))
                        for part, (w, h) in enumerate(((dH, hidL), (dL, hidH), (dH, hidH))):
                            last = nc.tensor.matmul(banks[0:n, 4 + j % 4, :], h[:, u, t0:t0 + n],
                                                    w[:, u, (j % 2) * 512:(j % 2 + 1) * 512],
                                                    start=(u == 0 and part == 0), stop=(u == 1 and part == 2))
                        if u == 1:
                            last.then_inc(s["d_psum"], 1)


def kernel(**inputs):
    import numpy as np
    import concourse.bacc as bacc
    from concourse.bass_utils import run_bass_kernel_spmd

    nc = bacc.Bacc("TRN2", target_bir_lowering=False, num_devices=1)
    arrays, ins = {}, {}
    for name, a in inputs.items():
        arrays[f"in_{name}"] = np.ascontiguousarray(a)
        ins[name] = nc.dram_tensor(f"in_{name}", a.shape, mybir.dt.from_np(arrays[f"in_{name}"].dtype),
                                   kind="ExternalInput").ap()
    out = nc.dram_tensor("out_0", (1, SEQ, D), F32, kind="ExternalOutput").ap()
    build(nc, ins, out)
    r = run_bass_kernel_spmd(nc, [arrays], core_ids=[0])
    return r.results[0]["out_0"]
```
